# Optimizing a Trainium2 kernel written in Bass

```python
import math
import jax, jax.numpy as jnp
from jax import lax
import numpy as np

D_MODEL = 1024
BATCH = 1
SEQ = 256
DEPTH = 2

N_META = 16
EPS = 1e-6
MASK_VALUE = -1e30

SWA_HEADS = 8
SWA_KV_HEADS = 2
SWA_HEAD_DIM = 64
SWA_WINDOW = 128
SWA_BLOCK = 128

MLA_HEADS = 8
MLA_Q_LORA = 384
MLA_KV_LORA = 256
MLA_NOPE_DIM = 64
MLA_ROPE_DIM = 32
MLA_V_DIM = 64
MLA_QUERY_BLOCK = 128
ROPE_THETA = 10000.0

ATTN_ALIGN = 128
ATTN_SPLITS = (SWA_HEADS * SWA_HEAD_DIM, SWA_KV_HEADS * SWA_HEAD_DIM, SWA_KV_HEADS * SWA_HEAD_DIM,
               MLA_Q_LORA, MLA_KV_LORA, MLA_ROPE_DIM)
ATTN_IN = sum(ATTN_SPLITS)
ATTN_MIX = SWA_HEADS * SWA_HEAD_DIM + MLA_HEADS * MLA_V_DIM

GLA_HEADS = 4
GLA_KEY_DIM = D_MODEL // 2
GLA_VALUE_DIM = D_MODEL
GLA_HEAD_K = GLA_KEY_DIM // GLA_HEADS
GLA_HEAD_V = GLA_VALUE_DIM // GLA_HEADS
GLA_GATE_RANK = 16
GLA_GATE_TAU = 16.0
GLA_CHUNK = 64
GLA_SPLITS = (GLA_KEY_DIM, GLA_KEY_DIM, GLA_VALUE_DIM, GLA_VALUE_DIM, GLA_GATE_RANK)
GLA_IN = sum(GLA_SPLITS)

PEER_N_KEYS = 128
PEER_EXPERTS = PEER_N_KEYS ** 2
PEER_HEADS = 8
PEER_TOPK = 16
PEER_KEY_DIM = 128
PEER_TOKEN_BLOCK = 256

N_ATTN_LAYERS = (DEPTH + 1) // 2
N_GLA_LAYERS = DEPTH // 2

kernel_name = "hybrid_swa_mla_gla_peer_meta"

def rmsnorm(x, g):
    xf = x.astype(jnp.float32)
    y = xf * lax.rsqrt(jnp.mean(xf * xf, axis=-1, keepdims=True) + EPS)
    return (y * g.astype(jnp.float32)).astype(x.dtype)

def split_cols(t, sizes):
    idx = [int(v) for v in np.cumsum(sizes)[:-1]]
    return jnp.split(t, idx, axis=-1)

def rope_tables(n, offset):
    pos = (jnp.arange(n) - offset).astype(jnp.float32)
    inv = ROPE_THETA ** (-jnp.arange(0, MLA_ROPE_DIM, 2, dtype=jnp.float32) / MLA_ROPE_DIM)
    ang = pos[:, None] * inv[None, :]
    return jnp.cos(ang), jnp.sin(ang)

def apply_rope(x, cos, sin):
    xf = x.astype(jnp.float32)
    x1, x2 = jnp.split(xf, 2, axis=-1)
    return jnp.concatenate([x1 * cos - x2 * sin, x2 * cos + x1 * sin], axis=-1).astype(x.dtype)

def swa_sink_attention(q, k, v, sinks, valid):
    B, Lp, Hq, d = q.shape
    nb = Lp // SWA_BLOCK
    G = Hq // SWA_KV_HEADS
    qb = q.reshape(B, nb, SWA_BLOCK, SWA_KV_HEADS, G, d)

    def with_prev(t):
        tb = t.reshape(t.shape[0], nb, SWA_BLOCK, *t.shape[2:])
        prev = jnp.concatenate([jnp.zeros_like(tb[:, :1]), tb[:, :-1]], axis=1)
        return jnp.concatenate([prev, tb], axis=2)

    kb = with_prev(k)
    vb = with_prev(v)
    validb = with_prev(valid[None])[0]
    q_idx = jnp.arange(SWA_BLOCK) + SWA_BLOCK
    k_idx = jnp.arange(2 * SWA_BLOCK)
    diff = q_idx[:, None] - k_idx[None, :]
    band = (diff >= 0) & (diff < SWA_WINDOW)
    mask = band[None] & validb[:, None, :]
    s = jnp.einsum('bnqhgd,bnkhd->bnhgqk', qb, kb).astype(jnp.float32) * (d ** -0.5)
    s = jnp.where(mask[None, :, None, None], s, MASK_VALUE)
    sink = jnp.broadcast_to(sinks.reshape(SWA_KV_HEADS, G).astype(jnp.float32)[None, None, :, :, None, None],
                            s.shape[:-1] + (1,))
    p = jax.nn.softmax(jnp.concatenate([s, sink], axis=-1), axis=-1)[..., :-1]
    o = jnp.einsum('bnhgqk,bnkhd->bnqhgd', p.astype(v.dtype), vb)
    return o.reshape(B, Lp, Hq * d)

def mla_attention(q_nope, q_rope, k_nope, k_rope, v, valid):
    B, Lp, H, _ = q_nope.shape
    nb = Lp // MLA_QUERY_BLOCK
    scale = (MLA_NOPE_DIM + MLA_ROPE_DIM) ** -0.5
    k_idx = jnp.arange(Lp)

    def block(i):
        start = i * MLA_QUERY_BLOCK
        qn = lax.dynamic_slice_in_dim(q_nope, start, MLA_QUERY_BLOCK, axis=1)
        qr = lax.dynamic_slice_in_dim(q_rope, start, MLA_QUERY_BLOCK, axis=1)
        s = (jnp.einsum('bqhd,bkhd->bhqk', qn, k_nope)
             + jnp.einsum('bqhd,bkd->bhqk', qr, k_rope)).astype(jnp.float32) * scale
        q_idx = start + jnp.arange(MLA_QUERY_BLOCK)
        mask = (k_idx[None, :] <= q_idx[:, None]) & valid[None, :]
        s = jnp.where(mask, s, MASK_VALUE)
        p = jax.nn.softmax(s, axis=-1).astype(v.dtype)
        return jnp.einsum('bhqk,bkhd->bqhd', p, v)

    o = lax.map(block, jnp.arange(nb))
    return jnp.transpose(o, (1, 0, 2, 3, 4)).reshape(B, Lp, H * MLA_V_DIM)

def attn_mixer(h, w_in, q_norm, w_uq, kv_norm, w_ukv, sinks, w_out):
    B, L, D = h.shape
    pad = (-L) % ATTN_ALIGN
    Lp = L + pad
    proj = jnp.pad(h @ w_in, ((0, 0), (pad, 0), (0, 0)))
    qa, ka, va, cq, ckv, kr = split_cols(proj, ATTN_SPLITS)
    valid = jnp.arange(Lp) >= pad
    o_a = swa_sink_attention(qa.reshape(B, Lp, SWA_HEADS, SWA_HEAD_DIM),
                             ka.reshape(B, Lp, SWA_KV_HEADS, SWA_HEAD_DIM),
                             va.reshape(B, Lp, SWA_KV_HEADS, SWA_HEAD_DIM), sinks, valid)
    qh = (rmsnorm(cq, q_norm) @ w_uq).reshape(B, Lp, MLA_HEADS, MLA_NOPE_DIM + MLA_ROPE_DIM)
    q_nope, q_rope = qh[..., :MLA_NOPE_DIM], qh[..., MLA_NOPE_DIM:]
    kvh = (rmsnorm(ckv, kv_norm) @ w_ukv).reshape(B, Lp, MLA_HEADS, MLA_NOPE_DIM + MLA_V_DIM)
    k_nope, v_b = kvh[..., :MLA_NOPE_DIM], kvh[..., MLA_NOPE_DIM:]
    cos, sin = rope_tables(Lp, pad)
    q_rope = apply_rope(q_rope, cos[:, None, :], sin[:, None, :])
    k_rope = apply_rope(kr, cos, sin)
    o_b = mla_attention(q_nope, q_rope, k_nope, k_rope, v_b, valid)
    o = jnp.concatenate([o_a, o_b], axis=-1)[:, pad:]
    return o @ w_out

def gla_mixer(h, w_in, w_gate, b_gate, out_norm, w_out):
    B, L, D = h.shape
    C = GLA_CHUNK
    pad = (-L) % C
    Lp = L + pad
    nc = Lp // C
    proj = jnp.pad(h @ w_in, ((0, 0), (pad, 0), (0, 0)))
    q, k, v, r, g1 = split_cols(proj, GLA_SPLITS)
    valid = (jnp.arange(Lp) >= pad).astype(jnp.float32)[None, :, None]
    log_a = jax.nn.log_sigmoid((g1 @ w_gate + b_gate).astype(jnp.float32)) / GLA_GATE_TAU
    qf = (q.astype(jnp.float32) * GLA_HEAD_K ** -0.5).reshape(B, nc, C, GLA_HEADS, GLA_HEAD_K)
    kf = (k.astype(jnp.float32) * valid).reshape(B, nc, C, GLA_HEADS, GLA_HEAD_K)
    vf = (v.astype(jnp.float32) * valid).reshape(B, nc, C, GLA_HEADS, GLA_HEAD_V)
    bcum = jnp.cumsum(log_a.reshape(B, nc, C, GLA_HEADS, GLA_HEAD_K), axis=2)
    q_dec = qf * jnp.exp(bcum)
    k_dec = kf * jnp.exp(-bcum)
    k_end = kf * jnp.exp(bcum[:, :, -1:] - bcum)
    chunk_decay = jnp.exp(bcum[:, :, -1])
    tri = jnp.tril(jnp.ones((C, C), dtype=bool))
    a = jnp.einsum('bnqhd,bnkhd->bnhqk', q_dec, k_dec)
    a = jnp.where(tri, a, 0.0)
    o_intra = jnp.einsum('bnhqk,bnkhe->bnqhe', a, vf)

    def step(state, inp):
        qd, ke, vc, dec = inp
        o = jnp.einsum('bqhd,bhde->bqhe', qd, state)
        state = dec[..., None] * state + jnp.einsum('bkhd,bkhe->bhde', ke, vc)
        return state, o

    state0 = jnp.zeros((B, GLA_HEADS, GLA_HEAD_K, GLA_HEAD_V), jnp.float32)
    xs = (jnp.moveaxis(q_dec, 1, 0), jnp.moveaxis(k_end, 1, 0),
          jnp.moveaxis(vf, 1, 0), jnp.moveaxis(chunk_decay, 1, 0))
    _, o_inter = lax.scan(step, state0, xs)
    o = (o_intra + jnp.moveaxis(o_inter, 0, 1)).reshape(B, Lp, GLA_HEADS, GLA_HEAD_V)
    o = rmsnorm(o, out_norm)
    rg = jax.nn.silu(r.astype(jnp.float32)).reshape(B, Lp, GLA_HEADS, GLA_HEAD_V)
    o = (o * rg).reshape(B, Lp, GLA_VALUE_DIM)[:, pad:].astype(h.dtype)
    return o @ w_out

def peer_ffn(h, w_query, sub_keys, expert_u, expert_v):
    B, L, D = h.shape
    T = B * L
    tb = PEER_TOKEN_BLOCK
    n_blocks = -(-T // tb)
    flat = jnp.pad(h.reshape(T, D), ((0, n_blocks * tb - T), (0, 0))).reshape(n_blocks, tb, D)
    k = PEER_TOPK

    def block(xb):
        q = (xb @ w_query).reshape(tb, PEER_HEADS, 2, PEER_KEY_DIM // 2)
        s = jnp.einsum('thpd,pnd->thpn', q, sub_keys).astype(jnp.float32)
        top_s, top_i = lax.top_k(s, k)
        cand_s = top_s[:, :, 0, :, None] + top_s[:, :, 1, None, :]
        cand_i = top_i[:, :, 0, :, None] * PEER_N_KEYS + top_i[:, :, 1, None, :]
        best_s, best_j = lax.top_k(cand_s.reshape(tb, PEER_HEADS, k * k), k)
        idx = jnp.take_along_axis(cand_i.reshape(tb, PEER_HEADS, k * k), best_j, axis=-1)
        gate = jax.nn.softmax(best_s, axis=-1)
        u = expert_u[idx]
        act = jax.nn.gelu(jnp.einsum('thkd,td->thk', u, xb).astype(jnp.float32))
        w = (gate * act).astype(xb.dtype)
        return jnp.einsum('thk,thkd->td', w, expert_v[idx])

    out = lax.map(block, flat).reshape(n_blocks * tb, D)[:T]
    return out.reshape(B, L, D)

def setup_inputs(seed: int = 0) -> dict:
    key = jax.random.key(seed)
    ks = jax.random.split(key, 22)

    def nrm(i, shape, scale):
        return jax.random.normal(ks[i], shape, jnp.float32) * scale

    NA, NG = N_ATTN_LAYERS, N_GLA_LAYERS
    return {
        "x": nrm(0, (BATCH, SEQ, D_MODEL), 1.0),
        "meta_tokens": nrm(1, (N_META, D_MODEL), 1.0),
        "attn_norm": 1.0 + nrm(2, (NA, D_MODEL), 0.02),
        "attn_w_in": nrm(3, (NA, D_MODEL, ATTN_IN), D_MODEL ** -0.5),
        "mla_q_norm": 1.0 + nrm(4, (NA, MLA_Q_LORA), 0.02),
        "mla_w_uq": nrm(5, (NA, MLA_Q_LORA, MLA_HEADS * (MLA_NOPE_DIM + MLA_ROPE_DIM)), MLA_Q_LORA ** -0.5),
        "mla_kv_norm": 1.0 + nrm(6, (NA, MLA_KV_LORA), 0.02),
        "mla_w_ukv": nrm(7, (NA, MLA_KV_LORA, MLA_HEADS * (MLA_NOPE_DIM + MLA_V_DIM)), MLA_KV_LORA ** -0.5),
        "swa_sinks": nrm(8, (NA, SWA_HEADS), 0.5),
        "attn_w_out": nrm(9, (NA, ATTN_MIX, D_MODEL), ATTN_MIX ** -0.5),
        "gla_norm": 1.0 + nrm(10, (NG, D_MODEL), 0.02),
        "gla_w_in": nrm(11, (NG, D_MODEL, GLA_IN), D_MODEL ** -0.5),
        "gla_w_gate": nrm(12, (NG, GLA_GATE_RANK, GLA_KEY_DIM), GLA_GATE_RANK ** -0.5),
        "gla_b_gate": nrm(13, (NG, GLA_KEY_DIM), 0.1),
        "gla_out_norm": 1.0 + nrm(14, (NG, GLA_HEAD_V), 0.02),
        "gla_w_out": nrm(15, (NG, GLA_VALUE_DIM, D_MODEL), GLA_VALUE_DIM ** -0.5),
        "ffn_norm": 1.0 + nrm(16, (DEPTH, D_MODEL), 0.02),
        "peer_w_query": nrm(17, (DEPTH, D_MODEL, PEER_HEADS * PEER_KEY_DIM), D_MODEL ** -0.5),
        "peer_sub_keys": nrm(18, (DEPTH, 2, PEER_N_KEYS, PEER_KEY_DIM // 2), (PEER_KEY_DIM // 2) ** -0.5),
        "peer_u": nrm(19, (DEPTH, PEER_EXPERTS, D_MODEL), D_MODEL ** -0.5),
        "peer_v": nrm(20, (DEPTH, PEER_EXPERTS, D_MODEL), (PEER_HEADS * PEER_TOPK) ** -0.5),
        "final_norm": 1.0 + nrm(21, (D_MODEL,), 0.02),
    }

def reference(x, meta_tokens, attn_norm, attn_w_in, mla_q_norm, mla_w_uq, mla_kv_norm, mla_w_ukv,
              swa_sinks, attn_w_out, gla_norm, gla_w_in, gla_w_gate, gla_b_gate, gla_out_norm, gla_w_out,
              ffn_norm, peer_w_query, peer_sub_keys, peer_u, peer_v, final_norm):
    B = x.shape[0]
    meta = jnp.broadcast_to(meta_tokens.astype(x.dtype)[None], (B, N_META, x.shape[-1]))
    h = jnp.concatenate([meta, x], axis=1)
    for layer in range(DEPTH):
        i = layer // 2
        if layer % 2 == 0:
            h = h + attn_mixer(rmsnorm(h, attn_norm[i]), attn_w_in[i], mla_q_norm[i], mla_w_uq[i],
                               mla_kv_norm[i], mla_w_ukv[i], swa_sinks[i], attn_w_out[i])
        else:
            h = h + gla_mixer(rmsnorm(h, gla_norm[i]), gla_w_in[i], gla_w_gate[i], gla_b_gate[i],
                              gla_out_norm[i], gla_w_out[i])
        h = h + peer_ffn(rmsnorm(h, ffn_norm[layer]), peer_w_query[layer], peer_sub_keys[layer],
                         peer_u[layer], peer_v[layer])
    return rmsnorm(h, final_norm)[:, N_META:]


_drawn_inputs = setup_inputs


def setup_inputs(seed=0):
    import zlib

    import numpy as np

    out = dict(_drawn_inputs(seed))
    spreads = {}
    factors = {'attn_norm': 5.688,
     'mla_q_norm': 8.0,
     'mla_kv_norm': 8.0,
     'swa_sinks': 64.0,
     'gla_norm': 2.686,
     'gla_out_norm': 19.144,
     'ffn_norm': 31.117,
     'final_norm': 7.555}
    for name, (base, spread) in spreads.items():
        noise = np.random.default_rng([zlib.crc32(name.encode()), seed]).standard_normal(out[name].shape)
        drawn = base * np.exp(spread * noise) if base else spread * noise
        out[name] = __import__('jax').numpy.asarray(drawn.astype(out[name].dtype))
    for name, factor in factors.items():
        out[name] = (out[name] * factor).astype(out[name].dtype)
    return out
```

```python
import numpy as np
import concourse.bass as bass
from concourse import mybir
from contextlib import ExitStack

F32 = mybir.dt.float32
U32 = mybir.dt.uint32
ALU = mybir.AluOpType
ACT = mybir.ActivationFunctionType
AX = mybir.AxisListType.X

P = 128
D = 1024
KC = D // P
N_META, SEQ = 16, 256
NB = 3
ROWS = NB * P
PAD = ROWS - N_META - SEQ
LIVE = ROWS - PAD
EPS = 1e-6
NEG = -1e30

HEADS = 16
HALF = HEADS // 2
HD = 64
QD = 96
ROPE = 16
Q_LORA, KV_LORA = 384, 256
WINDOW = 128

GH, GK, GV = 4, 128, 256
GKD, GVD, RANK = GH * GK, GH * GV, 16
TAU = 16.0
CHUNK = 64

TOPK, N_KEYS, PH = 16, 128, 8
EXPERTS = N_KEYS * N_KEYS
TT = P // PH
RING = 8
GELU_C = 0.7978845608028654
FIRST_TILE = PAD // TT
WSLOTS = 2

CONST_PARTS = [("ident", P), ("pick", TT * PH * 8), ("place", 112 + P), ("iota", 16), ("tri", P), ("after", P),
               ("chunks", 2), ("neghalf", 8), ("cos", NB * ROPE), ("sin", NB * ROPE), ("mask_swa", 768), ("mask_mla", 768)]
CONST_AT = {}
_at = 0
for _n, _w in CONST_PARTS:
    CONST_AT[_n] = (_at, _w)
    _at += _w
CONST_COLS = _at
LIVE_CONSTS = CONST_AT["cos"][0]

SCORE_AT = {2: (0, 384), 0: (384, 128), 1: (512, 256)}


def constants():
    c = np.zeros((P, CONST_COLS), np.float32)

    def put(name, a):
        at, w = CONST_AT[name]
        c[:, at:at + w] = a.reshape(P, w)

    i = np.arange(P)
    put("ident", np.eye(P, dtype=np.float32))
    put("pick", (np.arange(1024)[None] // PH == i[:, None]).astype(np.float32))
    put("place", (np.arange(112 + P)[None] == 112 + i[:, None] // PH).astype(np.float32))
    put("iota", np.broadcast_to(np.arange(16, dtype=np.float32), (P, 16)))
    same = i[:, None] // CHUNK == i[None] // CHUNK
    put("tri", (same & (i[:, None] <= i[None])).astype(np.float32))
    put("after", (same & (i[:, None] > i[None])).astype(np.float32))
    put("chunks", (i[:, None] // CHUNK == np.arange(2)[None]).astype(np.float32))
    put("neghalf", np.full((P, 8), -0.5, np.float32))
    inv = np.float32(10000.0) ** (-np.arange(0, 2 * ROPE, 2, dtype=np.float32) / np.float32(2 * ROPE))
    pos = (np.arange(ROWS) - PAD).astype(np.float32).reshape(NB, P).T
    ang = (pos[:, :, None] * inv[None, None]).astype(np.float32)
    put("cos", np.cos(ang))
    put("sin", np.sin(ang))
    for name, window in (("mask_swa", WINDOW), ("mask_mla", ROWS)):
        m = np.zeros((P, 768), np.float32)
        for b, (at, w) in SCORE_AT.items():
            q, k = (b * P + i)[:, None], np.arange(w)[None]
            m[:, at:at + w] = np.where((k <= q) & (q - k < window) & (k >= PAD), 0.0, NEG)
        put(name, m)
    return c


class Steps:

    def __init__(self, eng, sem):
        self.eng, self.sem, self.n = eng, sem, 0

    def did(self, ins):
        ins.then_inc(self.sem, 1)
        self.n += 1

    def settle(self):
        self.eng.wait_ge(self.sem, self.n)

    def chain(self, ins):
        self.did(ins)
        self.settle()

    def restart(self):
        self.eng.sem_clear(self.sem)
        self.n = 0


def groups_and_units():
    plan = []
    blocks = range(NB)
    plan.append(("tr", None, [("tr_attn", b, h) for b in blocks for h in range(2)]))
    plan.append(("in_qa", "w", [("qa", b) for b in blocks]))
    plan.append(("in_mid", "w", [("mid", b) for b in blocks]))
    plan.append(("in_low", "w", [("low", b) for b in blocks]))
    plan.append(("tr", None, [("tr_low", b, h) for b in blocks for h in range(2)]))
    plan.append(("uq", "w", [("uq", b, h) for b in blocks for h in range(2)]))
    plan.append(("ukv", "w", [("ukv", b, h) for b in blocks for h in range(2)]))
    plan.append(("tr", None, [("tr_o", b, h) for b in blocks for h in range(2)]))
    plan.append(("attn_out0", "w", [("ao", b, 0) for b in blocks]))
    plan.append(("attn_out1", "w", [("ao", b, 1) for b in blocks]))
    plan.append(("tr", None, [("tr_ffn0", b, h) for b in blocks for h in range(2)]))
    plan.append(("tr", None, [("sk", 0), ("sk", 1)]))
    plan.append(("wq0_0", "w", [("pq0", h) for h in range(4)]))
    plan.append(("wq0_1", "w", [("pq0", h) for h in range(4, 8)]))
    for n, bs in enumerate(((0, 1), (2,))):
        full = bs[-1]
        plan.append(("tr", None, [("tr_gla", b, h) for b in bs for h in range(2)]))
        plan.append(("gq", "w", [("gq", full)]))
        plan.append(("gk", "w", [("gk", b) for b in bs]))
        for h in range(2):
            plan.append((f"gv{h}", "w", [("gv", b, h) for b in bs]))
        for h in range(2):
            plan.append((f"gr{h}", "w", [("gr", full, h)]))
        for b in bs:
            whole = b == full
            plan.append(("x", None, [("g1", b), ("g1T", b), ("la", b), ("after", b), ("decay", b)]
                         + ([("cum", b), ("tr_qd", b), ("tr_kd", b), ("att", b)] if whole else [])))
            for h in range(GH):
                plan.append(("x", None, [("o", b, h)] * whole + [("st", b, 0, h), ("st", b, 1, h)]))
        plan.append(("tr", None, [("tr_go", full, h) for h in range(2)]))
        for h in range(2):
            plan.append((f"gla_out{h}", "w", [("go", full, h)]))
        plan.append(("tr", None, [("tr_ffn1", full, h) for h in range(2)]))
        for h in range(2):
            plan.append((f"wq1_{h}", "w", [("pq1", full, x) for x in range(4 * h, 4 * h + 4)]))
    return plan


PLAN = groups_and_units()
UNITS = [u for _, _, us in PLAN for u in us]
UNIT_AT = {u: n for n, u in enumerate(UNITS)}
assert len(UNIT_AT) == len(UNITS)
WEIGHTS = [(g, us) for g, w, us in PLAN if w]
UNIT_BANKS = (5, 6, 7)

SEGMENTS = [(0, 0, 7, 7), (0, 1, 0, 7), (0, 2, 0, 7), (1, 1, 0, 7), (1, 2, 0, 7)]
TILE0 = [0, 1, 9, 17, 25]


def build(nc, io, upto="all"):
    ctx = ExitStack()
    with ctx:
        def sb(name, shape, dt=F32):
            return ctx.enter_context(nc.sbuf_tensor(name, shape, dt))

        def sem(name):
            return ctx.enter_context(nc.semaphore(name))

        h = sb("h", [P, NB, D])
        hn = sb("hn", [P, NB, D])
        hT = sb("hT", [P, KC, ROWS])
        gain = sb("gain", [P, 2, D])
        qT = sb("qT", [P, LIVE * PH])
        skT = sb("skT", [P, 2, 2 * N_KEYS])
        con = sb("con", [P, LIVE_CONSTS])
        wring = sb("wring", [P, WSLOTS, KC * 512])
        arena = sb("arena", [P, 2 * RING * D + TOPK * P])
        gws = sb("gws", [P, 8704])
        small = sb("small", [P, 64])
        g1w = sb("g1w", [P, KC, RANK])
        wgate = sb("wgate", [32, GKD])
        onorm = sb("onorm", [P, GV])

        def part(t, at, *shape):
            n = int(np.prod(shape))
            ap = t[:, at:at + n]
            if len(shape) == 1:
                return ap
            names = "abcd"[:len(shape)]
            return ap.rearrange(f"p ({' '.join(names)}) -> p {' '.join(names)}", **dict(zip(names, shape)))

        def const(name):
            at, w = CONST_AT[name]
            return con[:, at:at + w]

        ident = const("ident")
        bank = ctx.enter_context(nc.psum_tensor("bank", [P, 8 * 512], F32))

        def bk(n, a=0, b=512):
            return bank[:, n * 512 + a:n * 512 + b]

        at = 0

        def take(*shape):
            nonlocal at
            ap = part(arena, at, *shape)
            at += int(np.prod(shape))
            return ap

        q_swa = take(NB, HALF, HD)
        k_swa = take(NB, 2, HD)
        v_all = take(NB, HEADS, HD)
        q_mla = take(NB, HALF, QD)
        k_mla = take(NB, HALF, QD)
        low = take(NB, Q_LORA + KV_LORA + 2 * ROPE)
        acon = take(CONST_COLS - LIVE_CONSTS)
        rotate_at = at
        q_stage = take(2, NB, QD)
        k_stage = take(2, NB, QD)
        qT_head = take(2, ROWS)
        kT_head = take(2, ROWS)
        prob = take(2, 768)
        probT = take(768)
        sink = take(HEADS)
        stat = take(2, 16)
        rt = part(arena, rotate_at, 4 * NB * HALF * ROPE)
        assert at <= 2 * RING * D + TOPK * P, at
        low_gain = gain[:, 1, 0:Q_LORA + KV_LORA]

        def acst(name):
            a, w = CONST_AT[name]
            return acon[:, a - LIVE_CONSTS:a - LIVE_CONSTS + w]

        urow = part(arena, 0, RING, D)
        vrow = part(arena, RING * D, RING, D)
        wplace = part(arena, 2 * RING * D, TOPK, P)
        pick_now = sb("pick_now", [P, P])
        q_now = sb("q_now", [P, P])
        top = sb("top", [P, 2, TOPK])
        top_i = sb("top_i", [P, 2, TOPK], U32)
        top_f = sb("top_f", [P, 2, TOPK])
        pairs = sb("pairs", [P, 2 * TOPK * TOPK])
        cand = pairs[:, 0:256]
        cand_rest = pairs[:, 256:512]
        onehot = part(pairs, 0, 2 * TOPK, TOPK)
        rest = part(pairs, 256, 2, N_KEYS)
        best = sb("best", [P, TOPK])
        best_j = sb("best_j", [P, TOPK], U32)
        digit = sb("digit", [P, 2, TOPK], U32)
        digit_f = sb("digit_f", [P, 2, TOPK])
        picked = sb("picked", [P, 2, TOPK])
        idx_next = sb("idx_next", [P, TOPK], U32)
        idx_now = sb("idx_now", [P, 2, TOPK], U32)
        dots = sb("dots", [P, TOPK])
        gl = sb("gl", [P, 4, TOPK])
        gate = sb("gate", [P, TOPK])
        gate_e = sb("gate_e", [P, TOPK])
        z = sb("z", [P, 4])
        wgt = sb("wgt", [P, TOPK])
        xrep = bank[:, 0:1024]
        score = bk(2, 0, 256)
        yacc = bank[:, 1536:2560]

        gq = part(gws, 0, GKD)
        gk = part(gws, 512, 2, GKD)
        gv = part(gws, 1536, 2, GVD)
        gr = part(gws, 3584, GVD)
        la = part(gws, 4608, GKD)
        ex = part(gws, 5120, GKD)
        qdT = part(gws, 5632, GKD)
        kdT = part(gws, 6144, GKD)
        atm = part(gws, 6656, GKD)
        state = part(gws, 7168, GH, GV)
        og = gws[:, 4608:5632]
        sq = gws[:, 0:1024]
        g1T = part(gws, 8192, P)
        g1 = part(gws, 8320, 32)
        dec = part(gws, 8352, 2 * GH)
        gms = part(gws, 8368, 16)

        x_in = sem("x_in")
        con_in = sem("con_in")
        small_in = sem("small_in")
        gain_in = [sem("gain_in0"), sem("gain_in1")]
        w_in = [sem(f"w_in{i}") for i in range(WSLOTS)]
        filled = [sem(f"filled{i}") for i in UNIT_BANKS]
        emptied = [sem(f"emptied{i}") for i in UNIT_BANKS]
        d_step = sem("d_step")
        a_step = sem("a_step")
        norm_ms = sem("norm_ms")
        norm_rs = sem("norm_rs")
        hn_ready = sem("hn_ready")
        low_ready = sem("low_ready")
        heads_ready = sem("heads_ready")
        staged = sem("staged")
        transposed = sem("transposed")
        qT_ready = sem("qT_ready")
        kT_ready = sem("kT_ready")
        scored = sem("scored")
        masked = sem("masked")
        nm_ready = sem("nm_ready")
        probs_ready = sem("probs_ready")
        p_transposed = sem("p_transposed")
        pt_low = sem("pt_low")
        pt_high = sem("pt_high")
        pv_done = sem("pv_done")
        o_taken = sem("o_taken")
        minus_abs = sem("minus_abs")
        gate_log = sem("gate_log")
        decay_ready = sem("decay_ready")
        qd_ready = sem("qd_ready")
        kd_ready = sem("kd_ready")
        kend_ready = sem("kend_ready")
        silu_in = sem("silu_in")
        silu_exp = sem("silu_exp")
        og_ready = sem("og_ready")
        den_ready = sem("den_ready")
        u_in = [sem(f"u_in{i}") for i in range(RING)]
        v_in = [sem(f"v_in{i}") for i in range(RING)]
        u_used = sem("u_used")
        v_used = sem("v_used")
        idx_ready = sem("idx_ready")
        idx_taken = sem("idx_taken")
        go = {e: sem(f"go_{e}") for e in ("pool", "act", "dve", "pe")}
        pad_zero = sem("pad_zero")
        sk_zero = sem("sk_zero")
        pick_ready = sem("pick_ready")
        qnow_ready = sem("qnow_ready")
        xrep_ready = sem("xrep_ready")
        scores_ready = sem("scores_ready")
        topk_step = sem("topk_step")
        mix_step = sem("mix_step")
        best_ready = sem("best_ready")
        gate_exp = sem("gate_exp")
        gelu_in = sem("gelu_in")
        gelu_exp = sem("gelu_exp")
        wgt_ready = sem("wgt_ready")
        placed = sem("placed")
        y_added = sem("y_added")
        out_done = sem("out_done")

        def at_least(eng, semaphore, n):
            if not (isinstance(n, int) and n <= 0):
                eng.wait_ge(semaphore, n)

        def unit_bank(u):
            return UNIT_BANKS[UNIT_AT[u] % 3]

        def wait_filled(eng, u):
            n = UNIT_AT[u]
            eng.wait_ge(filled[n % 3], n // 3 + 1)

        def wait_emptied(eng, u):
            n = UNIT_AT[u]
            eng.wait_ge(emptied[n % 3], n // 3 + 1)

        def is_emptied(ins, u):
            ins.then_inc(emptied[UNIT_AT[u] % 3], 1)

        def last_unit(group):
            return WEIGHTS[group][1][-1]

        def group_of(name, nth=0):
            return [n for n, (g, _) in enumerate(WEIGHTS) if g == name][nth]

        block = ctx.enter_context(nc.Block())

        gains = [io["attn_norm"], io["ffn_norm"][0:1, :], io["gla_norm"], io["ffn_norm"][1:2, :], io["gla_norm"],
                 io["ffn_norm"][1:2, :], io["final_norm"]]
        NORMS = [(0, b) for b in range(3)] + [(1, b) for b in range(3)] + [(2, 0), (2, 1), (3, 1), (4, 2), (5, 2), (6, 1), (6, 2)]

        def wait_normed(eng, n, b):
            eng.wait_ge(hn_ready, NORMS.index((n, b)) + 1)

        @block.sync
        def _(sp):
            sp.dma_start(h[PAD:P, 0, :], io["meta_tokens"]).then_inc(x_in, 16)
            sp.dma_start(h[:, 1:3, :], io["x"].rearrange("a (b p) d -> p (a b) d", p=P)).then_inc(x_in, 16)

            def load_gain(n):
                sp.dma_start(gain[:, n % 2, :], gains[n].broadcast_to([P, D])).then_inc(gain_in[n % 2], 16)

            load_gain(0)
            sp.dma_start(con[:, :], io["consts"][:, 0:LIVE_CONSTS]).then_inc(con_in, 16)
            sources = {
                "in_qa": (io["attn_w_in"][0, :, 0:512], KC), "in_mid": (io["attn_w_in"][0, :, 512:1024], KC),
                "in_low": (io["attn_w_in"][0, :, 1024:1440], KC),
                "uq": (io["mla_w_uq"][0], Q_LORA // P), "ukv": (io["mla_w_ukv"][0], KV_LORA // P),
                "gq": (io["gla_w_in"][0, :, 0:512], KC), "gk": (io["gla_w_in"][0, :, 512:1024], KC),
            }
            for i in range(2):
                c = slice(512 * i, 512 * i + 512)
                sources[f"attn_out{i}"] = (io["attn_w_out"][0, :, c], KC)
                sources[f"gla_out{i}"] = (io["gla_w_out"][0, :, c], KC)
                sources[f"wq0_{i}"] = (io["peer_w_query"][0, :, c], KC)
                sources[f"wq1_{i}"] = (io["peer_w_query"][1, :, c], KC)
                sources[f"gv{i}"] = (io["gla_w_in"][0, :, 1024 + 512 * i:1536 + 512 * i], KC)
                sources[f"gr{i}"] = (io["gla_w_in"][0, :, 2048 + 512 * i:2560 + 512 * i], KC)

            def load_group(n):
                if n >= WSLOTS:
                    wait_filled(sp, last_unit(n - WSLOTS))
                src, kc = sources[WEIGHTS[n][0]]
                w = src.shape[1]
                sp.dma_start(part(wring[:, n % WSLOTS, :], 0, kc, w),
                             src.rearrange("(k p) n -> p k n", p=P)).then_inc(w_in[n % WSLOTS], 16)

            load_group(0)
            sp.dma_start(acon, io["consts"][:, LIVE_CONSTS:CONST_COLS]).then_inc(small_in, 16)
            sp.dma_start(low_gain[:, 0:Q_LORA], io["mla_q_norm"].broadcast_to([P, Q_LORA])).then_inc(small_in, 16)
            sp.dma_start(low_gain[:, Q_LORA:], io["mla_kv_norm"].broadcast_to([P, KV_LORA])).then_inc(small_in, 16)
            sp.dma_start(sink[:, 0:HALF], io["swa_sinks"].broadcast_to([P, HALF])).then_inc(small_in, 16)
            for layer in range(2):
                sp.dma_start(cand[:, P * layer:P * layer + P].rearrange("n (s d) -> n s d", s=2),
                             io["peer_sub_keys"][layer].rearrange("s n d -> n s d")).then_inc(small_in, 16)
            load_group(1)
            sp.dma_start(g1w[:, :, :], io["gla_w_in"][0, :, 3072:3088].rearrange("(k p) n -> p k n", p=P)).then_inc(small_in, 16)
            sp.dma_start(wgate[0:RANK, :], io["gla_w_gate"][0]).then_inc(small_in, 16)
            sp.dma_start(wgate[RANK:RANK + 1, :], io["gla_b_gate"]).then_inc(small_in, 16)
            sp.dma_start(onorm[:, :], io["gla_out_norm"].broadcast_to([P, GV])).then_inc(small_in, 16)
            for n in range(2, group_of("attn_out0")):
                load_group(n)
            sp.wait_ge(low_ready, 1)
            load_gain(1)
            for n in range(group_of("attn_out0"), len(WEIGHTS)):
                if n == group_of("wq0_0"):
                    wait_normed(sp, 0, 2)
                    load_gain(2)
                if n == group_of("gq", 0):
                    wait_normed(sp, 1, 2)
                    load_gain(3)
                if n == group_of("wq1_0", 0):
                    wait_normed(sp, 2, 1)
                    load_gain(4)
                if n == group_of("gq", 1):
                    wait_normed(sp, 3, 1)
                    load_gain(5)
                if n == group_of("wq1_0", 1):
                    wait_normed(sp, 4, 2)
                    load_gain(6)
                load_group(n)
                if upto != "all" and n == group_of("wq0_1"):
                    return
            for i in range(2):
                wait_normed(sp, 6, i + 1)
                sp.dma_start(io["out"][0, P * i:P * i + P, :], hn[:, i + 1, :]).then_inc(out_done, 16)
            sp.wait_ge(out_done, 32)

        @block.gpsimd
        def _(pool):
            n_root = [0]

            def root(ap_in, ap_out, w):
                n_root[0] += 1
                pool.wait_ge(norm_ms, n_root[0])
                nc.gpsimd.tensor_tensor(ap_out, ap_in, const("neghalf")[:, 0:w], ALU.pow).then_inc(norm_rs, 1)

            pool.wait_ge(con_in, 16)
            root(small[:, 0:3], small[:, 3:6], 3)
            root(small[:, 6:12], small[:, 12:18], 6)

            def stage(hh, local, par, q_all, k_all, width, kv):
                pool.wait_ge(transposed, hh + 1)
                pool.sem_inc(go["pool"], 1)
                nc.gpsimd.tensor_copy(q_stage[:, par, :, 0:width], q_all[:, :, local, 0:width]).then_inc(staged, 1)
                nc.gpsimd.tensor_copy(k_stage[:, par, :, 0:width], k_all[:, :, kv, 0:width]).then_inc(staged, 1)

            pool.wait_ge(heads_ready, 1)
            for kind, (qa, ka, wd) in enumerate(((q_swa, k_swa, HD), (q_mla, k_mla, QD))):
                with pool.Fori(0, HALF // 2) as j:
                    for par in range(2):
                        stage(HALF * kind + 2 * j + par, 2 * j + par, par, qa, ka, wd,
                              2 * j + par if kind else j // 2)
            root(small[:, 0:3], small[:, 3:6], 3)

            def gathers(g, par, layer):
                pool.wait_ge(idx_ready, g + 1)
                pool.sem_inc(go["pool"], 1)
                nc.gpsimd.tensor_copy(idx_now[:, par, :], idx_next[:, :]).then_inc(idx_taken, 1)
                pool.wait_ge(idx_taken, g + 1)
                pool.sem_inc(go["pool"], 1)
                for table, rows, used, landed in ((io["peer_u"], urow, u_used, u_in), (io["peer_v"], vrow, v_used, v_in)):
                    for k in range(TOPK):
                        pool.wait_ge(used, TOPK * g + k + 1)
                        pool.sem_inc(go["pool"], 1)
                        nc.gpsimd.indirect_dma_start(
                            out=rows[:, k % RING, :], out_offset=None, in_=table.rearrange("l e d -> (l e) d"),
                            in_offset=bass.IndirectOffsetOnAxis(ap=idx_now[:, par, k:k + 1], axis=0)).then_inc(landed[k % RING], 16)

            def segment(s):
                layer, b, j0, j1 = SEGMENTS[s]
                if j0 < j1:
                    with pool.Fori(0, (j1 - j0 + 1) // 2) as j:
                        for i in range(2):
                            gathers(TILE0[s] + 2 * j + i, (TILE0[s] + i) % 2, layer)
                else:
                    gathers(TILE0[s], TILE0[s] % 2, layer)

            if upto == "attn":
                return
            for s in range(3):
                segment(s)
            if upto == "peer0":
                return
            for full in (1, 2):
                b = 0 if full == 1 else 2
                root(small[:, b:full + 1], small[:, 3 + b:4 + full], full + 1 - b)
                root(gms[:, 0:4], gms[:, 4:8], 4)
                root(small[:, full:full + 1], small[:, 3 + full:4 + full], 1)
            for s in range(3, 5):
                segment(s)
            for b in (1, 2):
                root(small[:, b:b + 1], small[:, 3 + b:4 + b], 1)

        @block.tensor
        def _(pe):
            pe.sem_inc(transposed, 2)
            pe.sem_inc(p_transposed, 2)
            pe.sem_inc(v_used, RING)

            def begin(u):
                n = UNIT_AT[u]
                if n >= 3:
                    pe.wait_ge(emptied[n % 3], n // 3)
                return UNIT_BANKS[n % 3]

            def end(ins, u):
                ins.then_inc(filled[UNIT_AT[u] % 3], 1)

            def transposes(u, sources, width=P, parts=P):
                b = begin(u)
                for i, src in enumerate(sources):
                    last = nc.tensor.transpose(bank[0:width, b * 512 + i * P:b * 512 + i * P + parts], src, ident)
                end(last, u)

            group = [0]

            def weights(name):
                n = group[0]
                assert WEIGHTS[n][0] == name, (WEIGHTS[n], name)
                group[0] += 1
                pe.wait_ge(w_in[n % WSLOTS], 16 * (n // WSLOTS + 1))
                return wring[:, n % WSLOTS, :]

            def project(u, w, lhs, n_k, width):
                b = begin(u)
                for k in range(n_k):
                    last = nc.tensor.matmul(bk(b, 0, width), lhs(k), w(k), start=(k == 0), stop=(k == n_k - 1))
                end(last, u)

            def rows_T(b):
                return lambda k: hT[:, k, b * P:b * P + P]

            def tr_stream(name, n, b, src=None):
                src = src or (lambda c: hn[:, b, c * P:c * P + P])
                if n is not None:
                    wait_normed(pe, n, b)
                for half in range(2):
                    transposes((name, b, half), [src(4 * half + i) for i in range(4)])

            def group_cols(w, width):
                v = part(w, 0, KC, width)
                return lambda k: v[:, k, :]

            pe.wait_ge(con_in, 16)
            for b in range(NB):
                tr_stream("tr_attn", 0, b)
            for name, u, width in (("in_qa", "qa", 512), ("in_mid", "mid", 512), ("in_low", "low", 416)):
                w = weights(name)
                for b in range(NB):
                    if name == "in_qa":
                        for half in range(2):
                            wait_emptied(pe, ("tr_attn", b, half))
                    project((u, b), group_cols(w, width), rows_T(b), KC, width)
            pe.wait_ge(low_ready, 1)
            for b in range(NB):
                for half, cs in enumerate((range(0, 4), range(4, 5))):
                    transposes(("tr_low", b, half), [low[:, b, c * P:c * P + P] for c in cs])
            w = part(weights("uq"), 0, Q_LORA // P, HALF * QD)
            for b in range(NB):
                for half in range(2):
                    wait_emptied(pe, ("tr_low", b, half))
                for half in range(2):
                    project(("uq", b, half), lambda k: w[:, k, 384 * half:384 * half + 384], rows_T(b), 3, 384)
            w = part(weights("ukv"), 0, KV_LORA // P, D)
            for b in range(NB):
                for half in range(2):
                    project(("ukv", b, half), lambda k: w[:, k, 512 * half:512 * half + 512],
                            lambda k: hT[:, 3 + k, b * P:b * P + P], 2, 512)

            def front(hh, par, width, prev=True):
                pe.wait_ge(staged, 2 * hh + 2)
                at_least(pe, qT_ready, hh)
                at_least(pe, kT_ready, hh)
                pe.sem_inc(go["pe"], 1)
                for i, st in enumerate((q_stage, k_stage)):
                    for b in range(NB):
                        last = nc.tensor.transpose(bank[0:width, i * 512 + b * P:i * 512 + b * P + P], st[:, par, b, 0:width], ident)
                last.then_inc(transposed, 1)
                pe.wait_ge(qT_ready, hh + 1)
                pe.wait_ge(kT_ready, hh + 1)
                at_least(pe, masked, NB * hh)
                pe.sem_inc(go["pe"], 1)
                for b in (2, 0, 1):
                    a, w = SCORE_AT[b]
                    last = nc.tensor.matmul(bank[:, 1024 + a:1024 + a + w], qT_head[0:width, par, b * P:b * P + P],
                                            kT_head[0:width, par, 0:w], start=True, stop=True)
                last.then_inc(scored, 1)

            def back(hh, par):
                pe.wait_ge(probs_ready, hh + 1)
                pe.wait_ge(pt_low, hh + 1)
                pe.wait_ge(pt_high, hh + 1)
                pe.sem_inc(go["pe"], 1)
                for c in range(6):
                    last = nc.tensor.transpose(bank[:, 2048 + c * P:2048 + c * P + P], prob[:, par, c * P:c * P + P], ident)
                last.then_inc(p_transposed, 1)
                pe.wait_ge(pt_low, hh + 2)
                pe.wait_ge(pt_high, hh + 2)
                pe.wait_ge(o_taken, hh + 1)
                pe.sem_inc(go["pe"], 1)
                for b in range(NB):
                    a = SCORE_AT[b][0]
                    for kb in range(b + 1):
                        last = nc.tensor.matmul(bk(6, b * HD, b * HD + HD), probT[:, a + kb * P:a + kb * P + P],
                                                v_all[:, kb, hh, :], start=(kb == 0), stop=(kb == b))
                last.then_inc(pv_done, 1)

            pe.wait_ge(heads_ready, 1)
            for kind, width in ((0, HD), (1, QD)):
                base = HALF * kind
                front(base, 0, width)
                with pe.Fori(0, HALF // 2 - 1) as j:
                    front(base + 2 * j + 1, 1, width)
                    back(base + 2 * j, 0)
                    front(base + 2 * j + 2, 0, width)
                    back(base + 2 * j + 1, 1)
                front(base + HALF - 1, 1, width)
                back(base + HALF - 2, 0)
                back(base + HALF - 1, 1)

            pe.wait_ge(o_taken, HEADS + 1)
            for b in range(NB):
                tr_stream("tr_o", None, b)
            for i in range(2):
                w = weights(f"attn_out{i}")
                for b in range(NB):
                    if i == 0:
                        for half in range(2):
                            wait_emptied(pe, ("tr_o", b, half))
                    project(("ao", b, i), group_cols(w, 512), rows_T(b), KC, 512)
            for b in range(NB):
                tr_stream("tr_ffn0", 1, b)
            for layer in range(2):
                transposes(("sk", layer), [cand[:, layer * P:layer * P + P]])
            for b in range(NB):
                for half in range(2):
                    wait_emptied(pe, ("tr_ffn0", b, half))
            for i in range(2):
                w = part(weights(f"wq0_{i}"), 0, KC, 512)
                for x in range(4):
                    b = begin(("pq0", 4 * i + x))
                    for k in range(KC):
                        last = nc.tensor.matmul(bk(b, 0, LIVE), w[:, k, x * P:x * P + P], hT[:, k, PAD:ROWS],
                                                start=(k == 0), stop=(k == KC - 1))
                    end(last, ("pq0", 4 * i + x))
            if upto == "attn":
                return

            def prepare(g, layer, b):
                pe.wait_ge(pick_ready, g + 1)
                pe.wait_ge(u_used, RING + TOPK * g)
                pe.sem_inc(go["pe"], 1)
                for i in range(2):
                    last = nc.tensor.matmul(bk(i), pick_now[:, :], hn[:, b, 512 * i:512 * i + 512], start=True, stop=True)
                last.then_inc(xrep_ready, 1)
                pe.wait_ge(qnow_ready, g + 1)
                pe.sem_inc(go["pe"], 1)
                nc.tensor.matmul(score, q_now[:, :], skT[:, layer, :], start=True, stop=True).then_inc(scores_ready, 1)

            def mix(g):
                for k in range(TOPK):
                    pe.wait_ge(v_in[k % RING], 16 * (2 * g + k // RING + 1))
                    pe.wait_ge(placed, TOPK * g + k + 1)
                    if k == 0:
                        at_least(pe, y_added, g)
                    pe.sem_inc(go["pe"], 1)
                    for i in range(2):
                        last = nc.tensor.matmul(yacc[:, 512 * i:512 * i + 512], wplace[:, k, :],
                                                vrow[:, k % RING, 512 * i:512 * i + 512], start=(k == 0), stop=(k == TOPK - 1))
                    last.then_inc(v_used, 1)

            def segment(s, more):
                layer, b, j0, j1 = SEGMENTS[s]
                if j0 < j1:
                    with pe.Fori(0, j1 - j0) as j:
                        prepare(TILE0[s] + j + 1, layer, b)
                        mix(TILE0[s] + j)
                g = TILE0[s] + j1 - j0
                if more:
                    prepare(g + 1, *SEGMENTS[s + 1][:2])
                mix(g)

            prepare(0, 0, 0)
            for s in range(3):
                segment(s, s < 2)
            if upto == "peer0":
                return

            def gla(blocks):
                full = blocks[-1]
                for b in blocks:
                    tr_stream("tr_gla", 2 if b < 2 else 4, b)
                for b in blocks:
                    for half in range(2):
                        wait_emptied(pe, ("tr_gla", b, half))
                for name, u, bs in [("gq", ("gq",), [full]), ("gk", ("gk",), blocks)] \
                        + [(f"gv{i}", ("gv", i), blocks) for i in range(2)] + [(f"gr{i}", ("gr", i), [full]) for i in range(2)]:
                    w = weights(name)
                    for b in bs:
                        project((u[0], b) + u[1:], group_cols(w, 512), rows_T(b), KC, 512)
                for b in blocks:
                    slot = 0 if b == full else 1
                    project(("g1", b), lambda k: g1w[:, k, :], rows_T(b), KC, RANK)
                    wait_emptied(pe, ("g1", b))
                    transposes(("g1T", b), [g1[:, 0:RANK]], width=RANK)
                    wait_emptied(pe, ("g1T", b))
                    u = begin(("la", b))
                    end(nc.tensor.matmul(bk(u), g1T[0:RANK + 1, :], wgate[0:RANK + 1, :], start=True, stop=True), ("la", b))
                    pe.wait_ge(decay_ready, b + 1)
                    u = begin(("after", b))
                    end(nc.tensor.matmul(bk(u), const("after"), la, start=True, stop=True), ("after", b))
                    u = begin(("decay", b))
                    for x in range(GH):
                        last = nc.tensor.matmul(bk(u, 2 * x, 2 * x + 2), la[:, x * GK:x * GK + GK], const("chunks"), start=True, stop=True)
                    end(last, ("decay", b))
                    if b == full:
                        u = begin(("cum", b))
                        end(nc.tensor.matmul(bk(u), const("tri"), la, start=True, stop=True), ("cum", b))
                        pe.wait_ge(qd_ready, b)
                        transposes(("tr_qd", b), [gq[:, x * GK:x * GK + GK] for x in range(GH)])
                        pe.wait_ge(kd_ready, b)
                        transposes(("tr_kd", b), [ex[:, x * GK:x * GK + GK] for x in range(GH)])
                        wait_emptied(pe, ("tr_qd", b))
                        wait_emptied(pe, ("tr_kd", b))
                        u = begin(("att", b))
                        for x in range(GH):
                            c = slice(x * GK, x * GK + GK)
                            last = nc.tensor.matmul(bk(u, x * GK, x * GK + GK), kdT[:, c], qdT[:, c], start=True, stop=True)
                        end(last, ("att", b))
                    pe.wait_ge(kend_ready, b + 1)
                    if b == full:
                        wait_emptied(pe, ("att", b))
                    for x in range(GH):
                        vh = gv[:, slot, x * GV:x * GV + GV]
                        for c in range(2):
                            rs = slice(c * CHUNK, c * CHUNK + CHUNK)
                            if b == full:
                                if c == 0:
                                    ub = begin(("o", b, x))
                                    nc.tensor.matmul(bk(ub, 0, GV), atm[:, x * GK:x * GK + GK], vh, start=True, stop=False)
                                if c == 1:
                                    wait_emptied(pe, ("st", b, 0, x))
                                elif b == 1:
                                    wait_emptied(pe, ("st", 0, 1, x))
                                else:
                                    wait_emptied(pe, ("st", 1, 1, x))
                                last = nc.tensor.matmul(bank[rs, ub * 512:ub * 512 + GV], qdT[:, x * GK + c * CHUNK:x * GK + c * CHUNK + CHUNK],
                                                        state[:, x, :], start=False, stop=True)
                                if c == 1:
                                    end(last, ("o", b, x))
                            us = begin(("st", b, c, x))
                            end(nc.tensor.matmul(bk(us, 0, GV), gk[rs, slot, x * GK:x * GK + GK], vh[rs, :], start=True, stop=True), ("st", b, c, x))
                pe.wait_ge(og_ready, full)
                for half in range(2):
                    transposes(("tr_go", full, half), [og[:, (4 * half + i) * P:(4 * half + i) * P + P] for i in range(4)])
                for half in range(2):
                    wait_emptied(pe, ("tr_go", full, half))
                for i in range(2):
                    w = weights(f"gla_out{i}")
                    project(("go", full, i), group_cols(w, 512), rows_T(full), KC, 512)
                tr_stream("tr_ffn1", 3 if full == 1 else 5, full)
                for half in range(2):
                    wait_emptied(pe, ("tr_ffn1", full, half))
                for i in range(2):
                    w = part(weights(f"wq1_{i}"), 0, KC, 512)
                    for x in range(4):
                        un = ("pq1", full, 4 * i + x)
                        b = begin(un)
                        for k in range(KC):
                            last = nc.tensor.matmul(bk(b, 0, P), w[:, k, x * P:x * P + P], hT[:, k, full * P:full * P + P],
                                                    start=(k == 0), stop=(k == KC - 1))
                        end(last, un)

            gla((0, 1))
            gla((2,))
            prepare(17, 1, 1)
            segment(3, True)
            segment(4, False)

        @block.scalar
        def _(act):
            def copy_unit(u, dst, src=None, width=512, parts=P):
                b = unit_bank(u)
                wait_filled(act, u)
                is_emptied(nc.scalar.activation(dst, bank[0:parts, b * 512:b * 512 + width] if src is None else src(b),
                                                ACT.Copy), u)

            def take_T(name, b, chunks=((0, 4), (4, 8))):
                for half, (c0, c1) in enumerate(chunks):
                    n = c1 - c0
                    copy_unit((name, b, half), hT[:, c0:c1, b * P:b * P + P],
                              lambda u: bk(u, 0, n * P).rearrange("p (c n) -> p c n", c=n))

            act.sem_inc(pt_low, 1)
            for b in range(NB):
                take_T("tr_attn", b)
            for b in range(NB):
                take_T("tr_low", b, ((0, 4), (4, 5)))

            def front_q(hh, par, width):
                act.wait_ge(transposed, hh + 3)
                nc.scalar.activation(qT_head[0:width, par, :], bank[0:width, 0:ROWS], ACT.Copy).then_inc(qT_ready, 1)

            def back_pt(hh):
                act.wait_ge(p_transposed, hh + 3)
                nc.scalar.activation(probT[:, 0:512], bk(4), ACT.Copy).then_inc(pt_low, 1)

            def exps(hh, par):
                act.wait_ge(nm_ready, hh + 1)
                act.sem_inc(go["act"], 1)
                nm = stat[:, par, 3:6]
                for b in range(NB):
                    a, w = SCORE_AT[b]
                    nc.scalar.activation(prob[:, par, a:a + w], prob[:, par, a:a + w], ACT.Exp, bias=nm[:, b:b + 1],
                                         accum_out=stat[:, par, 6 + b:7 + b])
                nc.scalar.activation(stat[:, par, 9:12], nm, ACT.Exp, bias=sink[:, bass.ds(hh, 1)]).then_inc(probs_ready, 1)

            for kind, width in ((0, HD), (1, QD)):
                base = HALF * kind
                front_q(base, 0, width)
                exps(base, 0)
                with act.Fori(0, HALF // 2 - 1) as j:
                    front_q(base + 2 * j + 1, 1, width)
                    back_pt(base + 2 * j)
                    exps(base + 2 * j + 1, 1)
                    front_q(base + 2 * j + 2, 0, width)
                    back_pt(base + 2 * j + 1)
                    exps(base + 2 * j + 2, 0)
                front_q(base + HALF - 1, 1, width)
                back_pt(base + HALF - 2)
                exps(base + HALF - 1, 1)
                back_pt(base + HALF - 1)
            for b in range(NB):
                take_T("tr_o", b)
            for b in range(NB):
                take_T("tr_ffn0", b)
            act.wait_ge(sk_zero, 1)
            for layer in range(2):
                u = ("sk", layer)
                wait_filled(act, u)
                b = unit_bank(u)
                nc.scalar.activation(skT[0:64, layer, 0:P], bank[0:64, b * 512:b * 512 + P], ACT.Copy)
                is_emptied(nc.scalar.activation(skT[64:P, layer, P:2 * P], bank[64:P, b * 512:b * 512 + P], ACT.Copy), u)
            if upto == "attn":
                return

            pick_all = const("pick")
            place_all = const("place")

            def prepare(g, j, q_tile):
                at_least(act, xrep_ready, g)
                act.sem_inc(go["act"], 1)
                nc.scalar.activation(pick_now[:, :], pick_all[:, bass.ds(P * j, P)], ACT.Copy).then_inc(pick_ready, 1)
                at_least(act, scores_ready, g)
                act.sem_inc(go["act"], 1)
                nc.scalar.activation(q_now[:, :], qT[:, bass.ds(P * q_tile, P)], ACT.Copy).then_inc(qnow_ready, 1)

            def gate_exps(g):
                act.wait_ge(best_ready, g + 1)
                nc.scalar.activation(gate_e[:, :], best[:, :], ACT.Exp, bias=z[:, 0:1], accum_out=z[:, 1:2]).then_inc(gate_exp, 1)

            def mix(g, j):
                act.wait_ge(gelu_in, g + 1)
                nc.scalar.activation(gl[:, 1, :], gl[:, 0, :], ACT.Exp).then_inc(gelu_exp, 1)
                act.wait_ge(wgt_ready, g + 1)
                act.wait_ge(v_used, RING + TOPK * g)
                act.sem_inc(go["act"], 1)
                for k in range(TOPK):
                    nc.scalar.activation(wplace[:, k, :], place_all[:, bass.ds(112 - TT * j, P)], ACT.Copy,
                                         scale=wgt[:, k:k + 1]).then_inc(placed, 1)

            def segment(s, more):
                layer, b, j0, j1 = SEGMENTS[s]
                q0 = P // TT * b + j0 - FIRST_TILE
                if j0 < j1:
                    with act.Fori(0, j1 - j0) as j:
                        prepare(TILE0[s] + j + 1, j + j0 + 1, q0 + j + 1)
                        mix(TILE0[s] + j, j + j0)
                        gate_exps(TILE0[s] + j + 1)
                g = TILE0[s] + j1 - j0
                if more:
                    nb_, nj = SEGMENTS[s + 1][1:3]
                    prepare(g + 1, nj, P // TT * nb_ + nj - FIRST_TILE)
                mix(g, j1)
                if more:
                    gate_exps(g + 1)

            wait_emptied(act, ("pq0", 7))
            prepare(0, 7, 0)
            gate_exps(0)
            for s in range(3):
                segment(s, s < 2)
            if upto == "peer0":
                return

            def gla(blocks):
                full = blocks[-1]
                for b in blocks:
                    take_T("tr_gla", b)
                steps = Steps(act, a_step)
                for b in blocks:
                    act.wait_ge(minus_abs, b + 1)
                    steps.restart()
                    steps.chain(nc.scalar.activation(ex, ex, ACT.Exp))
                    nc.scalar.activation(ex, ex, ACT.Ln, bias=1.0).then_inc(gate_log, 1)
                    if b == full:
                        wait_filled(act, ("cum", b))
                        nc.scalar.activation(qdT, bk(unit_bank(("cum", b))), ACT.Exp)
                        is_emptied(nc.scalar.activation(kdT, bk(unit_bank(("cum", b))), ACT.Exp, scale=-1.0), ("cum", b))
                    wait_filled(act, ("decay", b))
                    is_emptied(nc.scalar.activation(dec, bk(unit_bank(("decay", b)), 0, 2 * GH), ACT.Exp), ("decay", b))
                    wait_filled(act, ("after", b))
                    is_emptied(nc.scalar.activation(la, bk(unit_bank(("after", b))), ACT.Exp), ("after", b))
                    if b == full:
                        act.wait_ge(kd_ready, b)
                        copy_unit(("tr_qd", b), qdT)
                        copy_unit(("tr_kd", b), kdT)
                act.wait_ge(silu_in, full)
                nc.scalar.activation(sq, sq, ACT.Exp).then_inc(silu_exp, 1)
                for half in range(2):
                    copy_unit(("tr_go", full, half), hT[:, 4 * half:4 * half + 4, full * P:full * P + P],
                              lambda u: bk(u).rearrange("p (c n) -> p c n", c=4))
                take_T("tr_ffn1", full)

            gla((0, 1))
            gla((2,))
            prepare(17, 0, 1)
            gate_exps(17)
            segment(3, True)
            segment(4, False)

        @block.vector
        def _(dve):
            v = nc.vector
            steps = Steps(dve, d_step)
            n_norm = [0]

            def unit_ap(u, a=0, b=512):
                wait_filled(dve, u)
                return bk(unit_bank(u), a, b)

            def squares(src, junk, out):
                steps.did(v.tensor_tensor_reduce(out=junk, in0=src, in1=src, scale=1.0, scalar=0.0, op0=ALU.mult,
                                                 op1=ALU.add, accum_out=out))

            def mean(ap, width):
                steps.did(v.tensor_scalar(ap, ap, 1.0 / width, EPS, ALU.mult, ALU.add))

            def roots():
                n_norm[0] += 1
                steps.settle()
                dve.sem_inc(norm_ms, 1)
                dve.wait_ge(norm_rs, n_norm[0])

            def norm(n, blocks):
                for b in blocks:
                    squares(h[:, b, :], hn[:, b, :], small[:, b:b + 1])
                steps.settle()
                mean(small[:, blocks[0]:blocks[-1] + 1], D)
                roots()
                g = min(n, 6)
                dve.wait_ge(gain_in[g % 2], 16 * (g // 2 + 1))
                for b in blocks:
                    v.scalar_tensor_tensor(out=hn[:, b, :], in0=h[:, b, :], scalar=small[:, 3 + b:4 + b], in1=gain[:, g % 2, :],
                                           op0=ALU.mult, op1=ALU.mult).then_inc(hn_ready, 1)

            dve.sem_inc(pt_high, 1)
            dve.sem_inc(o_taken, 1)
            dve.sem_inc(u_used, RING)
            steps.did(v.memset(g1T[0:32, :], 1.0))
            steps.did(v.memset(part(gws, 7168, GH * GV), 0.0))
            steps.did(v.memset(h[0:PAD, 0, :], 0.0))
            v.memset(skT[:, :, :], 0.0).then_inc(sk_zero, 1)
            dve.wait_ge(x_in, 32)
            steps.settle()
            norm(0, range(NB))
            for b in range(NB):
                u = ("qa", b)
                is_emptied(v.tensor_scalar(q_swa[:, b].rearrange("p h d -> p (h d)"), unit_ap(u), HD ** -0.5, None, ALU.mult), u)
            for b in range(NB):
                u = ("mid", b)
                src = unit_ap(u)
                steps.did(v.tensor_copy(k_swa[:, b].rearrange("p h d -> p (h d)"), src[:, 0:P]))
                steps.did(v.tensor_copy(v_all[:, b, 0:HALF, :].rearrange("p (g r) d -> p g r d", g=2),
                                        src[:, P:2 * P].rearrange("p (g d) -> p g d", g=2).unsqueeze(2).broadcast_to([P, 2, 4, HD])))
                is_emptied(v.tensor_copy(low[:, b, 0:256], src[:, 256:512]), u)
            for b in range(NB):
                u = ("low", b)
                is_emptied(v.tensor_copy(low[:, b, 256:672], unit_ap(u, 0, 416)), u)
            dve.wait_ge(small_in, SMALL_LOADS * 16)
            steps.did(v.memset(sink[:, HALF:HEADS], NEG))
            for b in range(NB):
                wait_emptied(dve, ("mid", b))
                wait_emptied(dve, ("low", b))
                squares(low[:, b, 0:Q_LORA], rt[:, 0:Q_LORA], small[:, 6 + b:7 + b])
                steps.settle()
                squares(low[:, b, Q_LORA:Q_LORA + KV_LORA], rt[:, 0:KV_LORA], small[:, 9 + b:10 + b])
                steps.settle()
            mean(small[:, 6:9], Q_LORA)
            mean(small[:, 9:12], KV_LORA)
            roots()
            for b in range(NB):
                for a, w, s in ((0, Q_LORA, 12), (Q_LORA, KV_LORA, 15)):
                    ap = low[:, b, a:a + w]
                    steps.did(v.scalar_tensor_tensor(out=ap, in0=ap, scalar=small[:, s + b:s + b + 1], in1=low_gain[:, a:a + w],
                                                     op0=ALU.mult, op1=ALU.mult))
            steps.settle()
            dve.sem_inc(low_ready, 1)

            def rotate(x1, x2, t, shape, dst1, dst2, wide):
                cos, sin = (acst(n).rearrange("p (b r) -> p b r", b=NB) for n in ("cos", "sin"))
                if len(shape) == 4:
                    cos, sin = (a.unsqueeze(2).broadcast_to(shape) for a in (cos, sin))
                for i, (x, y) in enumerate(((x1, cos), (x2, sin), (x2, cos), (x1, sin))):
                    steps.did(v.tensor_tensor(t[i], x, y, ALU.mult))
                steps.settle()
                steps.did(v.tensor_tensor(dst1, wide(t[0]), wide(t[1]), ALU.subtract))
                steps.did(v.tensor_tensor(dst2, wide(t[2]), wide(t[3]), ALU.add))
                steps.settle()

            n = NB * ROPE
            t = [rt[:, i * n:(i + 1) * n].rearrange("p (b r) -> p b r", b=NB) for i in range(4)]
            rotate(low[:, :, 640:656], low[:, :, 656:672], t, [P, NB, ROPE], k_mla[:, :, :, 64:80], k_mla[:, :, :, 80:96],
                   lambda a: a.unsqueeze(2).broadcast_to([P, NB, HALF, ROPE]))
            for b in range(NB):
                for i in range(2):
                    u = ("uq", b, i)
                    is_emptied(v.tensor_scalar(q_mla[:, b, 4 * i:4 * i + 4, :].rearrange("p h d -> p (h d)"), unit_ap(u, 0, 384),
                                               QD ** -0.5, None, ALU.mult), u)
            for b in range(NB):
                for i in range(2):
                    u = ("ukv", b, i)
                    src = unit_ap(u).rearrange("p (h d) -> p h d", h=4)
                    steps.did(v.tensor_copy(k_mla[:, b, 4 * i:4 * i + 4, 0:HD], src[:, :, 0:HD]))
                    is_emptied(v.tensor_copy(v_all[:, b, HALF + 4 * i:HALF + 4 * i + 4, :], src[:, :, HD:2 * HD]), u)
            n = NB * HALF * ROPE
            t = [rt[:, i * n:(i + 1) * n].rearrange("p (b h r) -> p b h r", b=NB, h=HALF) for i in range(4)]
            for b in range(NB):
                for i in range(2):
                    wait_emptied(dve, ("uq", b, i))
                    wait_emptied(dve, ("ukv", b, i))
            rotate(q_mla[:, :, :, 64:80], q_mla[:, :, :, 80:96], t, [P, NB, HALF, ROPE], q_mla[:, :, :, 64:80],
                   q_mla[:, :, :, 80:96], lambda a: a)
            dve.sem_inc(heads_ready, 2)

            def front(hh, par, width, mask):
                dve.wait_ge(transposed, hh + 3)
                v.tensor_copy(kT_head[0:width, par, :], bank[0:width, 512:512 + ROWS]).then_inc(kT_ready, 1)
                dve.wait_ge(p_transposed, hh + 1)
                dve.wait_ge(scored, hh + 1)
                dve.sem_inc(go["dve"], 1)
                for b in range(NB):
                    a, w = SCORE_AT[b]
                    v.tensor_tensor_reduce(out=prob[:, par, a:a + w], in0=bank[:, 1024 + a:1024 + a + w], in1=mask[:, a:a + w],
                                           scale=1.0, scalar=-3e38, op0=ALU.add, op1=ALU.max,
                                           accum_out=stat[:, par, b:b + 1]).then_inc(masked, 1)
                dve.wait_ge(masked, NB * hh + NB)
                v.tensor_scalar(stat[:, par, 3:6], stat[:, par, 0:3], sink[:, bass.ds(hh, 1)], -1.0, ALU.max, ALU.mult)\
                    .then_inc(nm_ready, 1)

            def back(hh, par):
                dve.wait_ge(p_transposed, hh + 3)
                v.tensor_copy(probT[:, 512:768], bk(5, 0, 256)).then_inc(pt_high, 1)
                dve.wait_ge(probs_ready, hh + 1)
                v.tensor_tensor(stat[:, par, 12:15], stat[:, par, 6:9], stat[:, par, 9:12], ALU.add).then_inc(den_ready, 1)
                dve.wait_ge(den_ready, 2 * hh + 1)
                v.reciprocal(stat[:, par, 12:15], stat[:, par, 12:15]).then_inc(den_ready, 1)
                dve.wait_ge(den_ready, 2 * hh + 2)
                dve.wait_ge(pv_done, hh + 1)
                dve.sem_inc(go["dve"], 1)
                v.tensor_tensor(hn[:, :, bass.ds(hh * HD, HD)], bk(6, 0, NB * HD).rearrange("p (b d) -> p b d", b=NB),
                                stat[:, par, 12:15].unsqueeze(2).broadcast_to([P, NB, HD]), ALU.mult).then_inc(o_taken, 1)

            for kind, width in ((0, HD), (1, QD)):
                base = HALF * kind
                mask = acst("mask_mla" if kind else "mask_swa")
                front(base, 0, width, mask)
                with dve.Fori(0, HALF // 2 - 1) as j:
                    front(base + 2 * j + 1, 1, width, mask)
                    back(base + 2 * j, 0)
                    front(base + 2 * j + 2, 0, width, mask)
                    back(base + 2 * j + 1, 1)
                front(base + HALF - 1, 1, width, mask)
                back(base + HALF - 2, 0)
                back(base + HALF - 1, 1)

            def add_to_h(u, b, i):
                hs = h[:, b, 512 * i:512 * i + 512]
                is_emptied(v.tensor_tensor(hs, hs, unit_ap(u), ALU.add), u)

            for i in range(2):
                for b in range(NB):
                    add_to_h(("ao", b, i), b, i)
            wait_emptied(dve, ("ao", 2, 0))
            wait_emptied(dve, ("ao", 1, 1))
            wait_emptied(dve, ("ao", 2, 1))
            v.memset(h[0:PAD, 0, :], 0.0).then_inc(pad_zero, 1)
            dve.wait_ge(pad_zero, 1)
            norm(1, range(NB))
            for x in range(PH):
                u = ("pq0", x)
                is_emptied(v.tensor_copy(qT[:, :].rearrange("p (t h) -> p t h", h=PH)[:, :, x], unit_ap(u, 0, LIVE)), u)
            if upto == "attn":
                return

            def best16(vals, rest_ap, values, indices, topk):
                topk.chain(v.max(values[:, 0:8], vals))
                topk.did(v.max_index(indices[:, 0:8], values[:, 0:8], vals))
                topk.chain(v.match_replace(rest_ap, values[:, 0:8], vals, -3e38))
                topk.chain(v.max(values[:, 8:16], rest_ap))
                topk.chain(v.max_index(indices[:, 8:16], values[:, 8:16], rest_ap))

            topk = Steps(dve, topk_step)
            mixs = Steps(dve, mix_step)

            def choose(g, layer):
                dve.wait_ge(scores_ready, g + 1)
                at_least(dve, idx_taken, g)
                at_least(dve, gate_exp, g)
                dve.sem_inc(go["dve"], 1)
                topk.restart()
                for s in range(2):
                    best16(score[:, s * P:s * P + P], rest[:, s, :], top[:, s, :], top_i[:, s, :], topk)
                topk.did(v.tensor_copy(top_f[:, :, :], top_i[:, :, :]))
                pair = cand[:, :].rearrange("p (a b) -> p a b", a=TOPK)
                topk.chain(v.tensor_tensor(pair, top[:, 0, :].unsqueeze(2).broadcast_to([P, TOPK, TOPK]),
                                           top[:, 1, :].unsqueeze(1).broadcast_to([P, TOPK, TOPK]), ALU.add))
                best16(cand[:, :], cand_rest[:, :], best, best_j, topk)
                topk.did(v.tensor_scalar(digit[:, 0, :], best_j[:, :], 4, None, ALU.logical_shift_right))
                topk.did(v.tensor_scalar(digit[:, 1, :], best_j[:, :], 15, None, ALU.bitwise_and))
                topk.chain(v.tensor_scalar(z[:, 0:1], best[:, 0:1], -1.0, None, ALU.mult))
                dve.sem_inc(best_ready, 1)
                topk.chain(v.tensor_copy(digit_f[:, :, :], digit[:, :, :]))
                topk.chain(v.tensor_tensor(onehot[:, :, :], digit_f[:, :, :].rearrange("p s k -> p (s k)").unsqueeze(2).broadcast_to([P, 2 * TOPK, TOPK]),
                                           const("iota").unsqueeze(1).broadcast_to([P, 2 * TOPK, TOPK]), ALU.is_equal))
                one = onehot[:, :, :].rearrange("p (s k) a -> p s k a", s=2)
                topk.chain(v.tensor_tensor(one, one, top_f[:, :, :].unsqueeze(2).broadcast_to([P, 2, TOPK, TOPK]), ALU.mult))
                topk.chain(v.tensor_reduce(out=picked[:, :, :].rearrange("p s k -> p (s k)"), in_=onehot[:, :, :], axis=AX, op=ALU.add))
                topk.chain(v.tensor_scalar(picked[:, 0, :], picked[:, 0, :], float(N_KEYS), float(layer * EXPERTS), ALU.mult, ALU.add))
                topk.chain(v.tensor_tensor(idx_next[:, :], picked[:, 0, :], picked[:, 1, :], ALU.add))
                dve.sem_inc(idx_ready, 1)

            def experts(g, b):
                dve.wait_ge(xrep_ready, g + 1)
                dve.sem_inc(go["dve"], 1)
                for k in range(TOPK):
                    dve.wait_ge(u_in[k % RING], 16 * (2 * g + k // RING + 1))
                    v.tensor_tensor_reduce(out=urow[:, k % RING, :], in0=urow[:, k % RING, :], in1=xrep, scale=1.0, scalar=0.0,
                                           op0=ALU.mult, op1=ALU.add, accum_out=dots[:, k:k + 1]).then_inc(u_used, 1)
                dve.wait_ge(u_used, RING + TOPK * (g + 1))
                dve.wait_ge(gate_exp, g + 1)
                dve.sem_inc(go["dve"], 1)
                mixs.restart()
                a, c = gl[:, 0, :], gl[:, 2, :]
                mixs.did(v.reciprocal(z[:, 2:3], z[:, 1:2]))
                mixs.chain(v.tensor_tensor(a, dots[:, :], dots[:, :], ALU.mult))
                mixs.chain(v.tensor_scalar(a, a, 0.044715, 1.0, ALU.mult, ALU.add))
                mixs.chain(v.tensor_tensor(a, a, dots[:, :], ALU.mult))
                mixs.chain(v.tensor_scalar(a, a, -2.0 * GELU_C, 80.0, ALU.mult, ALU.min))
                dve.sem_inc(gelu_in, 1)
                mixs.chain(v.scalar_tensor_tensor(out=gate[:, :], in0=gate_e[:, :], scalar=z[:, 2:3], in1=dots[:, :],
                                                  op0=ALU.mult, op1=ALU.mult))
                dve.wait_ge(gelu_exp, g + 1)
                dve.sem_inc(go["dve"], 1)
                mixs.chain(v.tensor_scalar(c, gl[:, 1, :], 1.0, None, ALU.add))
                mixs.chain(v.reciprocal(c, c))
                mixs.chain(v.tensor_tensor(wgt[:, :], gate[:, :], c, ALU.mult))
                dve.sem_inc(wgt_ready, 1)

            def add_experts(g, b):
                dve.wait_ge(v_used, RING + TOPK * (g + 1))
                v.tensor_tensor(h[:, b, :], h[:, b, :], yacc, ALU.add).then_inc(y_added, 1)
                dve.wait_ge(y_added, g + 1)
                dve.sem_inc(go["dve"], 1)

            def segment(s, more):
                layer, b, j0, j1 = SEGMENTS[s]
                if j0 < j1:
                    with dve.Fori(0, j1 - j0) as j:
                        g = TILE0[s] + j
                        experts(g, b)
                        choose(g + 1, layer)
                        add_experts(g, b)
                g = TILE0[s] + j1 - j0
                experts(g, b)
                if more:
                    choose(g + 1, SEGMENTS[s + 1][0])
                add_experts(g, b)

            wait_emptied(dve, ("sk", 0))
            wait_emptied(dve, ("sk", 1))
            choose(0, 0)
            for s in range(3):
                segment(s, s < 2)
            if upto == "peer0":
                return

            def gla(blocks):
                full = blocks[-1]
                norm(2 if full == 1 else 4, blocks)
                wait_filled(dve, ("gq", full))
                is_emptied(v.tensor_scalar(gq, bk(unit_bank(("gq", full))), GK ** -0.5, None, ALU.mult), ("gq", full))
                for b in blocks:
                    u = ("gk", b)
                    is_emptied(v.tensor_copy(gk[:, int(b != full), :], unit_ap(u)), u)
                for i in range(2):
                    for b in blocks:
                        u = ("gv", b, i)
                        is_emptied(v.tensor_copy(gv[:, int(b != full), 512 * i:512 * i + 512], unit_ap(u)), u)
                for i in range(2):
                    u = ("gr", full, i)
                    is_emptied(v.tensor_copy(gr[:, 512 * i:512 * i + 512], unit_ap(u)), u)
                for b in blocks:
                    slot = int(b != full)
                    u = ("g1", b)
                    is_emptied(v.tensor_copy(g1[:, 0:RANK], unit_ap(u, 0, RANK)), u)
                    u = ("g1T", b)
                    wait_filled(dve, u)
                    is_emptied(v.tensor_copy(g1T[0:RANK, :], bank[0:RANK, unit_bank(u) * 512:unit_bank(u) * 512 + P]), u)
                    u = ("la", b)
                    src = unit_ap(u)
                    steps.did(v.tensor_scalar(la, src, 0.0, 1.0 / TAU, ALU.min, ALU.mult))
                    is_emptied(v.tensor_scalar(ex, src, 0.0, None, ALU.max), u)
                    steps.settle()
                    wait_emptied(dve, u)
                    v.scalar_tensor_tensor(out=ex, in0=la, scalar=TAU, in1=ex, op0=ALU.mult, op1=ALU.subtract).then_inc(minus_abs, 1)
                    dve.wait_ge(gate_log, b + 1)
                    v.scalar_tensor_tensor(out=la, in0=ex, scalar=-1.0 / TAU, in1=la, op0=ALU.mult, op1=ALU.add).then_inc(decay_ready, 1)
                    if b == full:
                        wait_emptied(dve, ("cum", b))
                        v.tensor_tensor(gq, gq, qdT, ALU.mult).then_inc(qd_ready, 1)
                        v.tensor_tensor(ex, gk[:, slot, :], kdT, ALU.mult).then_inc(kd_ready, 1)
                        dve.wait_ge(kd_ready, b)
                    wait_emptied(dve, ("after", b))
                    v.tensor_tensor(gk[:, slot, :], gk[:, slot, :], la, ALU.mult).then_inc(kend_ready, 1)
                    wait_emptied(dve, ("decay", b))
                    if b == full:
                        u = ("att", b)
                        is_emptied(v.tensor_tensor(atm.rearrange("p (h n) -> p h n", h=GH), unit_ap(u).rearrange("p (h n) -> p h n", h=GH),
                                                   const("tri").unsqueeze(1).broadcast_to([P, GH, P]), ALU.mult), u)
                    for x in range(GH):
                        for c in range(2):
                            u = ("st", b, c, x)
                            src = unit_ap(u, 0, GV)
                            if c == 0:
                                if (b, x) != (0, 0):
                                    wait_emptied(dve, ("st", b, 1, x - 1) if x else ("st", b - 1, 1, GH - 1))
                            else:
                                wait_emptied(dve, ("st", b, 0, x))
                                if b == full:
                                    uo = ("o", b, x)
                                    is_emptied(v.tensor_copy(og[:, x * GV:x * GV + GV], unit_ap(uo, 0, GV)), uo)
                            is_emptied(v.scalar_tensor_tensor(out=state[:, x, :], in0=state[:, x, :], scalar=dec[:, 2 * x + c:2 * x + c + 1],
                                                              in1=src, op0=ALU.mult, op1=ALU.add), u)
                wait_emptied(dve, ("st", full, 1, GH - 1))
                steps.chain(v.tensor_scalar(sq, gr, -1.0, 80.0, ALU.mult, ALU.min))
                dve.sem_inc(silu_in, 1)
                dve.wait_ge(silu_exp, full)
                steps.chain(v.tensor_scalar(sq, sq, 1.0, None, ALU.add))
                steps.chain(v.reciprocal(sq, sq))
                steps.chain(v.tensor_tensor(gr, gr, sq, ALU.mult))
                for x in range(GH):
                    c = slice(x * GV, x * GV + GV)
                    squares(og[:, c], sq[:, c], gms[:, x:x + 1])
                steps.settle()
                mean(gms[:, 0:4], GV)
                roots()
                for x in range(GH):
                    c = slice(x * GV, x * GV + GV)
                    steps.did(v.scalar_tensor_tensor(out=og[:, c], in0=og[:, c], scalar=gms[:, 4 + x:5 + x], in1=onorm[:, :],
                                                     op0=ALU.mult, op1=ALU.mult))
                steps.settle()
                v.tensor_tensor(og, og, gr, ALU.mult).then_inc(og_ready, 1)
                for i in range(2):
                    add_to_h(("go", full, i), full, i)
                for i in range(2):
                    wait_emptied(dve, ("go", full, i))
                norm(3 if full == 1 else 5, [full])
                t0 = (full * P - PAD) * PH
                for x in range(PH):
                    u = ("pq1", full, x)
                    is_emptied(v.tensor_copy(qT[:, t0:t0 + P * PH].rearrange("p (t h) -> p t h", h=PH)[:, :, x], unit_ap(u, 0, P)), u)

            gla((0, 1))
            gla((2,))
            choose(17, 1)
            segment(3, True)
            segment(4, False)
            norm(6, [1])
            norm(6, [2])


SMALL_LOADS = 10
_INS = ["x", "meta_tokens", "attn_norm", "attn_w_in", "mla_q_norm", "mla_w_uq", "mla_kv_norm", "mla_w_ukv", "swa_sinks",
        "attn_w_out", "gla_norm", "gla_w_in", "gla_w_gate", "gla_b_gate", "gla_out_norm", "gla_w_out", "ffn_norm",
        "peer_w_query", "peer_sub_keys", "peer_u", "peer_v", "final_norm"]


def kernel(**inputs):
    import concourse.bacc as bacc
    from concourse.bass_utils import run_bass_kernel_spmd

    nc = bacc.Bacc("TRN2", target_bir_lowering=False, num_devices=1)
    arrays = {n: np.ascontiguousarray(inputs[n]) for n in _INS}
    arrays["final_norm"] = arrays["final_norm"].reshape(1, D)
    arrays["consts"] = constants()
    io = {n: nc.dram_tensor(n, a.shape, mybir.dt.from_np(a.dtype), kind="ExternalInput").ap() for n, a in arrays.items()}
    io["out"] = nc.dram_tensor("out", (1, SEQ, D), F32, kind="ExternalOutput").ap()
    build(nc, io, UPTO)
    r = run_bass_kernel_spmd(nc, [arrays], core_ids=[0])
    return r.results[0]["out"]


UPTO = "all"
```

```python
import numpy as np
import concourse.bass as bass
from concourse import mybir
from contextlib import ExitStack

F32 = mybir.dt.float32
U32 = mybir.dt.uint32
ALU = mybir.AluOpType
ACT = mybir.ActivationFunctionType
AX = mybir.AxisListType.X

P = 128
D = 1024
KC = D // P
N_META, SEQ = 16, 256
NB = 3
ROWS = NB * P
PAD = ROWS - N_META - SEQ
LIVE = ROWS - PAD
EPS = 1e-6
NEG = -1e30

HEADS = 16
HALF = HEADS // 2
HD = 64
QD = 96
ROPE = 16
Q_LORA, KV_LORA = 384, 256
WINDOW = 128

GH, GK, GV = 4, 128, 256
GKD, GVD, RANK = GH * GK, GH * GV, 16
TAU = 16.0
CHUNK = 64

TOPK, N_KEYS, PH = 16, 128, 8
EXPERTS = N_KEYS * N_KEYS
TT = P // PH
RING = 8
GELU_C = 0.7978845608028654
FIRST_TILE = PAD // TT
WSLOTS = 2

CONST_PARTS = [("ident", P), ("row_token", P), ("token", 8), ("place", 112 + P), ("iota", 16), ("tri", P), ("after", P),
               ("chunks", 2), ("neghalf", 8), ("cos", NB * ROPE), ("sin", NB * ROPE), ("mask_swa", 768), ("mask_mla", 768)]
CONST_AT = {}
_at = 0
for _n, _w in CONST_PARTS:
    CONST_AT[_n] = (_at, _w)
    _at += _w
CONST_COLS = _at
LIVE_CONSTS = CONST_AT["cos"][0]

SCORE_AT = {2: (0, 384), 0: (384, 128), 1: (512, 256)}


def constants():
    c = np.zeros((P, CONST_COLS), np.float32)

    def put(name, a):
        at, w = CONST_AT[name]
        c[:, at:at + w] = a.reshape(P, w)

    i = np.arange(P)
    put("ident", np.eye(P, dtype=np.float32))
    put("row_token", np.broadcast_to((i // PH).astype(np.float32), (P, P)))
    put("token", (i[:, None] - TT * np.arange(8)[None]).astype(np.float32))
    put("place", (np.arange(112 + P)[None] == 112 + i[:, None] // PH).astype(np.float32))
    put("iota", np.broadcast_to(np.arange(16, dtype=np.float32), (P, 16)))
    same = i[:, None] // CHUNK == i[None] // CHUNK
    put("tri", (same & (i[:, None] <= i[None])).astype(np.float32))
    put("after", (same & (i[:, None] > i[None])).astype(np.float32))
    put("chunks", (i[:, None] // CHUNK == np.arange(2)[None]).astype(np.float32))
    put("neghalf", np.full((P, 8), -0.5, np.float32))
    inv = np.float32(10000.0) ** (-np.arange(0, 2 * ROPE, 2, dtype=np.float32) / np.float32(2 * ROPE))
    pos = (np.arange(ROWS) - PAD).astype(np.float32).reshape(NB, P).T
    ang = (pos[:, :, None] * inv[None, None]).astype(np.float32)
    put("cos", np.cos(ang))
    put("sin", np.sin(ang))
    for name, window in (("mask_swa", WINDOW), ("mask_mla", ROWS)):
        m = np.zeros((P, 768), np.float32)
        for b, (at, w) in SCORE_AT.items():
            q, k = (b * P + i)[:, None], np.arange(w)[None]
            m[:, at:at + w] = np.where((k <= q) & (q - k < window) & (k >= PAD), 0.0, NEG)
        put(name, m)
    return c


class Steps:

    def __init__(self, eng, sem):
        self.eng, self.sem, self.n = eng, sem, 0

    def did(self, ins):
        ins.then_inc(self.sem, 1)
        self.n += 1

    def settle(self):
        self.eng.wait_ge(self.sem, self.n)

    def chain(self, ins):
        self.did(ins)
        self.settle()

    def restart(self):
        self.eng.sem_clear(self.sem)
        self.n = 0


def gla_units(full, blocks):
    rest = blocks[:-1]
    every = [full] + rest
    return (
        [("tr_gla", b, i) for b in every for i in range(2)] + [("g1", b) for b in every] + [("gk", full)]
        + [("g1T", b) for b in every] + [("gk", b) for b in rest] + [("la", b) for b in every]
        + [("after", b) for b in every] + [("cum", full), ("decay", full), ("gq", full), ("gv", full, 0)]
        + [("gv", full, 1), ("tr_qd", full), ("tr_kd", full), ("att", full)] + [("gv", b, 0) for b in rest]
        + [("gv", b, 1) for b in rest] + [("gr", full, 0)] + [("st", b, i) for b in rest for i in range(2)]
        + [("u0", full, i) for i in range(2)]
        + [("gr", full, 1)] + [("o", full, i) for i in range(2)] + [("u1", full, i) for i in range(2)]
        + [("tr_go", full, i) for i in range(2)] + [("go", full, i) for i in range(2)]
        + [("tr_ffn1", full, i) for i in range(2)] + [("pq1", full, x) for x in range(PH)])


def gla_weights(full, rest):
    last = rest[-1] if rest else full
    return [(("gk", full), ("gk", last)), (("gq", full), ("gq", full)), (("gv0", full), ("gv", last, 0)),
            (("gv1", full), ("gv", last, 1)), (("gr0", full), ("gr", full, 0)), (("gr1", full), ("gr", full, 1)),
            (("gla_out0", full), ("go", full, 0)), (("gla_out1", full), ("go", full, 1)),
            (("wq1_0", full), ("pq1", full, 3)), (("wq1_1", full), ("pq1", full, 7))]


UNITS = (
    [("tr_attn", b, i) for b in range(NB) for i in range(2)] + [(n, b) for n in ("mid", "low", "qa") for b in range(NB)]
    + [(n, b, i) for n in ("tr_low", "uq", "ukv", "tr_o") for b in range(NB) for i in range(2)]
    + [("ao", b, i) for i in range(2) for b in range(NB)] + [("tr_ffn0", b, i) for b in range(NB) for i in range(2)]
    + [("sk", 0), ("sk", 1)] + [("pq0", x) for x in range(PH)]
    + gla_units(1, [0, 1]) + gla_units(2, [2]))
UNIT_AT = {u: n for n, u in enumerate(UNITS)}
assert len(UNIT_AT) == len(UNITS)
WEIGHTS = [("in_mid", ("mid", 2)), ("in_low", ("low", 2)), ("in_qa", ("qa", 2)), ("uq", ("uq", 2, 1)), ("ukv", ("ukv", 2, 1)),
           ("attn_out0", ("ao", 2, 0)), ("attn_out1", ("ao", 2, 1)), ("wq0_0", ("pq0", 3)), ("wq0_1", ("pq0", 7))]
WEIGHTS += gla_weights(1, [0]) + gla_weights(2, [])
GROUP_AT = {g: n for n, (g, _) in enumerate(WEIGHTS)}
UNIT_BANKS = (5, 6, 7)



def build(nc, io, upto="all"):
    ctx = ExitStack()
    with ctx:
        def sb(name, shape, dt=F32):
            return ctx.enter_context(nc.sbuf_tensor(name, shape, dt))

        def sem(name):
            return ctx.enter_context(nc.semaphore(name))

        h = sb("h", [P, NB, D])
        hn = sb("hn", [P, NB, D])
        hT = sb("hT", [P, KC, ROWS])
        gain = sb("gain", [P, D])
        qT = sb("qT", [P, LIVE * PH])
        skT = sb("skT", [P, 2, 2 * N_KEYS])
        con = sb("con", [P, LIVE_CONSTS])
        wring = sb("wring", [P, WSLOTS, KC * 512])
        arena = sb("arena", [P, 2 * RING * D + TOPK * P])
        gws = sb("gws", [P, 10128])
        small = sb("small", [P, 64])
        g1w = sb("g1w", [P, KC, RANK])
        wgate = sb("wgate", [32, GKD])
        onorm = sb("onorm", [P, GV])

        def part(t, at, *shape):
            n = int(np.prod(shape))
            ap = t[:, at:at + n]
            if len(shape) == 1:
                return ap
            names = "abcd"[:len(shape)]
            return ap.rearrange(f"p ({' '.join(names)}) -> p {' '.join(names)}", **dict(zip(names, shape)))

        def const(name):
            at, w = CONST_AT[name]
            return con[:, at:at + w]

        ident = const("ident")
        bank = ctx.enter_context(nc.psum_tensor("bank", [P, 8 * 512], F32))

        def bk(n, a=0, b=512):
            return bank[:, n * 512 + a:n * 512 + b]

        at = 0

        def take(*shape):
            nonlocal at
            ap = part(arena, at, *shape)
            at += int(np.prod(shape))
            return ap

        v_all = take(NB, HEADS, HD)
        low = take(NB, Q_LORA + KV_LORA + 2 * ROPE)
        acon = take(CONST_COLS - LIVE_CONSTS)
        rotate_at = at
        q_stage = take(2, NB, QD)
        k_stage = take(2, NB, QD)
        qT_head = take(2, ROWS)
        kT_head = take(2, ROWS)
        prob = take(2, 768)
        probT = take(768)
        sink = take(HEADS)
        low_gain = take(Q_LORA + KV_LORA)
        stat = take(2, 16)
        rt = part(arena, rotate_at, 4 * NB * HALF * ROPE)
        assert at <= 2 * RING * D + TOPK * P, at
        q_all = part(gws, 0, NB, HEADS, QD)
        k_all = part(gws, NB * HEADS * QD, NB, HEADS, QD)
        q_swa, q_mla = q_all[:, :, 0:HALF, 0:HD], q_all[:, :, HALF:HEADS, :]
        k_mla = k_all[:, :, HALF:HEADS, :]

        masks = acon[:, 2 * NB * ROPE:]

        def acst(name):
            a, w = CONST_AT[name]
            return acon[:, a - LIVE_CONSTS:a - LIVE_CONSTS + w]

        urow = part(arena, 0, RING, D)
        vrow = part(arena, RING * D, RING, D)
        wplace = part(arena, 2 * RING * D, TOPK, P)
        pick_now = sb("pick_now", [P, P])
        q_now = sb("q_now", [P, P])
        top = sb("top", [P, 2, TOPK])
        top_i = sb("top_i", [P, 2, TOPK], U32)
        top_f = sb("top_f", [P, 2, TOPK])
        pairs = sb("pairs", [P, 2 * TOPK * TOPK])
        cand = pairs[:, 0:256]
        cand_rest = pairs[:, 256:512]
        onehot = part(pairs, 0, 2 * TOPK, TOPK)
        rest = part(pairs, 256, 2, N_KEYS)
        best = sb("best", [P, TOPK])
        best_j = sb("best_j", [P, TOPK], U32)
        digit = sb("digit", [P, 2, TOPK], U32)
        digit_f = sb("digit_f", [P, 2, TOPK])
        picked = sb("picked", [P, 2, TOPK])
        idx_next = sb("idx_next", [P, TOPK], U32)
        idx_now = sb("idx_now", [P, 2, TOPK], U32)
        dots = sb("dots", [P, TOPK])
        gl = sb("gl", [P, 2, TOPK])
        gate = sb("gate", [P, TOPK])
        gate_e = sb("gate_e", [P, TOPK])
        z = sb("z", [P, 4])
        wgt = sb("wgt", [P, TOPK])
        xrep = bank[:, 0:1024]
        score = bk(2, 0, 256)
        yacc = bank[:, 1536:2560]

        gat = 0

        def gtake(*shape):
            nonlocal gat
            ap = part(gws, gat, *shape)
            gat += int(np.prod(shape))
            return ap

        gq = gtake(GKD)
        gk = gtake(2, GKD)
        gv = gtake(2, GVD)
        gr = gtake(GVD)
        la = gtake(2, GKD)
        ex = gtake(2, GKD)
        qdT = gtake(GKD)
        kdT = gtake(GKD)
        state0 = gtake(GH, GV)
        state1 = gtake(GH, GV)
        g1T = gtake(2, P)
        g1 = gtake(2, RANK)
        dec = gtake(2 * GH)
        gms = gtake(8)
        assert gat <= 10128, gat
        kd = la[:, 0, :]
        atm = la[:, 1, :]
        og = ex.rearrange("p s n -> p (s n)")
        sq = la.rearrange("p s n -> p (s n)")

        x_in = sem("x_in")
        con_in = sem("con_in")
        small_in = sem("small_in")
        gain_in = sem("gain_in")
        w_in = [sem(f"w_in{i}") for i in range(WSLOTS)]
        filled = [sem(f"filled{i}") for i in UNIT_BANKS]
        emptied = [sem(f"emptied{i}") for i in UNIT_BANKS]
        d_step = sem("d_step")
        a_step = sem("a_step")
        norm_ms = sem("norm_ms")
        norm_rs = sem("norm_rs")
        hn_ready = sem("hn_ready")
        low_ready = sem("low_ready")
        heads_ready = sem("heads_ready")
        staged = sem("staged")
        transposed = sem("transposed")
        qT_ready = sem("qT_ready")
        kT_ready = sem("kT_ready")
        scored = sem("scored")
        masked = sem("masked")
        nm_ready = sem("nm_ready")
        probs_ready = sem("probs_ready")
        p_transposed = sem("p_transposed")
        pt_low = sem("pt_low")
        pt_high = sem("pt_high")
        pv_done = sem("pv_done")
        o_taken = sem("o_taken")
        minus_abs = sem("minus_abs")
        gate_exp1 = sem("gate_exp1")
        state1_ready = sem("state1_ready")
        gate_log = sem("gate_log")
        decay_ready = sem("decay_ready")
        kd_ready = sem("kd_ready")
        kend_ready = sem("kend_ready")
        silu_tanh = sem("silu_tanh")
        og_ready = sem("og_ready")
        den_ready = sem("den_ready")
        u_in = [sem(f"u_in{i}") for i in range(RING)]
        v_in = [sem(f"v_in{i}") for i in range(RING)]
        u_used = sem("u_used")
        v_used = sem("v_used")
        idx_ready = sem("idx_ready")
        idx_taken = sem("idx_taken")
        go = {e: sem(f"go_{e}") for e in ("pool", "act", "dve", "pe")}
        pad_zero = sem("pad_zero")
        sk_zero = sem("sk_zero")
        pick_ready = sem("pick_ready")
        qnow_ready = sem("qnow_ready")
        xrep_ready = sem("xrep_ready")
        scores_ready = sem("scores_ready")
        topk_step = sem("topk_step")
        mix_step = sem("mix_step")
        best_ready = sem("best_ready")
        gate_exp = sem("gate_exp")
        gelu_in = sem("gelu_in")
        gelu_tanh = sem("gelu_tanh")
        wgt_ready = sem("wgt_ready")
        placed = sem("placed")
        y_added = sem("y_added")
        out_done = sem("out_done")

        def at_least(eng, semaphore, n):
            if not (isinstance(n, int) and n <= 0):
                eng.wait_ge(semaphore, n)

        def pipeline(eng, head_step):
            head_step(-2, 0, 0, (2,))
            head_step(-1, 1, 0, (1, 2))
            head_step(0, 0, 0, (0, 1, 2))
            for latent in range(2):
                with eng.Fori(3 * latent, 3 * latent + 3) as j:
                    head_step(2 * j + 1, 1, latent)
                    head_step(2 * j + 2, 0, latent)
            head_step(HEADS - 3, 1, 1)
            head_step(HEADS - 2, 0, 1, (-1, 0, 1))
            head_step(HEADS - 1, 1, 1, (-1, 0))
            head_step(HEADS, 0, 1, (-1,))

        def unit_bank(u):
            return UNIT_BANKS[UNIT_AT[u] % 3]

        def wait_filled(eng, u):
            n = UNIT_AT[u]
            eng.wait_ge(filled[n % 3], n // 3 + 1)

        def wait_emptied(eng, u):
            n = UNIT_AT[u]
            eng.wait_ge(emptied[n % 3], n // 3 + 1)

        def is_emptied(ins, u):
            ins.then_inc(emptied[UNIT_AT[u] % 3], 1)

        PASSES = {1: [0, 1], 2: [2]}

        def place_of(b, full):
            return int(b != full)

        def nth_gate(b):
            return (2, 1, 3)[b]

        block = ctx.enter_context(nc.Block())

        gains = [io["attn_norm"], io["ffn_norm"][0:1, :], io["gla_norm"], io["ffn_norm"][1:2, :], io["gla_norm"],
                 io["ffn_norm"][1:2, :], io["final_norm"]]
        NORMS = [(0, b) for b in range(3)] + [(1, b) for b in range(3)] + [(2, 0), (2, 1), (3, 1), (4, 2), (5, 2), (6, 1), (6, 2)]

        def wait_normed(eng, n, b):
            eng.wait_ge(hn_ready, NORMS.index((n, b)) + 1)

        @block.sync
        def _(sp):
            sp.dma_start(h[PAD:P, 0, :], io["meta_tokens"]).then_inc(x_in, 16)
            sp.dma_start(h[:, 1:3, :], io["x"].rearrange("a (b p) d -> p (a b) d", p=P)).then_inc(x_in, 16)

            def load_gain(n):
                sp.dma_start(gain[:, :], gains[n].broadcast_to([P, D])).then_inc(gain_in, 16)

            load_gain(0)
            sp.dma_start(con[:, :], io["consts"][:, 0:LIVE_CONSTS]).then_inc(con_in, 16)
            sources = {
                "in_qa": (io["attn_w_in"][0, :, 0:512], KC), "in_mid": (io["attn_w_in"][0, :, 512:1024], KC),
                "in_low": (io["attn_w_in"][0, :, 1024:1440], KC),
                "uq": (io["mla_w_uq"][0], Q_LORA // P), "ukv": (io["mla_w_ukv"][0], KV_LORA // P),
            }
            for i in range(2):
                c = slice(512 * i, 512 * i + 512)
                sources[f"attn_out{i}"] = (io["attn_w_out"][0, :, c], KC)
                sources[f"wq0_{i}"] = (io["peer_w_query"][0, :, c], KC)
                for full in PASSES:
                    sources[f"gla_out{i}", full] = (io["gla_w_out"][0, :, c], KC)
                    sources[f"wq1_{i}", full] = (io["peer_w_query"][1, :, c], KC)
                    sources[f"gv{i}", full] = (io["gla_w_in"][0, :, 1024 + 512 * i:1536 + 512 * i], KC)
                    sources[f"gr{i}", full] = (io["gla_w_in"][0, :, 2048 + 512 * i:2560 + 512 * i], KC)
                    sources[("gq", "gk")[i], full] = (io["gla_w_in"][0, :, c], KC)

            def load_group(n):
                if n >= WSLOTS:
                    wait_filled(sp, WEIGHTS[n - WSLOTS][1])
                src, kc = sources[WEIGHTS[n][0]]
                w = src.shape[1]
                sp.dma_start(part(wring[:, n % WSLOTS, :], 0, kc, w),
                             src.rearrange("(k p) n -> p k n", p=P)).then_inc(w_in[n % WSLOTS], 16)

            load_group(0)
            sp.dma_start(acon, io["consts"][:, LIVE_CONSTS:CONST_COLS]).then_inc(small_in, 16)
            sp.dma_start(low_gain[:, 0:Q_LORA], io["mla_q_norm"].broadcast_to([P, Q_LORA])).then_inc(small_in, 16)
            sp.dma_start(low_gain[:, Q_LORA:], io["mla_kv_norm"].broadcast_to([P, KV_LORA])).then_inc(small_in, 16)
            sp.dma_start(sink[:, 0:HALF], io["swa_sinks"].broadcast_to([P, HALF])).then_inc(small_in, 16)
            for layer in range(2):
                sp.dma_start(cand[:, P * layer:P * layer + P].rearrange("n (s d) -> n s d", s=2),
                             io["peer_sub_keys"][layer].rearrange("s n d -> n s d")).then_inc(small_in, 16)
            load_group(1)
            sp.dma_start(g1w[:, :, :], io["gla_w_in"][0, :, 3072:3088].rearrange("(k p) n -> p k n", p=P)).then_inc(small_in, 16)
            sp.dma_start(wgate[0:RANK, :], io["gla_w_gate"][0]).then_inc(small_in, 16)
            sp.dma_start(wgate[RANK:RANK + 1, :], io["gla_b_gate"]).then_inc(small_in, 16)
            sp.dma_start(onorm[:, :], io["gla_out_norm"].broadcast_to([P, GV])).then_inc(small_in, 16)
            wait_normed(sp, 0, 2)
            load_gain(1)
            before = {("gk", 1): (1, 2), ("gv1", 1): (2, 1), ("gk", 2): (3, 1), ("gv1", 2): (4, 2)}
            for n in range(2, len(WEIGHTS)):
                name = WEIGHTS[n][0]
                if name in before:
                    done = before[name]
                    wait_normed(sp, *done)
                    load_gain(done[0] + 1)
                load_group(n)
                if upto != "all" and name == "wq0_1":
                    return
            wait_normed(sp, 5, 2)
            load_gain(6)
            for i in range(2):
                wait_normed(sp, 6, i + 1)
                sp.dma_start(io["out"][0, P * i:P * i + P, :], hn[:, i + 1, :]).then_inc(out_done, 16)
            sp.wait_ge(out_done, 32)

        @block.gpsimd
        def _(pool):
            n_root = [0]

            def root(ap_in, ap_out, w):
                n_root[0] += 1
                pool.wait_ge(norm_ms, n_root[0])
                nc.gpsimd.tensor_tensor(ap_out, ap_in, const("neghalf")[:, 0:w], ALU.pow).then_inc(norm_rs, 1)

            pool.wait_ge(con_in, 16)
            root(small[:, 0:3], small[:, 3:6], 3)
            root(small[:, 6:12], small[:, 12:18], 6)

            def stage(hh, par):
                pool.wait_ge(transposed, hh + 1)
                pool.sem_inc(go["pool"], 1)
                nc.gpsimd.tensor_copy(q_stage[:, par], q_all[:, :, hh, :]).then_inc(staged, 1)
                nc.gpsimd.tensor_copy(k_stage[:, par], k_all[:, :, hh, :]).then_inc(staged, 1)

            pool.wait_ge(heads_ready, 1)
            with pool.Fori(0, HEADS // 2) as j:
                for par in range(2):
                    stage(2 * j + par, par)
            root(small[:, 0:3], small[:, 3:6], 3)

            def gathers(g, par, layer, side=None):
                pool.wait_ge(idx_ready, g + 1)
                pool.sem_inc(go["pool"], 1)
                nc.gpsimd.tensor_copy(idx_now[:, par, :], idx_next[:, :]).then_inc(idx_taken, 1)
                pool.wait_ge(idx_taken, g + 1)
                pool.sem_inc(go["pool"], 1)
                for table, rows, used, landed in ((io["peer_u"], urow, u_used, u_in), (io["peer_v"], vrow, v_used, v_in)):
                    for k in range(TOPK):
                        pool.wait_ge(used, TOPK * g + k + 1)
                        pool.sem_inc(go["pool"], 1)
                        nc.gpsimd.indirect_dma_start(
                            out=rows[:, k % RING, :], out_offset=None, in_=table.rearrange("l e d -> (l e) d"),
                            in_offset=bass.IndirectOffsetOnAxis(ap=idx_now[:, par, k:k + 1], axis=0)).then_inc(landed[k % RING], 16)
                        if rows is vrow and k == 11 and side:
                            side()

            def gathers_pairs(g0, n, layer):
                with pool.Fori(0, n) as j:
                    for i in range(2):
                        gathers(g0 + 2 * j + i, (g0 + i) % 2, layer)

            if upto == "attn":
                return
            gathers(0, 0, 0)
            gathers_pairs(1, 4, 0)
            for full in (1, 2):
                b = PASSES[full][0]
                sides = {0: lambda: root(small[:, b:full + 1], small[:, 3 + b:4 + full], full + 1 - b),
                         5: lambda: root(gms[:, 0:4], gms[:, 4:8], 4),
                         6: lambda: root(small[:, full:full + 1], small[:, 3 + full:4 + full], 1)}
                for t in range(8):
                    gathers(8 * full + 1 + t, (t + 1) % 2, full - 1, sides.get(t))
            gathers(25, 1, 1, lambda: root(small[:, 1:2], small[:, 4:5], 1))
            gathers_pairs(26, 3, 1)
            gathers(32, 0, 1)
            root(small[:, 2:3], small[:, 5:6], 1)

        @block.tensor
        def _(pe):
            pe.sem_inc(transposed, 2)
            pe.sem_inc(p_transposed, 2)
            pe.sem_inc(v_used, RING)

            def begin(u):
                n = UNIT_AT[u]
                if n >= 3:
                    pe.wait_ge(emptied[n % 3], n // 3)
                return UNIT_BANKS[n % 3]

            def end(ins, u):
                ins.then_inc(filled[UNIT_AT[u] % 3], 1)

            def transposes(u, sources, width=P, parts=P):
                b = begin(u)
                for i, src in enumerate(sources):
                    last = nc.tensor.transpose(bank[0:width, b * 512 + i * P:b * 512 + i * P + parts], src, ident)
                end(last, u)

            def weights(name):
                n = GROUP_AT[name]
                pe.wait_ge(w_in[n % WSLOTS], 16 * (n // WSLOTS + 1))
                return wring[:, n % WSLOTS, :]

            def project(u, w, lhs, n_k, width):
                b = begin(u)
                for k in range(n_k):
                    last = nc.tensor.matmul(bk(b, 0, width), lhs(k), w(k), start=(k == 0), stop=(k == n_k - 1))
                end(last, u)

            def rows_T(b):
                return lambda k: hT[:, k, b * P:b * P + P]

            def tr_stream(name, n, b, src=None):
                src = src or (lambda c: hn[:, b, c * P:c * P + P])
                if n is not None:
                    wait_normed(pe, n, b)
                for half in range(2):
                    transposes((name, b, half), [src(4 * half + i) for i in range(4)])

            def group_cols(w, width):
                v = part(w, 0, KC, width)
                return lambda k: v[:, k, :]

            pe.wait_ge(con_in, 16)
            for b in range(NB):
                tr_stream("tr_attn", 0, b)
            for name, u, width in (("in_mid", "mid", 512), ("in_low", "low", 416), ("in_qa", "qa", 512)):
                w = weights(name)
                for b in range(NB):
                    if name == "in_mid":
                        for half in range(2):
                            wait_emptied(pe, ("tr_attn", b, half))
                    project((u, b), group_cols(w, width), rows_T(b), KC, width)
            pe.wait_ge(low_ready, 1)
            for b in range(NB):
                for half, cs in enumerate((range(0, 4), range(4, 5))):
                    transposes(("tr_low", b, half), [low[:, b, c * P:c * P + P] for c in cs])
            w = part(weights("uq"), 0, Q_LORA // P, HALF * QD)
            for b in range(NB):
                for half in range(2):
                    wait_emptied(pe, ("tr_low", b, half))
                for half in range(2):
                    project(("uq", b, half), lambda k: w[:, k, 384 * half:384 * half + 384], rows_T(b), 3, 384)
            w = part(weights("ukv"), 0, KV_LORA // P, D)
            for b in range(NB):
                for half in range(2):
                    project(("ukv", b, half), lambda k: w[:, k, 512 * half:512 * half + 512],
                            lambda k: hT[:, 3 + k, b * P:b * P + P], 2, 512)

            def transpose_qk(hh, par):
                pe.wait_ge(staged, 2 * hh + 2)
                at_least(pe, qT_ready, hh)
                at_least(pe, kT_ready, hh)
                pe.sem_inc(go["pe"], 1)
                for i, st in enumerate((q_stage, k_stage)):
                    for b in range(NB):
                        last = nc.tensor.transpose(bank[0:QD, i * 512 + b * P:i * 512 + b * P + P], st[:, par, b, :], ident)
                last.then_inc(transposed, 1)

            def head_scores(hh, par):
                pe.wait_ge(qT_ready, hh + 1)
                pe.wait_ge(kT_ready, hh + 1)
                at_least(pe, masked, NB * hh)
                pe.sem_inc(go["pe"], 1)
                for b in (2, 0, 1):
                    a, w = SCORE_AT[b]
                    last = nc.tensor.matmul(bank[:, 1024 + a:1024 + a + w], qT_head[0:QD, par, b * P:b * P + P],
                                            kT_head[0:QD, par, 0:w], start=True, stop=True)
                last.then_inc(scored, 1)

            def transpose_probs(hh, par):
                pe.wait_ge(probs_ready, hh + 1)
                pe.wait_ge(pt_low, hh + 1)
                pe.wait_ge(pt_high, hh + 1)
                pe.sem_inc(go["pe"], 1)
                for c in range(6):
                    last = nc.tensor.transpose(bank[:, 2048 + c * P:2048 + c * P + P], prob[:, par, c * P:c * P + P], ident)
                last.then_inc(p_transposed, 1)

            def head_values(hh):
                pe.wait_ge(pt_low, hh + 2)
                pe.wait_ge(pt_high, hh + 2)
                pe.wait_ge(o_taken, hh + 1)
                pe.sem_inc(go["pe"], 1)
                for b in range(NB):
                    a = SCORE_AT[b][0]
                    for kb in range(b + 1):
                        last = nc.tensor.matmul(bk(6, b * HD, b * HD + HD), probT[:, a + kb * P:a + kb * P + P],
                                                v_all[:, kb, hh, :], start=(kb == 0), stop=(kb == b))
                last.then_inc(pv_done, 1)

            def head_step(i, par, latent, live=range(-1, 3)):
                if 2 in live:
                    transpose_qk(i + 2, par)
                if 1 in live:
                    head_scores(i + 1, 1 - par)
                if -1 in live:
                    head_values(i - 1)
                if 0 in live:
                    transpose_probs(i, par)

            pe.wait_ge(heads_ready, 1)
            pipeline(pe, head_step)

            pe.wait_ge(o_taken, HEADS + 1)
            for b in range(NB):
                tr_stream("tr_o", None, b)
            for i in range(2):
                w = weights(f"attn_out{i}")
                for b in range(NB):
                    if i == 0:
                        for half in range(2):
                            wait_emptied(pe, ("tr_o", b, half))
                    project(("ao", b, i), group_cols(w, 512), rows_T(b), KC, 512)
            for b in range(NB):
                tr_stream("tr_ffn0", 1, b)
            for layer in range(2):
                transposes(("sk", layer), [cand[:, layer * P:layer * P + P]])
            for b in range(NB):
                for half in range(2):
                    wait_emptied(pe, ("tr_ffn0", b, half))
            for i in range(2):
                w = part(weights(f"wq0_{i}"), 0, KC, 512)
                for x in range(4):
                    b = begin(("pq0", 4 * i + x))
                    for k in range(KC):
                        last = nc.tensor.matmul(bk(b, 0, LIVE), w[:, k, x * P:x * P + P], hT[:, k, PAD:ROWS],
                                                start=(k == 0), stop=(k == KC - 1))
                    end(last, ("pq0", 4 * i + x))
            if upto == "attn":
                return

            def prepare(g, layer, b):
                pe.wait_ge(pick_ready, g + 1)
                pe.wait_ge(u_used, RING + TOPK * g)
                pe.sem_inc(go["pe"], 1)
                for i in range(2):
                    last = nc.tensor.matmul(bk(i), pick_now[:, :], hn[:, b, 512 * i:512 * i + 512], start=True, stop=True)
                last.then_inc(xrep_ready, 1)
                pe.wait_ge(qnow_ready, g + 1)
                pe.sem_inc(go["pe"], 1)
                nc.tensor.matmul(score, q_now[:, :], skT[:, layer, :], start=True, stop=True).then_inc(scores_ready, 1)

            def mix(g):
                for k in range(TOPK):
                    pe.wait_ge(v_in[k % RING], 16 * (2 * g + k // RING + 1))
                    pe.wait_ge(placed, TOPK * g + k + 1)
                    if k == 0:
                        at_least(pe, y_added, g)
                    pe.sem_inc(go["pe"], 1)
                    for i in range(2):
                        last = nc.tensor.matmul(yacc[:, 512 * i:512 * i + 512], wplace[:, k, :],
                                                vrow[:, k % RING, 512 * i:512 * i + 512], start=(k == 0), stop=(k == TOPK - 1))
                    last.then_inc(v_used, 1)

            def gla(t, full):
                rest = PASSES[full][:-1]
                every = [full] + rest

                def gproject(u, name, b):
                    project(u, group_cols(weights((name, full)), 512), rows_T(b), KC, 512)

                def states(u, i, place, c):
                    rs = slice(c * CHUNK, c * CHUNK + CHUNK)
                    ub = begin(u)
                    for x in (2 * i, 2 * i + 1):
                        last = nc.tensor.matmul(bk(ub, (x % 2) * GV, (x % 2) * GV + GV), gk[rs, place, x * GK:x * GK + GK],
                                                gv[rs, place, x * GV:x * GV + GV], start=True, stop=True)
                    end(last, u)

                if t == 0:
                    for b in every:
                        tr_stream("tr_gla", 2 if full == 1 else 4, b)
                    for b in every:
                        for i in range(2):
                            wait_emptied(pe, ("tr_gla", b, i))
                        project(("g1", b), lambda k: g1w[:, k, :], rows_T(b), KC, RANK)
                    gproject(("gk", full), "gk", full)
                    for b in every:
                        wait_emptied(pe, ("g1", b))
                        transposes(("g1T", b), [g1[:, place_of(b, full), :]], width=RANK)
                    for b in rest:
                        gproject(("gk", b), "gk", b)
                    for b in every:
                        wait_emptied(pe, ("g1T", b))
                        u = begin(("la", b))
                        end(nc.tensor.matmul(bk(u), g1T[0:RANK + 1, place_of(b, full), :], wgate[0:RANK + 1, :], start=True, stop=True),
                            ("la", b))
                elif t == 1:
                    pe.wait_ge(decay_ready, full + 1)
                    for b in every:
                        u = begin(("after", b))
                        end(nc.tensor.matmul(bk(u), const("after"), la[:, place_of(b, full), :], start=True, stop=True), ("after", b))
                    u = begin(("cum", full))
                    end(nc.tensor.matmul(bk(u), const("tri"), la[:, 0, :], start=True, stop=True), ("cum", full))
                    u = begin(("decay", full))
                    for x in range(GH):
                        last = nc.tensor.matmul(bk(u, 2 * x, 2 * x + 2), la[:, 0, x * GK:x * GK + GK], const("chunks"), start=True, stop=True)
                    end(last, ("decay", full))
                    gproject(("gq", full), "gq", full)
                    gproject(("gv", full, 0), "gv0", full)
                elif t == 2:
                    gproject(("gv", full, 1), "gv1", full)
                    pe.wait_ge(kd_ready, full)
                    transposes(("tr_qd", full), [gq[:, x * GK:x * GK + GK] for x in range(GH)])
                    transposes(("tr_kd", full), [kd[:, x * GK:x * GK + GK] for x in range(GH)])
                    wait_emptied(pe, ("tr_qd", full))
                    wait_emptied(pe, ("tr_kd", full))
                    u = begin(("att", full))
                    for x in range(GH):
                        c = slice(x * GK, x * GK + GK)
                        last = nc.tensor.matmul(bk(u, x * GK, x * GK + GK), kdT[:, c], qdT[:, c], start=True, stop=True)
                    end(last, ("att", full))
                    for b in rest:
                        gproject(("gv", b, 0), "gv0", b)
                elif t == 3:
                    for b in rest:
                        gproject(("gv", b, 1), "gv1", b)
                    gproject(("gr", full, 0), "gr0", full)
                    pe.wait_ge(kend_ready, full + 1)
                    for b in rest:
                        for i in range(2):
                            wait_emptied(pe, ("gv", b, i))
                            states(("st", b, i), i, 1, 1)
                    for i in range(2):
                        wait_emptied(pe, ("gv", full, i))
                        states(("u0", full, i), i, 0, 0)
                elif t == 4:
                    gproject(("gr", full, 1), "gr1", full)
                    pe.wait_ge(state1_ready, full)
                    for i in range(2):
                        u = ("o", full, i)
                        ub = begin(u)
                        for x in (2 * i, 2 * i + 1):
                            a = ub * 512 + (x % 2) * GV
                            nc.tensor.matmul(bank[:, a:a + GV], atm[:, x * GK:x * GK + GK], gv[:, 0, x * GV:x * GV + GV],
                                             start=True, stop=False)
                            for c, st in enumerate((state0, state1)):
                                last = nc.tensor.matmul(bank[c * CHUNK:c * CHUNK + CHUNK, a:a + GV],
                                                        qdT[:, x * GK + c * CHUNK:x * GK + c * CHUNK + CHUNK],
                                                        st[:, x, :], start=False, stop=True)
                        end(last, u)
                    for i in range(2):
                        states(("u1", full, i), i, 0, 1)
                elif t == 5:
                    pe.wait_ge(og_ready, full)
                    for i in range(2):
                        transposes(("tr_go", full, i), [og[:, (4 * i + x) * P:(4 * i + x) * P + P] for x in range(4)])
                    for i in range(2):
                        wait_emptied(pe, ("tr_go", full, i))
                    for i in range(2):
                        gproject(("go", full, i), f"gla_out{i}", full)
                elif t == 6:
                    tr_stream("tr_ffn1", 3 if full == 1 else 5, full)
                    for i in range(2):
                        wait_emptied(pe, ("tr_ffn1", full, i))
                    for i in range(2):
                        w = part(weights((f"wq1_{i}", full)), 0, KC, 512)
                        for x in range(4):
                            un = ("pq1", full, 4 * i + x)
                            b = begin(un)
                            for k in range(KC):
                                last = nc.tensor.matmul(bk(b, 0, P), w[:, k, x * P:x * P + P], hT[:, k, full * P:full * P + P],
                                                        start=(k == 0), stop=(k == KC - 1))
                            end(last, un)

            prepare(0, 0, 0)
            prepare(1, 0, 1)
            mix(0)
            with pe.Fori(1, 8) as g:
                prepare(g + 1, 0, 1)
                mix(g)
            prepare(9, 0, 2)
            mix(8)
            if upto == "peer0":
                return
            for full in (1, 2):
                for t in range(8):
                    g = 8 * full + 1 + t
                    prepare(g + 1, *((full - 1, 2 if full == 1 else 1) if t < 7 else (1, full)))
                    mix(g)
                    gla(t, full)
            with pe.Fori(25, 32) as g:
                prepare(g + 1, 1, 2)
                mix(g)
            mix(32)

        @block.scalar
        def _(act):
            def copy_unit(u, dst, src=None, width=512, parts=P):
                b = unit_bank(u)
                wait_filled(act, u)
                is_emptied(nc.scalar.activation(dst, bank[0:parts, b * 512:b * 512 + width] if src is None else src(b),
                                                ACT.Copy), u)

            def take_T(name, b, chunks=((0, 4), (4, 8))):
                for half, (c0, c1) in enumerate(chunks):
                    n = c1 - c0
                    copy_unit((name, b, half), hT[:, c0:c1, b * P:b * P + P],
                              lambda u: bk(u, 0, n * P).rearrange("p (c n) -> p c n", c=n))

            act.sem_inc(pt_low, 1)
            for b in range(NB):
                take_T("tr_attn", b)
            for b in range(NB):
                take_T("tr_low", b, ((0, 4), (4, 5)))

            def take_qT(hh, par):
                act.wait_ge(transposed, hh + 3)
                nc.scalar.activation(qT_head[0:QD, par, :], bank[0:QD, 0:ROWS], ACT.Copy).then_inc(qT_ready, 1)

            def take_probT(hh):
                act.wait_ge(p_transposed, hh + 3)
                nc.scalar.activation(probT[:, 0:512], bk(4), ACT.Copy).then_inc(pt_low, 1)

            def exps(hh, par):
                act.wait_ge(nm_ready, hh + 1)
                act.sem_inc(go["act"], 1)
                nm = stat[:, par, 3:6]
                for b in range(NB):
                    a, w = SCORE_AT[b]
                    nc.scalar.activation(prob[:, par, a:a + w], prob[:, par, a:a + w], ACT.Exp, bias=nm[:, b:b + 1],
                                         accum_out=stat[:, par, 6 + b:7 + b])
                nc.scalar.activation(stat[:, par, 9:12], nm, ACT.Exp, bias=sink[:, bass.ds(hh, 1)]).then_inc(probs_ready, 1)

            def head_step(i, par, latent, live=range(-1, 3)):
                if 2 in live:
                    take_qT(i + 2, par)
                if 1 in live:
                    exps(i + 1, 1 - par)
                if 0 in live:
                    take_probT(i)

            pipeline(act, head_step)
            for b in range(NB):
                take_T("tr_o", b)
            for b in range(NB):
                take_T("tr_ffn0", b)
            act.wait_ge(sk_zero, 1)
            for layer in range(2):
                u = ("sk", layer)
                wait_filled(act, u)
                b = unit_bank(u)
                nc.scalar.activation(skT[0:64, layer, 0:P], bank[0:64, b * 512:b * 512 + P], ACT.Copy)
                is_emptied(nc.scalar.activation(skT[64:P, layer, P:2 * P], bank[64:P, b * 512:b * 512 + P], ACT.Copy), u)
            if upto == "attn":
                return

            place_all = const("place")

            def prepare(g, tile):
                at_least(act, scores_ready, g)
                act.sem_inc(go["act"], 1)
                nc.scalar.activation(q_now[:, :], qT[:, bass.ds(P * tile, P)], ACT.Copy).then_inc(qnow_ready, 1)

            def gate_exps(g):
                act.wait_ge(best_ready, g + 1)
                nc.scalar.activation(gate_e[:, :], best[:, :], ACT.Exp, bias=z[:, 0:1], accum_out=z[:, 1:2]).then_inc(gate_exp, 1)

            def mix(g, j):
                act.wait_ge(gelu_in, g + 1)
                nc.scalar.activation(gl[:, 1, :], gl[:, 0, :], ACT.Tanh, scale=GELU_C).then_inc(gelu_tanh, 1)
                act.wait_ge(wgt_ready, g + 1)
                act.wait_ge(v_used, RING + TOPK * g)
                act.sem_inc(go["act"], 1)
                for k in range(TOPK):
                    nc.scalar.activation(wplace[:, k, :], place_all[:, bass.ds(112 - TT * j, P)], ACT.Copy,
                                         scale=wgt[:, k:k + 1]).then_inc(placed, 1)

            def gla(t, full):
                rest = PASSES[full][:-1]
                every = [full] + rest

                def take_g(u, dst, scale=1.0):
                    wait_filled(act, u)
                    is_emptied(nc.scalar.activation(dst, bk(unit_bank(u)), ACT.Copy, scale=scale), u)

                if t == 0:
                    for b in every:
                        take_T("tr_gla", b)
                    for b in every:
                        copy_unit(("g1", b), g1[:, place_of(b, full), :], width=RANK)
                    take_g(("gk", full), gk[:, 0, :])
                    for b in every:
                        copy_unit(("g1T", b), g1T[0:RANK, place_of(b, full), :], width=P, parts=RANK)
                    for b in rest:
                        take_g(("gk", b), gk[:, 1, :])
                elif t == 1:
                    for b in every:
                        e = ex[:, place_of(b, full), :]
                        act.wait_ge(minus_abs, nth_gate(b))
                        nc.scalar.activation(e, e, ACT.Exp).then_inc(gate_exp1, 1)
                        act.wait_ge(gate_exp1, nth_gate(b))
                        nc.scalar.activation(e, e, ACT.Ln, bias=1.0).then_inc(gate_log, 1)
                    for b in every:
                        u = ("after", b)
                        wait_filled(act, u)
                        is_emptied(nc.scalar.activation(ex[:, place_of(b, full), :], bk(unit_bank(u)), ACT.Exp), u)
                    u = ("cum", full)
                    wait_filled(act, u)
                    nc.scalar.activation(qdT, bk(unit_bank(u)), ACT.Exp)
                    is_emptied(nc.scalar.activation(kdT, bk(unit_bank(u)), ACT.Exp, scale=-1.0), u)
                    u = ("decay", full)
                    wait_filled(act, u)
                    is_emptied(nc.scalar.activation(dec, bk(unit_bank(u), 0, 2 * GH), ACT.Exp), u)
                    take_g(("gq", full), gq, GK ** -0.5)
                    take_g(("gv", full, 0), gv[:, 0, 0:512])
                elif t == 2:
                    take_g(("gv", full, 1), gv[:, 0, 512:1024])
                    take_g(("tr_qd", full), qdT)
                    take_g(("tr_kd", full), kdT)
                    for b in rest:
                        take_g(("gv", b, 0), gv[:, 1, 0:512])
                elif t == 3:
                    for b in rest:
                        take_g(("gv", b, 1), gv[:, 1, 512:1024])
                    take_g(("gr", full, 0), gr[:, 0:512], 0.5)
                    for b in rest:
                        for i in range(2):
                            take_g(("st", b, i), state0[:, 2 * i:2 * i + 2, :].rearrange("p h n -> p (h n)"))
                elif t == 4:
                    take_g(("gr", full, 1), gr[:, 512:1024], 0.5)
                    for i in range(2):
                        take_g(("o", full, i), og[:, 512 * i:512 * i + 512])
                elif t == 5:
                    act.wait_ge(norm_ms, 5 if full == 1 else 8)
                    wait_emptied(act, ("gr", full, 0))
                    wait_emptied(act, ("gr", full, 1))
                    nc.scalar.activation(sq, gr, ACT.Tanh).then_inc(silu_tanh, 1)
                    take_T("tr_go", full)
                elif t == 6:
                    take_T("tr_ffn1", full)
                    t0 = (full * P - PAD) * PH
                    for x in range(PH):
                        copy_unit(("pq1", full, x), qT[:, t0:t0 + P * PH].rearrange("p (t h) -> p t h", h=PH)[:, :, x], width=P)

            wait_emptied(act, ("pq0", 7))
            prepare(0, 0)
            gate_exps(0)
            prepare(1, 1)
            mix(0, 7)
            gate_exps(1)
            with act.Fori(1, 8) as g:
                prepare(g + 1, g + 1)
                mix(g, g - 1)
                gate_exps(g + 1)
            prepare(9, 9)
            mix(8, 7)
            gate_exps(9)
            if upto == "peer0":
                return
            for full in (1, 2):
                for t in range(8):
                    g = 8 * full + 1 + t
                    if t == 7:
                        wait_emptied(act, ("pq1", full, PH - 1))
                    prepare(g + 1, g + 1 if g + 1 < 17 else g + 1 - 16)
                    mix(g, t)
                    gate_exps(g + 1)
                    gla(t, full)
            with act.Fori(25, 32) as g:
                prepare(g + 1, g - 15)
                mix(g, g - 25)
                gate_exps(g + 1)
            mix(32, 7)

        @block.vector
        def _(dve):
            v = nc.vector
            steps = Steps(dve, d_step)
            n_norm = [0]

            def unit_ap(u, a=0, b=512):
                wait_filled(dve, u)
                return bk(unit_bank(u), a, b)

            def squares(src, junk, out):
                steps.did(v.tensor_tensor_reduce(out=junk, in0=src, in1=src, scale=1.0, scalar=0.0, op0=ALU.mult,
                                                 op1=ALU.add, accum_out=out))

            def mean(ap, width):
                steps.did(v.tensor_scalar(ap, ap, 1.0 / width, EPS, ALU.mult, ALU.add))

            def roots():
                n_norm[0] += 1
                steps.settle()
                dve.sem_inc(norm_ms, 1)
                dve.wait_ge(norm_rs, n_norm[0])

            def norm(n, blocks):
                for b in blocks:
                    squares(h[:, b, :], hn[:, b, :], small[:, b:b + 1])
                steps.settle()
                mean(small[:, blocks[0]:blocks[-1] + 1], D)
                roots()
                dve.wait_ge(gain_in, 16 * (n + 1))
                for b in blocks:
                    v.scalar_tensor_tensor(out=hn[:, b, :], in0=h[:, b, :], scalar=small[:, 3 + b:4 + b], in1=gain[:, :],
                                           op0=ALU.mult, op1=ALU.mult).then_inc(hn_ready, 1)

            dve.sem_inc(pt_high, 1)
            dve.sem_inc(o_taken, 1)
            dve.sem_inc(u_used, RING)
            steps.did(v.memset(g1T[0:32, :, :], 1.0))
            steps.did(v.memset(h[0:PAD, 0, :], 0.0))
            for t in (q_all, k_all):
                steps.did(v.memset(t[:, :, 0:HALF, HD:QD], 0.0))
            v.memset(skT[:, :, :], 0.0).then_inc(sk_zero, 1)
            dve.wait_ge(x_in, 32)
            steps.settle()
            norm(0, range(NB))
            for b in range(NB):
                u = ("mid", b)
                src = unit_ap(u)
                steps.did(v.tensor_copy(k_all[:, b, 0:HALF, 0:HD].rearrange("p (g r) d -> p g r d", g=2),
                                        src[:, 0:P].rearrange("p (g d) -> p g d", g=2).unsqueeze(2).broadcast_to([P, 2, 4, HD])))
                steps.did(v.tensor_copy(v_all[:, b, 0:HALF, :].rearrange("p (g r) d -> p g r d", g=2),
                                        src[:, P:2 * P].rearrange("p (g d) -> p g d", g=2).unsqueeze(2).broadcast_to([P, 2, 4, HD])))
                is_emptied(v.tensor_copy(low[:, b, 0:256], src[:, 256:512]), u)
            for b in range(NB):
                u = ("low", b)
                is_emptied(v.tensor_copy(low[:, b, 256:672], unit_ap(u, 0, 416)), u)
            dve.wait_ge(small_in, SMALL_LOADS * 16)
            steps.did(v.memset(sink[:, HALF:HEADS], NEG))
            for b in range(NB):
                wait_emptied(dve, ("mid", b))
                wait_emptied(dve, ("low", b))
                squares(low[:, b, 0:Q_LORA], rt[:, 0:Q_LORA], small[:, 6 + b:7 + b])
                steps.settle()
                squares(low[:, b, Q_LORA:Q_LORA + KV_LORA], rt[:, 0:KV_LORA], small[:, 9 + b:10 + b])
                steps.settle()
            mean(small[:, 6:9], Q_LORA)
            mean(small[:, 9:12], KV_LORA)
            roots()
            for b in range(NB):
                for a, w, s in ((0, Q_LORA, 12), (Q_LORA, KV_LORA, 15)):
                    ap = low[:, b, a:a + w]
                    steps.did(v.scalar_tensor_tensor(out=ap, in0=ap, scalar=small[:, s + b:s + b + 1], in1=low_gain[:, a:a + w],
                                                     op0=ALU.mult, op1=ALU.mult))
            steps.settle()
            dve.sem_inc(low_ready, 1)

            def rotate(x1, x2, t, shape, dst1, dst2, wide):
                cos, sin = (acst(n).rearrange("p (b r) -> p b r", b=NB) for n in ("cos", "sin"))
                if len(shape) == 4:
                    cos, sin = (a.unsqueeze(2).broadcast_to(shape) for a in (cos, sin))
                for i, (x, y) in enumerate(((x1, cos), (x2, sin), (x2, cos), (x1, sin))):
                    steps.did(v.tensor_tensor(t[i], x, y, ALU.mult))
                steps.settle()
                steps.did(v.tensor_tensor(dst1, wide(t[0]), wide(t[1]), ALU.subtract))
                steps.did(v.tensor_tensor(dst2, wide(t[2]), wide(t[3]), ALU.add))
                steps.settle()

            n = NB * ROPE
            t = [rt[:, i * n:(i + 1) * n].rearrange("p (b r) -> p b r", b=NB) for i in range(4)]
            rotate(low[:, :, 640:656], low[:, :, 656:672], t, [P, NB, ROPE], k_mla[:, :, :, 64:80], k_mla[:, :, :, 80:96],
                   lambda a: a.unsqueeze(2).broadcast_to([P, NB, HALF, ROPE]))
            for b in range(NB):
                u = ("qa", b)
                is_emptied(v.tensor_scalar(q_swa[:, b], unit_ap(u).rearrange("p (h d) -> p h d", h=HALF), HD ** -0.5, None,
                                           ALU.mult), u)
            for b in range(NB):
                for i in range(2):
                    u = ("uq", b, i)
                    is_emptied(v.tensor_scalar(q_mla[:, b, 4 * i:4 * i + 4, :].rearrange("p h d -> p (h d)"), unit_ap(u, 0, 384),
                                               QD ** -0.5, None, ALU.mult), u)
            for b in range(NB):
                for i in range(2):
                    u = ("ukv", b, i)
                    src = unit_ap(u).rearrange("p (h d) -> p h d", h=4)
                    steps.did(v.tensor_copy(k_mla[:, b, 4 * i:4 * i + 4, 0:HD], src[:, :, 0:HD]))
                    is_emptied(v.tensor_copy(v_all[:, b, HALF + 4 * i:HALF + 4 * i + 4, :], src[:, :, HD:2 * HD]), u)
            n = NB * HALF * ROPE
            t = [rt[:, i * n:(i + 1) * n].rearrange("p (b h r) -> p b h r", b=NB, h=HALF) for i in range(4)]
            for b in range(NB):
                for i in range(2):
                    wait_emptied(dve, ("uq", b, i))
                    wait_emptied(dve, ("ukv", b, i))
            rotate(q_mla[:, :, :, 64:80], q_mla[:, :, :, 80:96], t, [P, NB, HALF, ROPE], q_mla[:, :, :, 64:80],
                   q_mla[:, :, :, 80:96], lambda a: a)
            dve.sem_inc(heads_ready, 2)

            def take_kT(hh, par):
                dve.wait_ge(transposed, hh + 3)
                v.tensor_copy(kT_head[0:QD, par, :], bank[0:QD, 512:512 + ROWS]).then_inc(kT_ready, 1)

            def mask_scores(hh, par, latent):
                dve.wait_ge(p_transposed, hh + 1)
                dve.wait_ge(scored, hh + 1)
                dve.sem_inc(go["dve"], 1)
                for b in range(NB):
                    a, w = SCORE_AT[b]
                    v.tensor_tensor_reduce(out=prob[:, par, a:a + w], in0=bank[:, 1024 + a:1024 + a + w],
                                           in1=masks[:, latent * 768 + a:latent * 768 + a + w], scale=1.0, scalar=-3e38, op0=ALU.add,
                                           op1=ALU.max, accum_out=stat[:, par, b:b + 1]).then_inc(masked, 1)
                dve.wait_ge(masked, NB * hh + NB)
                v.tensor_scalar(stat[:, par, 3:6], stat[:, par, 0:3], sink[:, bass.ds(hh, 1)], -1.0, ALU.max, ALU.mult)\
                    .then_inc(nm_ready, 1)

            def denominators(hh, par):
                dve.wait_ge(probs_ready, hh + 1)
                at_least(dve, o_taken, hh)
                dve.sem_inc(go["dve"], 1)
                v.tensor_tensor(stat[:, par, 12:15], stat[:, par, 6:9], stat[:, par, 9:12], ALU.add).then_inc(den_ready, 1)
                dve.wait_ge(den_ready, 2 * hh + 1)
                v.reciprocal(stat[:, par, 12:15], stat[:, par, 12:15]).then_inc(den_ready, 1)

            def take_values(hh, par):
                dve.wait_ge(den_ready, 2 * hh + 2)
                dve.wait_ge(pv_done, hh + 1)
                dve.sem_inc(go["dve"], 1)
                v.tensor_tensor(hn[:, :, bass.ds(hh * HD, HD)], bk(6, 0, NB * HD).rearrange("p (b d) -> p b d", b=NB),
                                stat[:, par, 12:15].unsqueeze(2).broadcast_to([P, NB, HD]), ALU.mult).then_inc(o_taken, 1)

            def take_probT(hh):
                dve.wait_ge(p_transposed, hh + 3)
                v.tensor_copy(probT[:, 512:768], bk(5, 0, 256)).then_inc(pt_high, 1)

            def head_step(i, par, latent, live=range(-1, 3)):
                if 2 in live:
                    take_kT(i + 2, par)
                if 1 in live:
                    mask_scores(i + 1, 1 - par, latent)
                if 0 in live:
                    denominators(i, par)
                if -1 in live:
                    take_values(i - 1, 1 - par)
                if 0 in live:
                    take_probT(i)

            pipeline(dve, head_step)

            def add_to_h(u, b, i):
                hs = h[:, b, 512 * i:512 * i + 512]
                is_emptied(v.tensor_tensor(hs, hs, unit_ap(u), ALU.add), u)

            for i in range(2):
                for b in range(NB):
                    add_to_h(("ao", b, i), b, i)
            wait_emptied(dve, ("ao", 2, 0))
            wait_emptied(dve, ("ao", 1, 1))
            wait_emptied(dve, ("ao", 2, 1))
            v.memset(h[0:PAD, 0, :], 0.0).then_inc(pad_zero, 1)
            dve.wait_ge(pad_zero, 1)
            norm(1, range(NB))
            for x in range(PH):
                u = ("pq0", x)
                is_emptied(v.tensor_copy(qT[:, :].rearrange("p (t h) -> p t h", h=PH)[:, :, x], unit_ap(u, 0, LIVE)), u)
            if upto == "attn":
                return

            def best16(vals, rest_ap, values, indices, topk):
                topk.chain(v.max(values[:, 0:8], vals))
                topk.did(v.max_index(indices[:, 0:8], values[:, 0:8], vals))
                topk.chain(v.match_replace(rest_ap, values[:, 0:8], vals, -3e38))
                topk.chain(v.max(values[:, 8:16], rest_ap))
                topk.chain(v.max_index(indices[:, 8:16], values[:, 8:16], rest_ap))

            topk = Steps(dve, topk_step)
            mixs = Steps(dve, mix_step)

            def choose(g, layer):
                dve.wait_ge(scores_ready, g + 1)
                at_least(dve, idx_taken, g)
                at_least(dve, gate_exp, g)
                dve.sem_inc(go["dve"], 1)
                topk.restart()
                for s in range(2):
                    best16(score[:, s * P:s * P + P], rest[:, s, :], top[:, s, :], top_i[:, s, :], topk)
                topk.did(v.tensor_copy(top_f[:, :, :], top_i[:, :, :]))
                pair = cand[:, :].rearrange("p (a b) -> p a b", a=TOPK)
                topk.chain(v.tensor_tensor(pair, top[:, 0, :].unsqueeze(2).broadcast_to([P, TOPK, TOPK]),
                                           top[:, 1, :].unsqueeze(1).broadcast_to([P, TOPK, TOPK]), ALU.add))
                best16(cand[:, :], cand_rest[:, :], best, best_j, topk)
                topk.did(v.tensor_scalar(digit[:, 0, :], best_j[:, :], 4, None, ALU.logical_shift_right))
                topk.did(v.tensor_scalar(digit[:, 1, :], best_j[:, :], 15, None, ALU.bitwise_and))
                topk.chain(v.tensor_scalar(z[:, 0:1], best[:, 0:1], -1.0, None, ALU.mult))
                dve.sem_inc(best_ready, 1)
                topk.chain(v.tensor_copy(digit_f[:, :, :], digit[:, :, :]))
                topk.chain(v.tensor_tensor(onehot[:, :, :], digit_f[:, :, :].rearrange("p s k -> p (s k)").unsqueeze(2).broadcast_to([P, 2 * TOPK, TOPK]),
                                           const("iota").unsqueeze(1).broadcast_to([P, 2 * TOPK, TOPK]), ALU.is_equal))
                one = onehot[:, :, :].rearrange("p (s k) a -> p s k a", s=2)
                topk.chain(v.tensor_tensor(one, one, top_f[:, :, :].unsqueeze(2).broadcast_to([P, 2, TOPK, TOPK]), ALU.mult))
                topk.chain(v.tensor_reduce(out=picked[:, :, :].rearrange("p s k -> p (s k)"), in_=onehot[:, :, :], axis=AX, op=ALU.add))
                topk.chain(v.tensor_scalar(picked[:, 0, :], picked[:, 0, :], float(N_KEYS), float(layer * EXPERTS), ALU.mult, ALU.add))
                topk.chain(v.tensor_tensor(idx_next[:, :], picked[:, 0, :], picked[:, 1, :], ALU.add))
                dve.sem_inc(idx_ready, 1)

            def pick(g, j):
                at_least(dve, xrep_ready, g)
                v.tensor_scalar(pick_now[:, :], const("row_token"), const("token")[:, bass.ds(j, 1)], None, ALU.is_equal)\
                    .then_inc(pick_ready, 1)

            def dot(g, slots):
                dve.wait_ge(xrep_ready, g + 1)
                dve.sem_inc(go["dve"], 1)
                for k in slots:
                    dve.wait_ge(u_in[k % RING], 16 * (2 * g + k // RING + 1))
                    v.tensor_tensor_reduce(out=urow[:, k % RING, :], in0=urow[:, k % RING, :], in1=xrep, scale=1.0, scalar=0.0,
                                           op0=ALU.mult, op1=ALU.add, accum_out=dots[:, k:k + 1]).then_inc(u_used, 1)

            def weigh(g):
                dve.wait_ge(u_used, RING + TOPK * (g + 1))
                dve.wait_ge(gate_exp, g + 1)
                dve.sem_inc(go["dve"], 1)
                mixs.restart()
                a = gl[:, 0, :]
                mixs.did(v.reciprocal(z[:, 2:3], z[:, 1:2]))
                mixs.chain(v.tensor_tensor(a, dots[:, :], dots[:, :], ALU.mult))
                mixs.chain(v.tensor_scalar(a, a, 0.044715, 1.0, ALU.mult, ALU.add))
                mixs.chain(v.tensor_tensor(a, a, dots[:, :], ALU.mult))
                dve.sem_inc(gelu_in, 1)
                mixs.chain(v.scalar_tensor_tensor(out=gate[:, :], in0=gate_e[:, :], scalar=z[:, 2:3], in1=dots[:, :],
                                                  op0=ALU.mult, op1=ALU.mult))
                mixs.chain(v.tensor_scalar(gate[:, :], gate[:, :], 0.5, None, ALU.mult))
                dve.wait_ge(gelu_tanh, g + 1)
                dve.sem_inc(go["dve"], 1)
                mixs.chain(v.scalar_tensor_tensor(out=wgt[:, :], in0=gl[:, 1, :], scalar=1.0, in1=gate[:, :], op0=ALU.add, op1=ALU.mult))
                dve.sem_inc(wgt_ready, 1)

            def add_experts(g, b):
                dve.wait_ge(v_used, RING + TOPK * (g + 1))
                v.tensor_tensor(h[:, b, :], h[:, b, :], yacc, ALU.add).then_inc(y_added, 1)
                dve.wait_ge(y_added, g + 1)
                dve.sem_inc(go["dve"], 1)

            FIRST, SECOND = range(0, TOPK // 2), range(TOPK // 2, TOPK)

            def tile(g, b, layer, j, side=None):
                pick(g + 1, j)
                dot(g, SECOND)
                weigh(g)
                choose(g + 1, layer)
                if side:
                    side()
                dot(g + 1, FIRST)
                add_experts(g, b)

            def gla(t, full):
                rest = PASSES[full][:-1]
                every = [full] + rest
                if t == 0:
                    norm(2 if full == 1 else 4, PASSES[full])
                elif t == 1:
                    for b in every:
                        u = ("la", b)
                        src = unit_ap(u)
                        l, e = la[:, place_of(b, full), :], ex[:, place_of(b, full), :]
                        steps.did(v.tensor_scalar(l, src, 0.0, 1.0 / TAU, ALU.min, ALU.mult))
                        is_emptied(v.tensor_scalar(e, src, 0.0, None, ALU.max), u)
                        steps.settle()
                        wait_emptied(dve, u)
                        v.scalar_tensor_tensor(out=e, in0=l, scalar=TAU, in1=e, op0=ALU.mult, op1=ALU.subtract).then_inc(minus_abs, 1)
                    for b in every:
                        l, e = la[:, place_of(b, full), :], ex[:, place_of(b, full), :]
                        dve.wait_ge(gate_log, nth_gate(b))
                        v.scalar_tensor_tensor(out=l, in0=e, scalar=-1.0 / TAU, in1=l, op0=ALU.mult, op1=ALU.add).then_inc(decay_ready, 1)
                elif t == 2:
                    wait_emptied(dve, ("decay", full))
                    wait_emptied(dve, ("gq", full))
                    steps.chain(v.tensor_tensor(gq, gq, qdT, ALU.mult))
                    v.tensor_tensor(kd, gk[:, 0, :], kdT, ALU.mult).then_inc(kd_ready, 1)
                    dve.wait_ge(kd_ready, full)
                    for b in every:
                        k = gk[:, place_of(b, full), :]
                        wait_emptied(dve, ("gk", b))
                        v.tensor_tensor(k, k, ex[:, place_of(b, full), :], ALU.mult).then_inc(kend_ready, 1)
                elif t == 3:
                    u = ("att", full)
                    is_emptied(v.tensor_tensor(atm.rearrange("p (h n) -> p h n", h=GH), unit_ap(u).rearrange("p (h n) -> p h n", h=GH),
                                               const("tri").unsqueeze(1).broadcast_to([P, GH, P]), ALU.mult), u)
                elif t == 4:
                    wait_emptied(dve, ("att", full))
                    for b in rest:
                        for i in range(2):
                            wait_emptied(dve, ("st", b, i))
                    for x in range(GH):
                        next_state(("u0", full, x // 2), state1, state0, x, 0)
                    wait_emptied(dve, ("u0", full, 1))
                    dve.sem_inc(state1_ready, 1)
                elif t == 5:
                    wait_emptied(dve, ("o", full, 1))
                    for x in range(GH):
                        c = slice(x * GV, x * GV + GV)
                        squares(og[:, c], sq[:, c], gms[:, x:x + 1])
                    steps.settle()
                    mean(gms[:, 0:4], GV)
                    steps.settle()
                    dve.sem_inc(norm_ms, 1)
                    for x in range(GH):
                        next_state(("u1", full, x // 2), state0, state1, x, 1)
                    wait_emptied(dve, ("u1", full, 1))
                    dve.wait_ge(silu_tanh, full)
                    steps.chain(v.scalar_tensor_tensor(out=gr, in0=sq, scalar=1.0, in1=gr, op0=ALU.add, op1=ALU.mult))
                    n_norm[0] += 1
                    dve.wait_ge(norm_rs, n_norm[0])
                    for x in range(GH):
                        c = slice(x * GV, x * GV + GV)
                        steps.did(v.scalar_tensor_tensor(out=og[:, c], in0=og[:, c], scalar=gms[:, 4 + x:5 + x], in1=onorm[:, :],
                                                         op0=ALU.mult, op1=ALU.mult))
                    steps.settle()
                    v.tensor_tensor(og, og, gr, ALU.mult).then_inc(og_ready, 1)
                elif t == 6:
                    for i in range(2):
                        add_to_h(("go", full, i), full, i)
                    for i in range(2):
                        wait_emptied(dve, ("go", full, i))
                    norm(3 if full == 1 else 5, [full])

            def next_state(u, out, before, x, c):
                src = unit_ap(u)[:, (x % 2) * GV:(x % 2) * GV + GV]
                ins = v.scalar_tensor_tensor(out=out[:, x, :], in0=before[:, x, :], scalar=dec[:, 2 * x + c:2 * x + c + 1],
                                             in1=src, op0=ALU.mult, op1=ALU.add)
                if x % 2:
                    is_emptied(ins, u)

            wait_emptied(dve, ("sk", 0))
            wait_emptied(dve, ("sk", 1))
            pick(0, 7)
            choose(0, 0)
            dot(0, FIRST)
            tile(0, 0, 0, 0)
            with dve.Fori(1, 8) as g:
                tile(g, 1, 0, g)
            tile(8, 1, 0, 0)
            if upto == "peer0":
                return
            for full in (1, 2):
                for t in range(8):
                    g = 8 * full + 1 + t
                    tile(g, 2 if full == 1 else 1, full - 1 if t < 7 else 1, (t + 1) % 8, lambda: gla(t, full))
            tile(25, 2, 1, 1, lambda: norm(6, [1]))
            with dve.Fori(26, 32) as g:
                tile(g, 2, 1, g - 24)
            dot(32, SECOND)
            weigh(32)
            add_experts(32, 2)
            norm(6, [2])


SMALL_LOADS = 10
_INS = ["x", "meta_tokens", "attn_norm", "attn_w_in", "mla_q_norm", "mla_w_uq", "mla_kv_norm", "mla_w_ukv", "swa_sinks",
        "attn_w_out", "gla_norm", "gla_w_in", "gla_w_gate", "gla_b_gate", "gla_out_norm", "gla_w_out", "ffn_norm",
        "peer_w_query", "peer_sub_keys", "peer_u", "peer_v", "final_norm"]


def kernel(**inputs):
    import concourse.bacc as bacc
    from concourse.bass_utils import run_bass_kernel_spmd

    nc = bacc.Bacc("TRN2", target_bir_lowering=False, num_devices=1)
    arrays = {n: np.ascontiguousarray(inputs[n]) for n in _INS}
    arrays["final_norm"] = arrays["final_norm"].reshape(1, D)
    arrays["consts"] = constants()
    io = {n: nc.dram_tensor(n, a.shape, mybir.dt.from_np(a.dtype), kind="ExternalInput").ap() for n, a in arrays.items()}
    io["out"] = nc.dram_tensor("out", (1, SEQ, D), F32, kind="ExternalOutput").ap()
    build(nc, io, UPTO)
    r = run_bass_kernel_spmd(nc, [arrays], core_ids=[0])
    return r.results[0]["out"]


UPTO = "all"
```

```python
import numpy as np
import concourse.bass as bass
from concourse import mybir
from contextlib import ExitStack

F32 = mybir.dt.float32
U32 = mybir.dt.uint32
ALU = mybir.AluOpType
ACT = mybir.ActivationFunctionType
AX = mybir.AxisListType.X

P = 128
D = 1024
KC = D // P
N_META, SEQ = 16, 256
NB = 3
ROWS = NB * P
PAD = ROWS - N_META - SEQ
LIVE = ROWS - PAD
EPS = 1e-6
NEG = -1e30

HEADS = 16
HALF = HEADS // 2
HD = 64
QD = 96
ROPE = 16
Q_LORA, KV_LORA = 384, 256
WINDOW = 128

GH, GK, GV = 4, 128, 256
GKD, GVD, RANK = GH * GK, GH * GV, 16
TAU = 16.0
CHUNK = 64

TOPK, N_KEYS, PH = 16, 128, 8
EXPERTS = N_KEYS * N_KEYS
TT = P // PH
RING = 8
GELU_C = 0.7978845608028654
WSLOTS = 2

CONST_PARTS = [("ident", P), ("row_token", P), ("token", 8), ("place", 112 + P), ("iota", 16), ("tri", P), ("after", P),
               ("chunks", 2), ("neghalf", 8), ("cos", NB * ROPE), ("sin", NB * ROPE), ("mask_swa", 432), ("mask_mla", 432)]
CONST_AT = {}
_at = 0
for _n, _w in CONST_PARTS:
    CONST_AT[_n] = (_at, _w)
    _at += _w
CONST_COLS = _at
LIVE_CONSTS = CONST_AT["cos"][0]

SCORE_AT = {2: (0, 272), 0: (272, 16), 1: (288, 144)}
SCORES = 432
LIVE_AT = (0, N_META, N_META + P)


def constants():
    c = np.zeros((P, CONST_COLS), np.float32)

    def put(name, a):
        at, w = CONST_AT[name]
        c[:, at:at + w] = a.reshape(P, w)

    i = np.arange(P)
    put("ident", np.eye(P, dtype=np.float32))
    put("row_token", np.broadcast_to((i // PH).astype(np.float32), (P, P)))
    put("token", (i[:, None] - TT * np.arange(8)[None]).astype(np.float32))
    put("place", (np.arange(112 + P)[None] == 112 + i[:, None] // PH).astype(np.float32))
    put("iota", np.broadcast_to(np.arange(16, dtype=np.float32), (P, 16)))
    same = i[:, None] // CHUNK == i[None] // CHUNK
    put("tri", (same & (i[:, None] <= i[None])).astype(np.float32))
    put("after", (same & (i[:, None] > i[None])).astype(np.float32))
    put("chunks", (i[:, None] // CHUNK == np.arange(2)[None]).astype(np.float32))
    put("neghalf", np.full((P, 8), -0.5, np.float32))
    inv = np.float32(10000.0) ** (-np.arange(0, 2 * ROPE, 2, dtype=np.float32) / np.float32(2 * ROPE))
    pos = np.stack([i + at for at in LIVE_AT], axis=1).astype(np.float32)
    ang = (pos[:, :, None] * inv[None, None]).astype(np.float32)
    put("cos", np.cos(ang))
    put("sin", np.sin(ang))
    for name, window in (("mask_swa", WINDOW), ("mask_mla", ROWS)):
        m = np.zeros((P, SCORES), np.float32)
        for b, (at, w) in SCORE_AT.items():
            q, k = (LIVE_AT[b] + i)[:, None], np.arange(w)[None]
            m[:, at:at + w] = np.where(((k <= q) & (q - k < window)) | ((b == 0) & (i[:, None] >= N_META)), 0.0, NEG)
        put(name, m)
    return c


class Steps:

    def __init__(self, eng, sem):
        self.eng, self.sem, self.n = eng, sem, 0

    def did(self, ins):
        ins.then_inc(self.sem, 1)
        self.n += 1

    def settle(self):
        self.eng.wait_ge(self.sem, self.n)

    def chain(self, ins):
        self.did(ins)
        self.settle()

    def restart(self):
        self.eng.sem_clear(self.sem)
        self.n = 0


def gain_units(n):
    return [("gain", n, i) for i in range(2)]


def gla_units(full, blocks):
    rest = blocks[:-1]
    every = [full] + rest
    return (
        [("tr_gla", b, i) for b in every for i in range(2)] + gain_units(3 if full == 1 else 5)
        + [("g1", b) for b in every] + [("gk", full)]
        + [("g1T", b) for b in every] + [("gk", b) for b in rest] + [("la", b) for b in every]
        + [("after", b) for b in every] + [("cum", full), ("decay", full), ("gq", full), ("gv", full, 0)]
        + [("gv", full, 1), ("tr_qd", full), ("tr_kd", full), ("att", full)] + [("gv", b, 0) for b in rest]
        + [("gv", b, 1) for b in rest] + [("gr", full, 0)] + [("st", b, i) for b in rest for i in range(2)]
        + [("u0", full, i) for i in range(2)]
        + [("gr", full, 1)] + [("o", full, i) for i in range(2)] + [("u1", full, i) for i in range(2)]
        + [("tr_go", full, i) for i in range(2)] + [("go", full, i) for i in range(2)]
        + [("tr_ffn1", full, i) for i in range(2)] + gain_units(4 if full == 1 else 6) + [("pq1", full, x) for x in range(PH)])


def gla_weights(full, rest):
    last = rest[-1] if rest else full
    return [(("gk", full), ("gk", last)), (("gq", full), ("gq", full)), (("gv0", full), ("gv", last, 0)),
            (("gv1", full), ("gv", last, 1)), (("gr0", full), ("gr", full, 0)), (("gr1", full), ("gr", full, 1)),
            (("gla_out0", full), ("go", full, 0)), (("gla_out1", full), ("go", full, 1)),
            (("wq1_0", full), ("pq1", full, 3)), (("wq1_1", full), ("pq1", full, 7))]


def query_units(b):
    queries = [("pq0", b, x) for x in range(PH)] if b else [("pq0_rows", 0), ("pq0_rows", 1), ("pq0_T",)]
    return [("tr_ffn0", b, i) for i in range(2)] + queries


UNITS = (
    gain_units(0) + [("tr_attn", b, i) for b in range(NB) for i in range(2)]
    + [(n, b) for n in ("mid", "low", "qa") for b in range(NB)]
    + [(n, b, i) for n in ("tr_low", "uq", "ukv") for b in range(NB) for i in range(2)] + [("sk", 0), ("sk", 1)]
    + [("tr_o", 0, 0), ("tr_o", 0, 1), ("ao", 0, 0), ("ao", 0, 1)] + gain_units(1) + [("tr_o", b, i) for b in (1, 2) for i in range(2)]
    + query_units(0) + [("ao", 1, 0), ("ao", 1, 1)] + query_units(1)
    + [("ao", 2, 0), ("ao", 2, 1)] + query_units(2)[:2] + gain_units(2) + query_units(2)[2:]
    + gla_units(1, [0, 1]) + gla_units(2, [2]))
UNIT_AT = {u: n for n, u in enumerate(UNITS)}
assert len(UNIT_AT) == len(UNITS)
WEIGHTS = [("in_mid", ("mid", 2)), ("in_low", ("low", 2)), ("in_qa", ("qa", 2)), ("uq", ("uq", 2, 1)), ("ukv", ("ukv", 2, 1)),
           ("attn_out0", ("ao", 2, 0)), ("attn_out1", ("ao", 2, 1))]
WEIGHTS += gla_weights(1, [0]) + gla_weights(2, [])
GROUP_AT = {g: n for n, (g, _) in enumerate(WEIGHTS)}
UNIT_BANKS = (5, 6, 7)



def build(nc, io):
    ctx = ExitStack()
    with ctx:
        def sb(name, shape, dt=F32):
            return ctx.enter_context(nc.sbuf_tensor(name, shape, dt))

        def sem(name):
            return ctx.enter_context(nc.semaphore(name))

        h = sb("h", [P, NB, D])
        hn = sb("hn", [P, NB, D])
        hT = sb("hT", [P, KC, ROWS])
        gain_rows = sb("gain_rows", [16, D // 2])
        gain = sb("gain", [P, D])
        qT = sb("qT", [P, LIVE * PH])
        skT = sb("skT", [P, 2, 2 * N_KEYS])
        con = sb("con", [P, LIVE_CONSTS])
        wring = sb("wring", [P, WSLOTS, KC * 512])
        arena = sb("arena", [P, 2 * RING * D + TOPK * P])
        gws = sb("gws", [P, 10128])
        small = sb("small", [P, 64])
        g1w = sb("g1w", [P, KC, RANK])
        wgate = sb("wgate", [32, GKD])
        onorm = sb("onorm", [P, GV])

        def part(t, at, *shape):
            n = int(np.prod(shape))
            ap = t[:, at:at + n]
            if len(shape) == 1:
                return ap
            names = "abcd"[:len(shape)]
            return ap.rearrange(f"p ({' '.join(names)}) -> p {' '.join(names)}", **dict(zip(names, shape)))

        def const(name):
            at, w = CONST_AT[name]
            return con[:, at:at + w]

        ident = const("ident")
        bank = ctx.enter_context(nc.psum_tensor("bank", [P, 8 * 512], F32))

        def bk(n, a=0, b=512):
            return bank[:, n * 512 + a:n * 512 + b]

        at = 0

        def take(*shape):
            nonlocal at
            ap = part(arena, at, *shape)
            at += int(np.prod(shape))
            return ap

        v_all = take(NB, HEADS, HD)
        low = take(NB, Q_LORA + KV_LORA + 2 * ROPE)
        acon = take(CONST_COLS - LIVE_CONSTS)
        q_stage = take(2, NB, QD)
        k_stage = take(2, NB, QD)
        qT_head = take(2, LIVE)
        kT_head = take(2, LIVE)
        prob = take(2, SCORES)
        probT = take(2, NB * P)
        sink = take(HEADS)
        low_gain = take(Q_LORA + KV_LORA)
        stat = take(2, 16)
        rt = take(4 * NB * HALF * ROPE)
        assert at <= 2 * RING * D + TOPK * P, at
        wq0 = part(gws, 0, 2, KC, 512)
        q_rows = part(gws, 2 * KC * 512, D)
        q_all = part(gws, 0, NB, HEADS, QD)
        k_all = part(gws, NB * HEADS * QD, NB, HEADS, QD)
        q_swa, q_mla = q_all[:, :, 0:HALF, 0:HD], q_all[:, :, HALF:HEADS, :]
        k_mla = k_all[:, :, HALF:HEADS, :]

        masks = acon[:, 2 * NB * ROPE:]

        def acst(name):
            a, w = CONST_AT[name]
            return acon[:, a - LIVE_CONSTS:a - LIVE_CONSTS + w]

        urow = part(arena, 0, RING, D)
        vrow = part(arena, RING * D, RING, D)
        wplace = part(arena, 2 * RING * D, TOPK, P)
        pick_now = sb("pick_now", [P, P])
        q_now = sb("q_now", [P, P])
        top = sb("top", [P, 2, TOPK])
        top_i = sb("top_i", [P, 2, TOPK], U32)
        top_f = sb("top_f", [P, 2, TOPK])
        pairs = sb("pairs", [P, 2 * TOPK * TOPK])
        cand = pairs[:, 0:256]
        cand_rest = pairs[:, 256:512]
        onehot = part(pairs, 0, 2 * TOPK, TOPK)
        rest = part(pairs, 256, 2, N_KEYS)
        best = sb("best", [P, TOPK])
        best_j = sb("best_j", [P, TOPK], U32)
        digit = sb("digit", [P, 2, TOPK], U32)
        digit_f = sb("digit_f", [P, 2, TOPK])
        picked = sb("picked", [P, 2, TOPK])
        idx_next = sb("idx_next", [P, TOPK], U32)
        idx_now = sb("idx_now", [P, 2, TOPK], U32)
        dots = sb("dots", [P, TOPK])
        gl = sb("gl", [P, 2, TOPK])
        gate = sb("gate", [P, TOPK])
        gate_e = sb("gate_e", [P, TOPK])
        z = sb("z", [P, 4])
        wgt = sb("wgt", [P, TOPK])
        xrep = bank[:, 0:1024]
        score = bk(2, 0, 256)
        yacc = bank[:, 1536:2560]

        gat = 0

        def gtake(*shape):
            nonlocal gat
            ap = part(gws, gat, *shape)
            gat += int(np.prod(shape))
            return ap

        gq = gtake(GKD)
        gk = gtake(2, GKD)
        gv = gtake(2, GVD)
        gr = gtake(GVD)
        la = gtake(2, GKD)
        ex = gtake(2, GKD)
        qdT = gtake(GKD)
        kdT = gtake(GKD)
        state0 = gtake(GH, GV)
        state1 = gtake(GH, GV)
        g1T = gtake(2, P)
        g1 = gtake(2, RANK)
        dec = gtake(2 * GH)
        gms = gtake(8)
        assert gat <= 10128, gat
        kd = la[:, 0, :]
        atm = la[:, 1, :]
        og = ex.rearrange("p s n -> p (s n)")
        sq = la.rearrange("p s n -> p (s n)")

        x_in = sem("x_in")
        con_in = sem("con_in")
        small_in = sem("small_in")
        rows_in = sem("rows_in")
        wq0_in = sem("wq0_in")
        w_in = [sem(f"w_in{i}") for i in range(WSLOTS)]
        filled = [sem(f"filled{i}") for i in UNIT_BANKS]
        emptied = [sem(f"emptied{i}") for i in UNIT_BANKS]
        d_step = sem("d_step")
        norm_ms = sem("norm_ms")
        norm_rs = sem("norm_rs")
        hn_ready = sem("hn_ready")
        low_ready = sem("low_ready")
        heads_ready = sem("heads_ready")
        staged = sem("staged")
        transposed = sem("transposed")
        qT_ready = sem("qT_ready")
        kT_ready = sem("kT_ready")
        scored = sem("scored")
        masked = sem("masked")
        nm_ready = sem("nm_ready")
        probs_ready = sem("probs_ready")
        p_transposed = sem("p_transposed")
        pt_low = sem("pt_low")
        pt_high = sem("pt_high")
        pv_done = sem("pv_done")
        o_taken = sem("o_taken")
        minus_abs = sem("minus_abs")
        gate_exp1 = sem("gate_exp1")
        state1_ready = sem("state1_ready")
        gate_log = sem("gate_log")
        decay_ready = sem("decay_ready")
        kd_ready = sem("kd_ready")
        kend_ready = sem("kend_ready")
        silu_tanh = sem("silu_tanh")
        og_ready = sem("og_ready")
        den_ready = sem("den_ready")
        u_in = [sem(f"u_in{i}") for i in range(RING)]
        v_in = [sem(f"v_in{i}") for i in range(RING)]
        u_used = sem("u_used")
        v_used = sem("v_used")
        idx_ready = sem("idx_ready")
        idx_taken = sem("idx_taken")
        go = {e: sem(f"go_{e}") for e in ("pool", "act", "dve", "pe")}
        rows_zero = sem("rows_zero")
        sk_zero = sem("sk_zero")
        pick_ready = sem("pick_ready")
        qnow_ready = sem("qnow_ready")
        xrep_ready = sem("xrep_ready")
        scores_ready = sem("scores_ready")
        topk_step = sem("topk_step")
        mix_step = sem("mix_step")
        best_ready = sem("best_ready")
        gate_exp = sem("gate_exp")
        gelu_in = sem("gelu_in")
        gelu_tanh = sem("gelu_tanh")
        wgt_ready = sem("wgt_ready")
        placed = sem("placed")
        y_added = sem("y_added")
        out_done = sem("out_done")

        def at_least(eng, semaphore, n):
            if not (isinstance(n, int) and n <= 0):
                eng.wait_ge(semaphore, n)

        def pipeline(eng, head_step):
            head_step(0, 0, 0, (0, 1, 2))
            for latent in range(2):
                with eng.Fori(3 * latent, 3 * latent + 3) as j:
                    head_step(2 * j + 1, 1, latent)
                    head_step(2 * j + 2, 0, latent)
            head_step(HEADS - 3, 1, 1)
            head_step(HEADS - 2, 0, 1, (-1, 0, 1))
            head_step(HEADS - 1, 1, 1, (-1, 0))
            head_step(HEADS, 0, 1, (-1,))

        KEY_BLOCKS = [(2, 1), (2, 2), (1, 1)]

        def live_parts(b):
            return P if b else N_META

        def unit_bank(u):
            return UNIT_BANKS[UNIT_AT[u] % 3]

        def wait_filled(eng, u):
            n = UNIT_AT[u]
            eng.wait_ge(filled[n % 3], n // 3 + 1)

        def wait_emptied(eng, u):
            n = UNIT_AT[u]
            eng.wait_ge(emptied[n % 3], n // 3 + 1)

        def is_emptied(ins, u):
            ins.then_inc(emptied[UNIT_AT[u] % 3], 1)

        PASSES = {1: [0, 1], 2: [2]}

        def place_of(b, full):
            return int(b != full)

        def nth_gate(b):
            return (2, 1, 3)[b]

        block = ctx.enter_context(nc.Block())

        GAIN_ROW = (0, 4, 2, 6, 2, 6, 8)
        NORMS = [(0, b) for b in range(3)] + [(1, b) for b in range(3)] + [(2, 0), (2, 1), (3, 1), (4, 2), (5, 2), (6, 1), (6, 2)]

        def wait_normed(eng, n, b):
            eng.wait_ge(hn_ready, NORMS.index((n, b)) + 1)

        @block.sync
        def _(sp):
            sp.dma_start(h[PAD:P, 0, :], io["meta_tokens"]).then_inc(x_in, 16)
            sp.dma_start(h[:, 1:3, :], io["x"].rearrange("a (b p) d -> p (a b) d", p=P)).then_inc(x_in, 16)
            sp.dma_start(ident, io["consts"][:, 0:P]).then_inc(rows_in, 16)
            for r, source in ((0, io["attn_norm"]), (2, io["gla_norm"]), (4, io["ffn_norm"]), (8, io["final_norm"])):
                sp.dma_start(gain_rows[r:r + 2 * source.shape[0], :], source.rearrange("l (i c) -> (l i) c", i=2)).then_inc(rows_in, 16)
            sp.dma_start(con[:, P:], io["consts"][:, P:LIVE_CONSTS]).then_inc(con_in, 16)
            sources = {
                "in_qa": (io["attn_w_in"][0, :, 0:512], KC), "in_mid": (io["attn_w_in"][0, :, 512:1024], KC),
                "in_low": (io["attn_w_in"][0, :, 1024:1440], KC),
                "uq": (io["mla_w_uq"][0], Q_LORA // P), "ukv": (io["mla_w_ukv"][0], KV_LORA // P),
            }
            for i in range(2):
                c = slice(512 * i, 512 * i + 512)
                sources[f"attn_out{i}"] = (io["attn_w_out"][0, :, c], KC)
                for full in PASSES:
                    sources[f"gla_out{i}", full] = (io["gla_w_out"][0, :, c], KC)
                    sources[f"wq1_{i}", full] = (io["peer_w_query"][1, :, c], KC)
                    sources[f"gv{i}", full] = (io["gla_w_in"][0, :, 1024 + 512 * i:1536 + 512 * i], KC)
                    sources[f"gr{i}", full] = (io["gla_w_in"][0, :, 2048 + 512 * i:2560 + 512 * i], KC)
                    sources[("gq", "gk")[i], full] = (io["gla_w_in"][0, :, c], KC)

            def load_group(n):
                if n >= WSLOTS:
                    wait_filled(sp, WEIGHTS[n - WSLOTS][1])
                src, kc = sources[WEIGHTS[n][0]]
                w = src.shape[1]
                sp.dma_start(part(wring[:, n % WSLOTS, :], 0, kc, w),
                             src.rearrange("(k p) n -> p k n", p=P)).then_inc(w_in[n % WSLOTS], 16)

            load_group(0)
            sp.dma_start(acon, io["consts"][:, LIVE_CONSTS:CONST_COLS]).then_inc(small_in, 16)
            sp.dma_start(low_gain[:, 0:Q_LORA], io["mla_q_norm"].broadcast_to([P, Q_LORA])).then_inc(small_in, 16)
            sp.dma_start(low_gain[:, Q_LORA:], io["mla_kv_norm"].broadcast_to([P, KV_LORA])).then_inc(small_in, 16)
            sp.dma_start(sink[:, 0:HALF], io["swa_sinks"].broadcast_to([P, HALF])).then_inc(small_in, 16)
            for layer in range(2):
                sp.dma_start(cand[:, P * layer:P * layer + P].rearrange("n (s d) -> n s d", s=2),
                             io["peer_sub_keys"][layer].rearrange("s n d -> n s d")).then_inc(small_in, 16)
            load_group(1)
            sp.dma_start(g1w[:, :, :], io["gla_w_in"][0, :, 3072:3088].rearrange("(k p) n -> p k n", p=P)).then_inc(small_in, 16)
            sp.dma_start(wgate[0:RANK, :], io["gla_w_gate"][0]).then_inc(small_in, 16)
            sp.dma_start(wgate[RANK:RANK + 1, :], io["gla_b_gate"]).then_inc(small_in, 16)
            sp.dma_start(onorm[:, :], io["gla_out_norm"].broadcast_to([P, GV])).then_inc(small_in, 16)
            for n in range(2, len(WEIGHTS)):
                name = WEIGHTS[n][0]
                load_group(n)
                if name == "attn_out1":
                    sp.wait_ge(staged, 2 * HEADS)
                    for i in range(2):
                        sp.dma_start(wq0[:, i], io["peer_w_query"][0, :, 512 * i:512 * i + 512].rearrange("(k p) n -> p k n", p=P))\
                            .then_inc(wq0_in, 16)
            for i in range(2):
                wait_normed(sp, 6, i + 1)
                sp.dma_start(io["out"][0, P * i:P * i + P, :], hn[:, i + 1, :]).then_inc(out_done, 16)
            sp.wait_ge(out_done, 32)

        @block.gpsimd
        def _(pool):
            n_root = [0]

            def root(ap_in, ap_out, w):
                n_root[0] += 1
                pool.wait_ge(norm_ms, n_root[0])
                nc.gpsimd.tensor_tensor(ap_out, ap_in, const("neghalf")[:, 0:w], ALU.pow).then_inc(norm_rs, 1)

            for t in (low[:, 0], q_all[:, 0], k_all[:, 0], q_all[:, 1:3, 0:HALF, HD:QD], k_all[:, 1:3, 0:HALF, HD:QD]):
                nc.gpsimd.memset(t, 0.0).then_inc(rows_zero, 1)
            pool.wait_ge(con_in, 16)
            root(small[:, 0:3], small[:, 3:6], 3)
            root(small[:, 6:12], small[:, 12:18], 6)

            def stage(hh, par):
                pool.wait_ge(transposed, hh + 1)
                pool.sem_inc(go["pool"], 1)
                nc.gpsimd.tensor_copy(q_stage[:, par], q_all[:, :, hh, :]).then_inc(staged, 1)
                nc.gpsimd.tensor_copy(k_stage[:, par], k_all[:, :, hh, :]).then_inc(staged, 1)

            for kind in range(2):
                pool.wait_ge(heads_ready, kind + 1)
                with pool.Fori(kind * HALF // 2, kind * HALF // 2 + HALF // 2) as j:
                    for par in range(2):
                        stage(2 * j + par, par)
            root(small[:, 0:1], small[:, 3:4], 1)

            def gathers(g, par, layer, side=None, side_at=("v", 11)):
                pool.wait_ge(idx_ready, g + 1)
                pool.sem_inc(go["pool"], 1)
                nc.gpsimd.tensor_copy(idx_now[:, par, :], idx_next[:, :]).then_inc(idx_taken, 1)
                pool.wait_ge(idx_taken, g + 1)
                pool.sem_inc(go["pool"], 1)
                for kind, table, rows, used, landed in (("u", io["peer_u"], urow, u_used, u_in), ("v", io["peer_v"], vrow, v_used, v_in)):
                    for k in range(TOPK):
                        pool.wait_ge(used, TOPK * g + k + 1)
                        pool.sem_inc(go["pool"], 1)
                        nc.gpsimd.indirect_dma_start(
                            out=rows[:, k % RING, :], out_offset=None, in_=table.rearrange("l e d -> (l e) d"),
                            in_offset=bass.IndirectOffsetOnAxis(ap=idx_now[:, par, k:k + 1], axis=0)).then_inc(landed[k % RING], 16)
                        if side and (kind, k) == side_at:
                            side()

            def gathers_pairs(g0, n, layer):
                with pool.Fori(0, n) as j:
                    for i in range(2):
                        gathers(g0 + 2 * j + i, (g0 + i) % 2, layer)

            gathers(0, 0, 0, lambda: root(small[:, 1:2], small[:, 4:5], 1), ("u", 7))
            gathers(1, 1, 0, lambda: root(small[:, 2:3], small[:, 5:6], 1))
            gathers_pairs(2, 3, 0)
            gathers(8, 0, 0)
            for full in (1, 2):
                b = PASSES[full][0]
                sides = {0: lambda: root(small[:, b:full + 1], small[:, 3 + b:4 + full], full + 1 - b),
                         5: lambda: root(gms[:, 0:4], gms[:, 4:8], 4),
                         6: lambda: root(small[:, full:full + 1], small[:, 3 + full:4 + full], 1)}
                for t in range(8):
                    gathers(8 * full + 1 + t, (t + 1) % 2, full - 1, sides.get(t))
            gathers(25, 1, 1, lambda: root(small[:, 1:2], small[:, 4:5], 1))
            gathers_pairs(26, 3, 1)
            gathers(32, 0, 1)
            root(small[:, 2:3], small[:, 5:6], 1)

        @block.tensor
        def _(pe):
            pe.sem_inc(transposed, 2)
            pe.sem_inc(p_transposed, 2)
            pe.sem_inc(v_used, RING)

            def begin(u):
                n = UNIT_AT[u]
                if n >= 3:
                    pe.wait_ge(emptied[n % 3], n // 3)
                return UNIT_BANKS[n % 3]

            def end(ins, u):
                ins.then_inc(filled[UNIT_AT[u] % 3], 1)

            def transposes(u, sources, width=P, parts=P):
                b = begin(u)
                for i, src in enumerate(sources):
                    last = nc.tensor.transpose(bank[0:width, b * 512 + i * parts:b * 512 + (i + 1) * parts], src, ident[0:parts, 0:parts])
                end(last, u)

            def weights(name):
                n = GROUP_AT[name]
                pe.wait_ge(w_in[n % WSLOTS], 16 * (n // WSLOTS + 1))
                return wring[:, n % WSLOTS, :]

            def project(u, w, lhs, n_k, width, parts=P):
                b = begin(u)
                for k in range(n_k):
                    last = nc.tensor.matmul(bank[0:parts, b * 512:b * 512 + width], lhs(k), w(k), start=(k == 0), stop=(k == n_k - 1))
                end(last, u)

            def rows_T(b):
                return lambda k: hT[:, k, b * P:b * P + P]

            def live_T(b, first=0):
                return lambda k: hT[:, first + k, max(b * P, PAD):b * P + P]

            def tr_stream(name, n, b, src=None):
                src = src or (lambda c: hn[:, b, c * P:c * P + P])
                if n is not None:
                    wait_normed(pe, n, b)
                for half in range(2):
                    transposes((name, b, half), [src(4 * half + i) for i in range(4)])

            def group_cols(w, width):
                v = part(w, 0, KC, width)
                return lambda k: v[:, k, :]

            def spread_gains(n):
                for i in range(2):
                    u = begin(("gain", n, i))
                    pick_row = ident[0:10, GAIN_ROW[n] + i:GAIN_ROW[n] + i + 1].broadcast_to([10, P])
                    end(nc.tensor.matmul(bk(u), pick_row, gain_rows[0:10, :], start=True, stop=True), ("gain", n, i))

            pe.wait_ge(rows_in, 80)
            spread_gains(0)
            pe.wait_ge(con_in, 16)
            for b in range(NB):
                tr_stream("tr_attn", 0, b)
            for name, u, width in (("in_mid", "mid", 512), ("in_low", "low", 416), ("in_qa", "qa", 512)):
                w = weights(name)
                for b in range(NB):
                    if name == "in_mid":
                        for half in range(2):
                            wait_emptied(pe, ("tr_attn", b, half))
                    project((u, b), group_cols(w, width), live_T(b), KC, width, live_parts(b))
            pe.wait_ge(low_ready, 1)
            for b in range(NB):
                for half, cs in enumerate((range(0, 4), range(4, 5))):
                    n = live_parts(b)
                    transposes(("tr_low", b, half), [low[0:n, b, c * P:c * P + P] for c in cs], parts=n)
            w = part(weights("uq"), 0, Q_LORA // P, HALF * QD)
            for b in range(NB):
                for half in range(2):
                    wait_emptied(pe, ("tr_low", b, half))
                for half in range(2):
                    project(("uq", b, half), lambda k: w[:, k, 384 * half:384 * half + 384], live_T(b), 3, 384,
                            live_parts(b))
            def transpose_qk(hh, par):
                pe.wait_ge(staged, 2 * hh + 2)
                at_least(pe, qT_ready, hh)
                at_least(pe, kT_ready, hh)
                pe.sem_inc(go["pe"], 1)
                for i, st in enumerate((q_stage, k_stage)):
                    for b in range(NB):
                        n, a = live_parts(b), i * 512 + LIVE_AT[b]
                        last = nc.tensor.transpose(bank[0:QD, a:a + n], st[0:n, par, b, :], ident[0:n, 0:n])
                last.then_inc(transposed, 1)

            def head_scores(hh, par):
                pe.wait_ge(qT_ready, hh + 1)
                pe.wait_ge(kT_ready, hh + 1)
                at_least(pe, masked, NB * hh)
                pe.sem_inc(go["pe"], 1)
                for b in (2, 0, 1):
                    a, w = SCORE_AT[b]
                    last = nc.tensor.matmul(bk(2, a, a + w), qT_head[0:QD, par, LIVE_AT[b]:LIVE_AT[b] + P],
                                            kT_head[0:QD, par, 0:w], start=True, stop=True)
                last.then_inc(scored, 1)

            def transpose_probs(hh, par):
                pe.wait_ge(probs_ready, hh + 1)
                pe.wait_ge(pt_low, hh + 1)
                pe.wait_ge(pt_high, hh + 1)
                pe.sem_inc(go["pe"], 1)
                for at, (b, kb) in enumerate(KEY_BLOCKS):
                    a = SCORE_AT[b][0] + LIVE_AT[kb]
                    last = nc.tensor.transpose(bk(4, at * P, at * P + P), prob[:, par, a:a + P], ident)
                for b in range(NB):
                    a = SCORE_AT[b][0]
                    last = nc.tensor.transpose(bank[0:N_META, 2560 + b * P:2560 + b * P + P], prob[:, par, a:a + N_META], ident)
                last.then_inc(p_transposed, 1)

            def head_values(hh):
                pe.wait_ge(pt_low, hh + 2)
                pe.wait_ge(pt_high, hh + 2)
                pe.wait_ge(o_taken, hh + 1)
                pe.sem_inc(go["pe"], 1)
                for b in range(NB):
                    for kb in range(b + 1):
                        n = live_parts(kb)
                        at = KEY_BLOCKS.index((b, kb)) if kb else b
                        last = nc.tensor.matmul(bk(6, b * HD, b * HD + HD), probT[0:n, int(kb == 0), at * P:at * P + P],
                                                v_all[0:n, kb, hh, :], start=(kb == 0), stop=(kb == b))
                last.then_inc(pv_done, 1)

            def head_step(i, par, latent, live=range(-1, 3)):
                if 2 in live:
                    transpose_qk(i + 2, par)
                if 1 in live:
                    head_scores(i + 1, 1 - par)
                if -1 in live:
                    head_values(i - 1)
                if 0 in live:
                    transpose_probs(i, par)

            pe.wait_ge(heads_ready, 1)
            head_step(-2, 0, 0, (2,))
            w = part(weights("ukv"), 0, KV_LORA // P, D)
            for b in range(NB):
                for half in range(2):
                    project(("ukv", b, half), lambda k: w[:, k, 512 * half:512 * half + 512],
                            live_T(b, 3), 2, 512, live_parts(b))

            for layer in range(2):
                transposes(("sk", layer), [cand[:, layer * P:layer * P + P]])
            head_step(-1, 1, 0, (1, 2))
            pipeline(pe, head_step)

            pe.wait_ge(o_taken, HEADS + 1)
            for half in range(2):
                transposes(("tr_o", 0, half), [hn[0:N_META, 0, (4 * half + i) * P:(4 * half + i) * P + P] for i in range(4)],
                           parts=N_META)

            def out_project(b, i):
                project(("ao", b, i), group_cols(weights(f"attn_out{i}"), 512), rows_T(b), KC, 512)

            def expert_queries(b):
                tr_stream("tr_ffn0", 1, b)
                if b == 2:
                    spread_gains(2)
                for i in range(2):
                    wait_emptied(pe, ("tr_ffn0", b, i))
                pe.wait_ge(wq0_in, 32)
                if b == 0:
                    for i in range(2):
                        u = begin(("pq0_rows", i))
                        for k in range(KC):
                            last = nc.tensor.matmul(bank[0:N_META, u * 512:u * 512 + 512], hT[:, k, PAD:P], wq0[:, i, k, :],
                                                    start=(k == 0), stop=(k == KC - 1))
                        end(last, ("pq0_rows", i))
                    for i in range(2):
                        wait_emptied(pe, ("pq0_rows", i))
                    u = begin(("pq0_T",))
                    for x in range(PH):
                        last = nc.tensor.transpose(bk(u, x * N_META, x * N_META + N_META), q_rows[0:N_META, x * P:x * P + P],
                                                   ident[0:N_META, 0:N_META])
                    end(last, ("pq0_T",))
                    return
                for x in range(PH):
                    u = begin(("pq0", b, x))
                    for k in range(KC):
                        last = nc.tensor.matmul(bk(u, 0, P), wq0[:, x // 4, k, (x % 4) * P:(x % 4) * P + P],
                                                hT[:, k, b * P:b * P + P], start=(k == 0), stop=(k == KC - 1))
                    end(last, ("pq0", b, x))

            for half in range(2):
                wait_emptied(pe, ("tr_o", 0, half))
            out_project(0, 0)
            out_project(0, 1)
            spread_gains(1)
            for b in (1, 2):
                tr_stream("tr_o", None, b)
            expert_queries(0)

            def prepare(g, layer, b):
                pe.wait_ge(pick_ready, g + 1)
                pe.wait_ge(u_used, RING + TOPK * g)
                pe.sem_inc(go["pe"], 1)
                pe.wait_ge(qnow_ready, g + 1)
                pe.sem_inc(go["pe"], 1)
                nc.tensor.matmul(score, q_now[:, :], skT[:, layer, :], start=True, stop=True).then_inc(scores_ready, 1)
                for i in range(2):
                    last = nc.tensor.matmul(bk(i), pick_now[:, :], hn[:, b, 512 * i:512 * i + 512], start=True, stop=True)
                last.then_inc(xrep_ready, 1)

            def mix(g):
                for k in range(TOPK):
                    pe.wait_ge(v_in[k % RING], 16 * (2 * g + k // RING + 1))
                    pe.wait_ge(placed, TOPK * g + k + 1)
                    if k == 0:
                        at_least(pe, y_added, g)
                    pe.sem_inc(go["pe"], 1)
                    for i in range(2):
                        last = nc.tensor.matmul(yacc[:, 512 * i:512 * i + 512], wplace[:, k, :],
                                                vrow[:, k % RING, 512 * i:512 * i + 512], start=(k == 0), stop=(k == TOPK - 1))
                    last.then_inc(v_used, 1)

            def gla(t, full):
                rest = PASSES[full][:-1]
                every = [full] + rest

                def gproject(u, name, b):
                    project(u, group_cols(weights((name, full)), 512), rows_T(b), KC, 512)

                def states(u, i, place, c):
                    rs = slice(c * CHUNK, c * CHUNK + CHUNK)
                    ub = begin(u)
                    for x in (2 * i, 2 * i + 1):
                        last = nc.tensor.matmul(bk(ub, (x % 2) * GV, (x % 2) * GV + GV), gk[rs, place, x * GK:x * GK + GK],
                                                gv[rs, place, x * GV:x * GV + GV], start=True, stop=True)
                    end(last, u)

                if t == 0:
                    for b in every:
                        tr_stream("tr_gla", 2 if full == 1 else 4, b)
                    spread_gains(3 if full == 1 else 5)
                    for b in every:
                        for i in range(2):
                            wait_emptied(pe, ("tr_gla", b, i))
                        project(("g1", b), lambda k: g1w[:, k, :], rows_T(b), KC, RANK)
                    gproject(("gk", full), "gk", full)
                    for b in every:
                        wait_emptied(pe, ("g1", b))
                        transposes(("g1T", b), [g1[:, place_of(b, full), :]], width=RANK)
                    for b in rest:
                        gproject(("gk", b), "gk", b)
                    for b in every:
                        wait_emptied(pe, ("g1T", b))
                        u = begin(("la", b))
                        end(nc.tensor.matmul(bk(u), g1T[0:RANK + 1, place_of(b, full), :], wgate[0:RANK + 1, :], start=True, stop=True),
                            ("la", b))
                elif t == 1:
                    pe.wait_ge(decay_ready, full + 1)
                    for b in every:
                        u = begin(("after", b))
                        end(nc.tensor.matmul(bk(u), const("after"), la[:, place_of(b, full), :], start=True, stop=True), ("after", b))
                    u = begin(("cum", full))
                    end(nc.tensor.matmul(bk(u), const("tri"), la[:, 0, :], start=True, stop=True), ("cum", full))
                    u = begin(("decay", full))
                    for x in range(GH):
                        last = nc.tensor.matmul(bk(u, 2 * x, 2 * x + 2), la[:, 0, x * GK:x * GK + GK], const("chunks"), start=True, stop=True)
                    end(last, ("decay", full))
                    gproject(("gq", full), "gq", full)
                    gproject(("gv", full, 0), "gv0", full)
                elif t == 2:
                    gproject(("gv", full, 1), "gv1", full)
                    pe.wait_ge(kd_ready, full)
                    transposes(("tr_qd", full), [gq[:, x * GK:x * GK + GK] for x in range(GH)])
                    transposes(("tr_kd", full), [kd[:, x * GK:x * GK + GK] for x in range(GH)])
                    wait_emptied(pe, ("tr_qd", full))
                    wait_emptied(pe, ("tr_kd", full))
                    u = begin(("att", full))
                    for x in range(GH):
                        c = slice(x * GK, x * GK + GK)
                        last = nc.tensor.matmul(bk(u, x * GK, x * GK + GK), kdT[:, c], qdT[:, c], start=True, stop=True)
                    end(last, ("att", full))
                    for b in rest:
                        gproject(("gv", b, 0), "gv0", b)
                elif t == 3:
                    for b in rest:
                        gproject(("gv", b, 1), "gv1", b)
                    gproject(("gr", full, 0), "gr0", full)
                    pe.wait_ge(kend_ready, full + 1)
                    for b in rest:
                        for i in range(2):
                            wait_emptied(pe, ("gv", b, i))
                            states(("st", b, i), i, 1, 1)
                    for i in range(2):
                        wait_emptied(pe, ("gv", full, i))
                        states(("u0", full, i), i, 0, 0)
                elif t == 4:
                    gproject(("gr", full, 1), "gr1", full)
                    pe.wait_ge(state1_ready, full)
                    for i in range(2):
                        u = ("o", full, i)
                        ub = begin(u)
                        for x in (2 * i, 2 * i + 1):
                            a = ub * 512 + (x % 2) * GV
                            nc.tensor.matmul(bank[:, a:a + GV], atm[:, x * GK:x * GK + GK], gv[:, 0, x * GV:x * GV + GV],
                                             start=True, stop=False)
                            for c, st in enumerate((state0, state1)):
                                last = nc.tensor.matmul(bank[c * CHUNK:c * CHUNK + CHUNK, a:a + GV],
                                                        qdT[:, x * GK + c * CHUNK:x * GK + c * CHUNK + CHUNK],
                                                        st[:, x, :], start=False, stop=True)
                        end(last, u)
                    for i in range(2):
                        states(("u1", full, i), i, 0, 1)
                elif t == 5:
                    pe.wait_ge(og_ready, full)
                    for i in range(2):
                        transposes(("tr_go", full, i), [og[:, (4 * i + x) * P:(4 * i + x) * P + P] for x in range(4)])
                    for i in range(2):
                        wait_emptied(pe, ("tr_go", full, i))
                    for i in range(2):
                        gproject(("go", full, i), f"gla_out{i}", full)
                elif t == 6:
                    tr_stream("tr_ffn1", 3 if full == 1 else 5, full)
                    spread_gains(4 if full == 1 else 6)
                    for i in range(2):
                        wait_emptied(pe, ("tr_ffn1", full, i))
                    for i in range(2):
                        w = part(weights((f"wq1_{i}", full)), 0, KC, 512)
                        for x in range(4):
                            un = ("pq1", full, 4 * i + x)
                            b = begin(un)
                            for k in range(KC):
                                last = nc.tensor.matmul(bk(b, 0, P), w[:, k, x * P:x * P + P], hT[:, k, full * P:full * P + P],
                                                        start=(k == 0), stop=(k == KC - 1))
                            end(last, un)

            prepare(0, 0, 0)
            for b in (1, 2):
                for half in range(2):
                    wait_emptied(pe, ("tr_o", b, half))
            out_project(1, 0)
            out_project(1, 1)
            expert_queries(1)
            prepare(1, 0, 1)
            mix(0)
            out_project(2, 0)
            out_project(2, 1)
            prepare(2, 0, 1)
            mix(1)
            expert_queries(2)
            with pe.Fori(2, 8) as g:
                prepare(g + 1, 0, 1)
                mix(g)
            prepare(9, 0, 2)
            mix(8)
            for full in (1, 2):
                for t in range(8):
                    g = 8 * full + 1 + t
                    prepare(g + 1, *((full - 1, 2 if full == 1 else 1) if t < 7 else (1, full)))
                    mix(g)
                    gla(t, full)
            with pe.Fori(25, 32) as g:
                prepare(g + 1, 1, 2)
                mix(g)
            mix(32)

        @block.scalar
        def _(act):
            def copy_unit(u, dst, src=None, width=512, parts=P):
                b = unit_bank(u)
                wait_filled(act, u)
                is_emptied(nc.scalar.activation(dst, bank[0:parts, b * 512:b * 512 + width] if src is None else src(b),
                                                ACT.Copy), u)

            def take_T(name, b, chunks=((0, 4), (4, 8)), tokens=P):
                for half, (c0, c1) in enumerate(chunks):
                    n = c1 - c0
                    copy_unit((name, b, half), hT[:, c0:c1, b * P + P - tokens:b * P + P],
                              lambda u: bk(u, 0, n * tokens).rearrange("p (c n) -> p c n", c=n))

            def take_gains(n):
                if n:
                    act.wait_ge(hn_ready, NORMS.index(next(x for x in NORMS if x[0] == n)))
                for i in range(2):
                    u = ("gain", n, i)
                    copy_unit(u, gain[:, 512 * i:512 * i + 512])

            act.sem_inc(pt_low, 1)
            take_gains(0)
            for b in range(NB):
                take_T("tr_attn", b)
            for b in range(NB):
                take_T("tr_low", b, ((0, 4), (4, 5)), live_parts(b))

            act.wait_ge(sk_zero, 1)
            for layer in range(2):
                u = ("sk", layer)
                wait_filled(act, u)
                b = unit_bank(u)
                nc.scalar.activation(skT[0:64, layer, 0:P], bank[0:64, b * 512:b * 512 + P], ACT.Copy)
                is_emptied(nc.scalar.activation(skT[64:P, layer, P:2 * P], bank[64:P, b * 512:b * 512 + P], ACT.Copy), u)

            def take_qT(hh, par):
                act.wait_ge(transposed, hh + 3)
                nc.scalar.activation(qT_head[0:QD, par, :], bank[0:QD, 0:LIVE], ACT.Copy).then_inc(qT_ready, 1)

            def take_probT(hh):
                act.wait_ge(p_transposed, hh + 3)
                nc.scalar.activation(probT[:, 0], bk(4, 0, NB * P), ACT.Copy).then_inc(pt_low, 1)

            def exps(hh, par):
                act.wait_ge(nm_ready, hh + 1)
                act.sem_inc(go["act"], 1)
                nm = stat[:, par, 3:6]
                for b in range(NB):
                    a, w = SCORE_AT[b]
                    nc.scalar.activation(prob[:, par, a:a + w], prob[:, par, a:a + w], ACT.Exp, bias=nm[:, b:b + 1],
                                         accum_out=stat[:, par, 6 + b:7 + b])
                nc.scalar.activation(stat[:, par, 9:12], nm, ACT.Exp, bias=sink[:, bass.ds(hh, 1)]).then_inc(probs_ready, 1)

            def head_step(i, par, latent, live=range(-1, 3)):
                if 2 in live:
                    take_qT(i + 2, par)
                if 1 in live:
                    exps(i + 1, 1 - par)
                if 0 in live:
                    take_probT(i)

            head_step(-2, 0, 0, (2,))
            head_step(-1, 1, 0, (1, 2))
            pipeline(act, head_step)
            for b in range(NB):
                take_T("tr_o", b, tokens=live_parts(b))
                if b == 0:
                    take_gains(1)

            def take_queries(b):
                take_T("tr_ffn0", b)
                if b == 2:
                    take_gains(2)
                if b == 0:
                    for i in range(2):
                        copy_unit(("pq0_rows", i), q_rows[0:N_META, 512 * i:512 * i + 512], parts=N_META)
                    copy_unit(("pq0_T",), qT[:, 0:N_META * PH].rearrange("p (t h) -> p h t", h=PH),
                              lambda u: bk(u, 0, P).rearrange("p (h t) -> p h t", h=PH))
                    wait_emptied(act, ("pq0_T",))
                    return
                t0 = (b * P - PAD) * PH
                for x in range(PH):
                    copy_unit(("pq0", b, x), qT[:, t0:t0 + P * PH].rearrange("p (t h) -> p t h", h=PH)[:, :, x], width=P)
                wait_emptied(act, ("pq0", b, PH - 1))

            place_all = const("place")

            def prepare(g, tile):
                at_least(act, scores_ready, g)
                act.sem_inc(go["act"], 1)
                nc.scalar.activation(q_now[:, :], qT[:, bass.ds(P * tile, P)], ACT.Copy).then_inc(qnow_ready, 1)

            def gate_exps(g):
                act.wait_ge(best_ready, g + 1)
                nc.scalar.activation(gate_e[:, :], best[:, :], ACT.Exp, bias=z[:, 0:1], accum_out=z[:, 1:2]).then_inc(gate_exp, 1)

            def mix(g, j):
                act.wait_ge(gelu_in, g + 1)
                nc.scalar.activation(gl[:, 1, :], gl[:, 0, :], ACT.Tanh, scale=GELU_C).then_inc(gelu_tanh, 1)
                act.wait_ge(wgt_ready, g + 1)
                act.wait_ge(v_used, RING + TOPK * g)
                act.sem_inc(go["act"], 1)
                for k in range(TOPK):
                    nc.scalar.activation(wplace[:, k, :], place_all[:, bass.ds(112 - TT * j, P)], ACT.Copy,
                                         scale=wgt[:, k:k + 1]).then_inc(placed, 1)

            def gla(t, full):
                rest = PASSES[full][:-1]
                every = [full] + rest

                def take_g(u, dst, scale=1.0):
                    wait_filled(act, u)
                    is_emptied(nc.scalar.activation(dst, bk(unit_bank(u)), ACT.Copy, scale=scale), u)

                if t == 0:
                    for b in every:
                        take_T("tr_gla", b)
                    take_gains(3 if full == 1 else 5)
                    for b in every:
                        copy_unit(("g1", b), g1[:, place_of(b, full), :], width=RANK)
                    take_g(("gk", full), gk[:, 0, :])
                    for b in every:
                        copy_unit(("g1T", b), g1T[0:RANK, place_of(b, full), :], width=P, parts=RANK)
                    for b in rest:
                        take_g(("gk", b), gk[:, 1, :])
                elif t == 1:
                    for b in every:
                        e = ex[:, place_of(b, full), :]
                        act.wait_ge(minus_abs, nth_gate(b))
                        nc.scalar.activation(e, e, ACT.Exp).then_inc(gate_exp1, 1)
                        act.wait_ge(gate_exp1, nth_gate(b))
                        nc.scalar.activation(e, e, ACT.Ln, bias=1.0).then_inc(gate_log, 1)
                    for b in every:
                        u = ("after", b)
                        wait_filled(act, u)
                        is_emptied(nc.scalar.activation(ex[:, place_of(b, full), :], bk(unit_bank(u)), ACT.Exp), u)
                    u = ("cum", full)
                    wait_filled(act, u)
                    nc.scalar.activation(qdT, bk(unit_bank(u)), ACT.Exp)
                    is_emptied(nc.scalar.activation(kdT, bk(unit_bank(u)), ACT.Exp, scale=-1.0), u)
                    u = ("decay", full)
                    wait_filled(act, u)
                    is_emptied(nc.scalar.activation(dec, bk(unit_bank(u), 0, 2 * GH), ACT.Exp), u)
                    take_g(("gq", full), gq, GK ** -0.5)
                    take_g(("gv", full, 0), gv[:, 0, 0:512])
                elif t == 2:
                    take_g(("gv", full, 1), gv[:, 0, 512:1024])
                    take_g(("tr_qd", full), qdT)
                    take_g(("tr_kd", full), kdT)
                    for b in rest:
                        take_g(("gv", b, 0), gv[:, 1, 0:512])
                elif t == 3:
                    for b in rest:
                        take_g(("gv", b, 1), gv[:, 1, 512:1024])
                    take_g(("gr", full, 0), gr[:, 0:512], 0.5)
                    for b in rest:
                        for i in range(2):
                            take_g(("st", b, i), state0[:, 2 * i:2 * i + 2, :].rearrange("p h n -> p (h n)"))
                elif t == 4:
                    take_g(("gr", full, 1), gr[:, 512:1024], 0.5)
                    for i in range(2):
                        take_g(("o", full, i), og[:, 512 * i:512 * i + 512])
                elif t == 5:
                    act.wait_ge(norm_ms, 7 if full == 1 else 10)
                    wait_emptied(act, ("gr", full, 0))
                    wait_emptied(act, ("gr", full, 1))
                    nc.scalar.activation(sq, gr, ACT.Tanh).then_inc(silu_tanh, 1)
                    take_T("tr_go", full)
                elif t == 6:
                    take_T("tr_ffn1", full)
                    take_gains(4 if full == 1 else 6)
                    t0 = (full * P - PAD) * PH
                    for x in range(PH):
                        copy_unit(("pq1", full, x), qT[:, t0:t0 + P * PH].rearrange("p (t h) -> p t h", h=PH)[:, :, x], width=P)

            take_queries(0)
            prepare(0, 0)
            gate_exps(0)
            take_queries(1)
            prepare(1, 1)
            mix(0, 7)
            gate_exps(1)
            prepare(2, 2)
            mix(1, 0)
            gate_exps(2)
            take_queries(2)
            with act.Fori(2, 8) as g:
                prepare(g + 1, g + 1)
                mix(g, g - 1)
                gate_exps(g + 1)
            prepare(9, 9)
            mix(8, 7)
            gate_exps(9)
            for full in (1, 2):
                for t in range(8):
                    g = 8 * full + 1 + t
                    if t == 7:
                        wait_emptied(act, ("pq1", full, PH - 1))
                    prepare(g + 1, g + 1 if g + 1 < 17 else g + 1 - 16)
                    mix(g, t)
                    gate_exps(g + 1)
                    gla(t, full)
            with act.Fori(25, 32) as g:
                prepare(g + 1, g - 15)
                mix(g, g - 25)
                gate_exps(g + 1)
            mix(32, 7)

        @block.vector
        def _(dve):
            v = nc.vector
            steps = Steps(dve, d_step)
            n_norm = [0]

            def unit_ap(u, a=0, b=512):
                wait_filled(dve, u)
                return bk(unit_bank(u), a, b)

            def squares(src, junk, out):
                steps.did(v.tensor_tensor_reduce(out=junk, in0=src, in1=src, scale=1.0, scalar=0.0, op0=ALU.mult,
                                                 op1=ALU.add, accum_out=out))

            def mean(ap, width):
                steps.did(v.tensor_scalar(ap, ap, 1.0 / width, EPS, ALU.mult, ALU.add))

            def roots():
                n_norm[0] += 1
                steps.settle()
                dve.sem_inc(norm_ms, 1)
                dve.wait_ge(norm_rs, n_norm[0])

            def norm(n, blocks):
                for b in blocks:
                    squares(h[:, b, :], hn[:, b, :], small[:, b:b + 1])
                steps.settle()
                mean(small[:, blocks[0]:blocks[-1] + 1], D)
                roots()
                for i in range(2):
                    wait_emptied(dve, ("gain", n, i))
                for b in blocks:
                    v.scalar_tensor_tensor(out=hn[:, b, :], in0=h[:, b, :], scalar=small[:, 3 + b:4 + b], in1=gain[:, :],
                                           op0=ALU.mult, op1=ALU.mult).then_inc(hn_ready, 1)

            dve.sem_inc(pt_high, 1)
            dve.sem_inc(o_taken, 1)
            dve.sem_inc(u_used, RING)
            steps.did(v.memset(g1T[0:32, :, :], 1.0))
            steps.did(v.memset(h[0:PAD, 0, :], 0.0))
            v.memset(skT[:, :, :], 0.0).then_inc(sk_zero, 1)
            dve.wait_ge(x_in, 32)
            steps.settle()
            norm(0, range(NB))
            dve.wait_ge(rows_zero, 5)
            for b in range(NB):
                u = ("mid", b)
                src = unit_ap(u)
                n = live_parts(b)
                for to, a in ((k_all, 0), (v_all, P)):
                    steps.did(v.tensor_copy(to[0:n, b, 0:HALF, 0:HD].rearrange("p (g r) d -> p g r d", g=2),
                                            src[0:n, a:a + P].rearrange("p (g d) -> p g d", g=2).unsqueeze(2)
                                            .broadcast_to([n, 2, 4, HD])))
                is_emptied(v.tensor_copy(low[0:n, b, 0:256], src[0:n, 256:512]), u)
            for b in range(NB):
                u = ("low", b)
                n = live_parts(b)
                is_emptied(v.tensor_copy(low[0:n, b, 256:672], unit_ap(u, 0, 416)[0:n]), u)
            dve.wait_ge(small_in, SMALL_LOADS * 16)
            steps.did(v.memset(sink[:, HALF:HEADS], NEG))
            for b in range(NB):
                wait_emptied(dve, ("mid", b))
                wait_emptied(dve, ("low", b))
                squares(low[:, b, 0:Q_LORA], rt[:, 0:Q_LORA], small[:, 6 + b:7 + b])
                steps.settle()
                squares(low[:, b, Q_LORA:Q_LORA + KV_LORA], rt[:, 0:KV_LORA], small[:, 9 + b:10 + b])
                steps.settle()
            mean(small[:, 6:9], Q_LORA)
            mean(small[:, 9:12], KV_LORA)
            roots()
            for b in range(NB):
                for a, w, s in ((0, Q_LORA, 12), (Q_LORA, KV_LORA, 15)):
                    ap = low[:, b, a:a + w]
                    steps.did(v.scalar_tensor_tensor(out=ap, in0=ap, scalar=small[:, s + b:s + b + 1], in1=low_gain[:, a:a + w],
                                                     op0=ALU.mult, op1=ALU.mult))
            steps.settle()
            dve.sem_inc(low_ready, 1)

            def rotate(x1, x2, t, shape, dst1, dst2, wide):
                cos, sin = (acst(n).rearrange("p (b r) -> p b r", b=NB) for n in ("cos", "sin"))
                if len(shape) == 4:
                    cos, sin = (a.unsqueeze(2).broadcast_to(shape) for a in (cos, sin))
                for i, (x, y) in enumerate(((x1, cos), (x2, sin), (x2, cos), (x1, sin))):
                    steps.did(v.tensor_tensor(t[i], x, y, ALU.mult))
                steps.settle()
                steps.did(v.tensor_tensor(dst1, wide(t[0]), wide(t[1]), ALU.subtract))
                steps.did(v.tensor_tensor(dst2, wide(t[2]), wide(t[3]), ALU.add))
                steps.settle()

            n = NB * ROPE
            t = [rt[:, i * n:(i + 1) * n].rearrange("p (b r) -> p b r", b=NB) for i in range(4)]
            rotate(low[:, :, 640:656], low[:, :, 656:672], t, [P, NB, ROPE], k_mla[:, :, :, 64:80], k_mla[:, :, :, 80:96],
                   lambda a: a.unsqueeze(2).broadcast_to([P, NB, HALF, ROPE]))
            for b in range(NB):
                u = ("qa", b)
                n = live_parts(b)
                is_emptied(v.tensor_scalar(q_swa[0:n, b], unit_ap(u)[0:n].rearrange("p (h d) -> p h d", h=HALF), HD ** -0.5, None,
                                           ALU.mult), u)
            for b in range(NB):
                wait_emptied(dve, ("qa", b))
            dve.sem_inc(heads_ready, 1)
            steps.did(v.memset(hT[:, :, 0:PAD], 0.0))
            for b in range(NB):
                for i in range(2):
                    u = ("uq", b, i)
                    n = live_parts(b)
                    is_emptied(v.tensor_scalar(q_mla[0:n, b, 4 * i:4 * i + 4, :].rearrange("p h d -> p (h d)"),
                                               unit_ap(u, 0, 384)[0:n], QD ** -0.5, None, ALU.mult), u)
            for b in range(NB):
                for i in range(2):
                    wait_emptied(dve, ("uq", b, i))

            def take_kT(hh, par):
                dve.wait_ge(transposed, hh + 3)
                v.tensor_copy(kT_head[0:QD, par, :], bank[0:QD, 512:512 + LIVE]).then_inc(kT_ready, 1)

            def mask_scores(hh, par, latent):
                dve.wait_ge(p_transposed, hh + 1)
                dve.wait_ge(scored, hh + 1)
                dve.sem_inc(go["dve"], 1)
                for b in range(NB):
                    a, w = SCORE_AT[b]
                    v.tensor_tensor_reduce(out=prob[:, par, a:a + w], in0=bk(2, a, a + w),
                                           in1=masks[:, latent * SCORES + a:latent * SCORES + a + w], scale=1.0, scalar=-3e38, op0=ALU.add,
                                           op1=ALU.max, accum_out=stat[:, par, b:b + 1]).then_inc(masked, 1)
                dve.wait_ge(masked, NB * hh + NB)
                v.tensor_scalar(stat[:, par, 3:6], stat[:, par, 0:3], sink[:, bass.ds(hh, 1)], -1.0, ALU.max, ALU.mult)\
                    .then_inc(nm_ready, 1)

            def denominators(hh, par):
                dve.wait_ge(probs_ready, hh + 1)
                at_least(dve, o_taken, hh)
                dve.sem_inc(go["dve"], 1)
                v.tensor_tensor(stat[:, par, 12:15], stat[:, par, 6:9], stat[:, par, 9:12], ALU.add).then_inc(den_ready, 1)
                dve.wait_ge(den_ready, 2 * hh + 1)
                v.reciprocal(stat[:, par, 12:15], stat[:, par, 12:15]).then_inc(den_ready, 1)

            def take_values(hh, par):
                dve.wait_ge(den_ready, 2 * hh + 2)
                dve.wait_ge(pv_done, hh + 1)
                dve.sem_inc(go["dve"], 1)
                v.tensor_tensor(hn[:, :, bass.ds(hh * HD, HD)], bk(6, 0, NB * HD).rearrange("p (b d) -> p b d", b=NB),
                                stat[:, par, 12:15].unsqueeze(2).broadcast_to([P, NB, HD]), ALU.mult).then_inc(o_taken, 1)

            def take_probT(hh):
                dve.wait_ge(p_transposed, hh + 3)
                v.tensor_copy(probT[0:N_META, 1], bank[0:N_META, 2560:2560 + NB * P]).then_inc(pt_high, 1)

            def head_step(i, par, latent, live=range(-1, 3)):
                if 2 in live:
                    take_kT(i + 2, par)
                if 1 in live:
                    mask_scores(i + 1, 1 - par, latent)
                if 0 in live:
                    denominators(i, par)
                if -1 in live:
                    take_values(i - 1, 1 - par)
                if 0 in live:
                    take_probT(i)

            head_step(-2, 0, 0, (2,))
            n = NB * HALF * ROPE
            t = [rt[:, i * n:(i + 1) * n].rearrange("p (b h r) -> p b h r", b=NB, h=HALF) for i in range(4)]
            rotate(q_mla[:, :, :, 64:80], q_mla[:, :, :, 80:96], t, [P, NB, HALF, ROPE], q_mla[:, :, :, 64:80],
                   q_mla[:, :, :, 80:96], lambda a: a)
            for b in range(NB):
                for i in range(2):
                    u = ("ukv", b, i)
                    n = live_parts(b)
                    src = unit_ap(u)[0:n].rearrange("p (h d) -> p h d", h=4)
                    steps.did(v.tensor_copy(k_mla[0:n, b, 4 * i:4 * i + 4, 0:HD], src[:, :, 0:HD]))
                    is_emptied(v.tensor_copy(v_all[0:n, b, HALF + 4 * i:HALF + 4 * i + 4, :], src[:, :, HD:2 * HD]), u)
            for b in range(NB):
                for i in range(2):
                    wait_emptied(dve, ("ukv", b, i))
            dve.sem_inc(heads_ready, 1)
            head_step(-1, 1, 0, (1, 2))
            pipeline(dve, head_step)

            def add_to_h(u, b, i):
                hs = h[:, b, 512 * i:512 * i + 512]
                is_emptied(v.tensor_tensor(hs, hs, unit_ap(u), ALU.add), u)

            for i in range(2):
                add_to_h(("ao", 0, i), 0, i)
            for i in range(2):
                wait_emptied(dve, ("ao", 0, i))
            norm(1, [0])

            def ready_for_queries(b):
                for i in range(2):
                    add_to_h(("ao", b, i), b, i)
                for i in range(2):
                    wait_emptied(dve, ("ao", b, i))
                norm(1, [b])

            def best16(vals, rest_ap, values, indices, topk):
                topk.chain(v.max(values[:, 0:8], vals))
                topk.did(v.max_index(indices[:, 0:8], values[:, 0:8], vals))
                topk.chain(v.match_replace(rest_ap, values[:, 0:8], vals, -3e38))
                topk.chain(v.max(values[:, 8:16], rest_ap))
                topk.chain(v.max_index(indices[:, 8:16], values[:, 8:16], rest_ap))

            topk = Steps(dve, topk_step)
            mixs = Steps(dve, mix_step)

            def choose(g, layer):
                dve.wait_ge(scores_ready, g + 1)
                at_least(dve, idx_taken, g)
                at_least(dve, gate_exp, g)
                dve.sem_inc(go["dve"], 1)
                topk.restart()
                for s in range(2):
                    best16(score[:, s * P:s * P + P], rest[:, s, :], top[:, s, :], top_i[:, s, :], topk)
                topk.did(v.tensor_copy(top_f[:, :, :], top_i[:, :, :]))
                pair = cand[:, :].rearrange("p (a b) -> p a b", a=TOPK)
                topk.chain(v.tensor_tensor(pair, top[:, 0, :].unsqueeze(2).broadcast_to([P, TOPK, TOPK]),
                                           top[:, 1, :].unsqueeze(1).broadcast_to([P, TOPK, TOPK]), ALU.add))
                best16(cand[:, :], cand_rest[:, :], best, best_j, topk)
                topk.did(v.tensor_scalar(digit[:, 0, :], best_j[:, :], 4, None, ALU.logical_shift_right))
                topk.did(v.tensor_scalar(digit[:, 1, :], best_j[:, :], 15, None, ALU.bitwise_and))
                topk.chain(v.tensor_scalar(z[:, 0:1], best[:, 0:1], -1.0, None, ALU.mult))
                dve.sem_inc(best_ready, 1)
                topk.chain(v.tensor_copy(digit_f[:, :, :], digit[:, :, :]))
                topk.chain(v.tensor_tensor(onehot[:, :, :], digit_f[:, :, :].rearrange("p s k -> p (s k)").unsqueeze(2)
                                           .broadcast_to([P, 2 * TOPK, TOPK]),
                                           const("iota").unsqueeze(1).broadcast_to([P, 2 * TOPK, TOPK]), ALU.is_equal))
                one = onehot[:, :, :].rearrange("p (s k) a -> p s k a", s=2)
                topk.chain(v.tensor_tensor(one, one, top_f[:, :, :].unsqueeze(2).broadcast_to([P, 2, TOPK, TOPK]), ALU.mult))
                topk.chain(v.tensor_reduce(out=picked[:, :, :].rearrange("p s k -> p (s k)"), in_=onehot[:, :, :], axis=AX, op=ALU.add))
                topk.chain(v.tensor_scalar(picked[:, 0, :], picked[:, 0, :], float(N_KEYS), float(layer * EXPERTS), ALU.mult, ALU.add))
                topk.chain(v.tensor_tensor(idx_next[:, :], picked[:, 0, :], picked[:, 1, :], ALU.add))
                dve.sem_inc(idx_ready, 1)

            def pick(g, j):
                at_least(dve, xrep_ready, g)
                v.tensor_scalar(pick_now[:, :], const("row_token"), const("token")[:, bass.ds(j, 1)], None, ALU.is_equal)\
                    .then_inc(pick_ready, 1)

            def dot(g, slots):
                dve.wait_ge(xrep_ready, g + 1)
                dve.sem_inc(go["dve"], 1)
                for k in slots:
                    dve.wait_ge(u_in[k % RING], 16 * (2 * g + k // RING + 1))
                    v.tensor_tensor_reduce(out=urow[:, k % RING, :], in0=urow[:, k % RING, :], in1=xrep, scale=1.0, scalar=0.0,
                                           op0=ALU.mult, op1=ALU.add, accum_out=dots[:, k:k + 1]).then_inc(u_used, 1)

            def weigh(g):
                dve.wait_ge(u_used, RING + TOPK * (g + 1))
                dve.wait_ge(gate_exp, g + 1)
                dve.sem_inc(go["dve"], 1)
                mixs.restart()
                a = gl[:, 0, :]
                mixs.did(v.reciprocal(z[:, 2:3], z[:, 1:2]))
                mixs.chain(v.tensor_tensor(a, dots[:, :], dots[:, :], ALU.mult))
                mixs.chain(v.tensor_scalar(a, a, 0.044715, 1.0, ALU.mult, ALU.add))
                mixs.chain(v.tensor_tensor(a, a, dots[:, :], ALU.mult))
                dve.sem_inc(gelu_in, 1)
                mixs.chain(v.scalar_tensor_tensor(out=gate[:, :], in0=gate_e[:, :], scalar=z[:, 2:3], in1=dots[:, :],
                                                  op0=ALU.mult, op1=ALU.mult))
                mixs.chain(v.tensor_scalar(gate[:, :], gate[:, :], 0.5, None, ALU.mult))
                dve.wait_ge(gelu_tanh, g + 1)
                dve.sem_inc(go["dve"], 1)
                mixs.chain(v.scalar_tensor_tensor(out=wgt[:, :], in0=gl[:, 1, :], scalar=1.0, in1=gate[:, :], op0=ALU.add, op1=ALU.mult))
                dve.sem_inc(wgt_ready, 1)

            def add_experts(g, b):
                dve.wait_ge(v_used, RING + TOPK * (g + 1))
                v.tensor_tensor(h[:, b, :], h[:, b, :], yacc, ALU.add).then_inc(y_added, 1)
                dve.wait_ge(y_added, g + 1)
                dve.sem_inc(go["dve"], 1)

            FIRST, SECOND = range(0, TOPK // 2), range(TOPK // 2, TOPK)

            def tile(g, b, layer, j, side=None):
                pick(g + 1, j)
                dot(g, SECOND)
                weigh(g)
                choose(g + 1, layer)
                if side:
                    side()
                dot(g + 1, FIRST)
                add_experts(g, b)

            def gla(t, full):
                rest = PASSES[full][:-1]
                every = [full] + rest
                if t == 0:
                    norm(2 if full == 1 else 4, PASSES[full])
                elif t == 1:
                    for b in every:
                        u = ("la", b)
                        src = unit_ap(u)
                        l, e = la[:, place_of(b, full), :], ex[:, place_of(b, full), :]
                        steps.did(v.tensor_scalar(l, src, 0.0, 1.0 / TAU, ALU.min, ALU.mult))
                        is_emptied(v.tensor_scalar(e, src, 0.0, None, ALU.max), u)
                        steps.settle()
                        wait_emptied(dve, u)
                        v.scalar_tensor_tensor(out=e, in0=l, scalar=TAU, in1=e, op0=ALU.mult, op1=ALU.subtract).then_inc(minus_abs, 1)
                    for b in every:
                        l, e = la[:, place_of(b, full), :], ex[:, place_of(b, full), :]
                        dve.wait_ge(gate_log, nth_gate(b))
                        v.scalar_tensor_tensor(out=l, in0=e, scalar=-1.0 / TAU, in1=l, op0=ALU.mult, op1=ALU.add).then_inc(decay_ready, 1)
                elif t == 2:
                    wait_emptied(dve, ("decay", full))
                    wait_emptied(dve, ("gq", full))
                    steps.chain(v.tensor_tensor(gq, gq, qdT, ALU.mult))
                    v.tensor_tensor(kd, gk[:, 0, :], kdT, ALU.mult).then_inc(kd_ready, 1)
                    dve.wait_ge(kd_ready, full)
                    for b in every:
                        k = gk[:, place_of(b, full), :]
                        wait_emptied(dve, ("gk", b))
                        v.tensor_tensor(k, k, ex[:, place_of(b, full), :], ALU.mult).then_inc(kend_ready, 1)
                elif t == 3:
                    u = ("att", full)
                    is_emptied(v.tensor_tensor(atm.rearrange("p (h n) -> p h n", h=GH), unit_ap(u).rearrange("p (h n) -> p h n", h=GH),
                                               const("tri").unsqueeze(1).broadcast_to([P, GH, P]), ALU.mult), u)
                elif t == 4:
                    wait_emptied(dve, ("att", full))
                    for b in rest:
                        for i in range(2):
                            wait_emptied(dve, ("st", b, i))
                    for x in range(GH):
                        next_state(("u0", full, x // 2), state1, state0, x, 0)
                    wait_emptied(dve, ("u0", full, 1))
                    dve.sem_inc(state1_ready, 1)
                elif t == 5:
                    wait_emptied(dve, ("o", full, 1))
                    for x in range(GH):
                        c = slice(x * GV, x * GV + GV)
                        squares(og[:, c], sq[:, c], gms[:, x:x + 1])
                    steps.settle()
                    mean(gms[:, 0:4], GV)
                    steps.settle()
                    dve.sem_inc(norm_ms, 1)
                    for x in range(GH):
                        next_state(("u1", full, x // 2), state0, state1, x, 1)
                    wait_emptied(dve, ("u1", full, 1))
                    dve.wait_ge(silu_tanh, full)
                    steps.chain(v.scalar_tensor_tensor(out=gr, in0=sq, scalar=1.0, in1=gr, op0=ALU.add, op1=ALU.mult))
                    n_norm[0] += 1
                    dve.wait_ge(norm_rs, n_norm[0])
                    for x in range(GH):
                        c = slice(x * GV, x * GV + GV)
                        steps.did(v.scalar_tensor_tensor(out=og[:, c], in0=og[:, c], scalar=gms[:, 4 + x:5 + x], in1=onorm[:, :],
                                                         op0=ALU.mult, op1=ALU.mult))
                    steps.settle()
                    v.tensor_tensor(og, og, gr, ALU.mult).then_inc(og_ready, 1)
                elif t == 6:
                    for i in range(2):
                        add_to_h(("go", full, i), full, i)
                    for i in range(2):
                        wait_emptied(dve, ("go", full, i))
                    norm(3 if full == 1 else 5, [full])

            def next_state(u, out, before, x, c):
                src = unit_ap(u)[:, (x % 2) * GV:(x % 2) * GV + GV]
                ins = v.scalar_tensor_tensor(out=out[:, x, :], in0=before[:, x, :], scalar=dec[:, 2 * x + c:2 * x + c + 1],
                                             in1=src, op0=ALU.mult, op1=ALU.add)
                if x % 2:
                    is_emptied(ins, u)

            wait_emptied(dve, ("sk", 0))
            wait_emptied(dve, ("sk", 1))
            pick(0, 7)
            choose(0, 0)
            ready_for_queries(1)
            dot(0, FIRST)
            tile(0, 0, 0, 0)
            tile(1, 1, 0, 1, lambda: ready_for_queries(2))
            with dve.Fori(2, 8) as g:
                tile(g, 1, 0, g)
            tile(8, 1, 0, 0)
            for full in (1, 2):
                for t in range(8):
                    g = 8 * full + 1 + t
                    tile(g, 2 if full == 1 else 1, full - 1 if t < 7 else 1, (t + 1) % 8, lambda: gla(t, full))
            tile(25, 2, 1, 1, lambda: norm(6, [1]))
            with dve.Fori(26, 32) as g:
                tile(g, 2, 1, g - 24)
            dot(32, SECOND)
            weigh(32)
            add_experts(32, 2)
            norm(6, [2])


SMALL_LOADS = 10
_INS = ["x", "meta_tokens", "attn_norm", "attn_w_in", "mla_q_norm", "mla_w_uq", "mla_kv_norm", "mla_w_ukv", "swa_sinks",
        "attn_w_out", "gla_norm", "gla_w_in", "gla_w_gate", "gla_b_gate", "gla_out_norm", "gla_w_out", "ffn_norm",
        "peer_w_query", "peer_sub_keys", "peer_u", "peer_v", "final_norm"]


def kernel(**inputs):
    import concourse.bacc as bacc
    from concourse.bass_utils import run_bass_kernel_spmd

    nc = bacc.Bacc("TRN2", target_bir_lowering=False, num_devices=1)
    arrays = {n: np.ascontiguousarray(inputs[n]) for n in _INS}
    arrays["final_norm"] = arrays["final_norm"].reshape(1, D)
    arrays["consts"] = constants()
    io = {n: nc.dram_tensor(n, a.shape, mybir.dt.from_np(a.dtype), kind="ExternalInput").ap() for n, a in arrays.items()}
    io["out"] = nc.dram_tensor("out", (1, SEQ, D), F32, kind="ExternalOutput").ap()
    build(nc, io)
    r = run_bass_kernel_spmd(nc, [arrays], core_ids=[0])
    return r.results[0]["out"]
```
